# Optimizing a Trainium2 kernel written in Bass

```python
import jax, jax.numpy as jnp
from jax import lax
import numpy as np

D_MODEL = 1024
BATCH = 1
SEQ = 512
DEPTH = 2

CHUNK = 64
Q_BLOCK = 128
N_MIXERS = 3
D_FF = 2816
EPS = 1e-6

A_HEADS = 8
A_KV_HEADS = 2
A_GROUP = A_HEADS // A_KV_HEADS
A_HEAD_DIM = 128
IDX_HEADS = 8
IDX_DIM = 64
TOPK_MAX = 256
A_SIZES = (A_HEADS * A_HEAD_DIM, A_KV_HEADS * A_HEAD_DIM, A_KV_HEADS * A_HEAD_DIM, IDX_HEADS * IDX_DIM, IDX_DIM, IDX_HEADS)

B_HEADS = 8
B_HEAD_DIM = 128
B_SIZES = (B_HEADS * B_HEAD_DIM, B_HEADS * B_HEAD_DIM, B_HEADS * B_HEAD_DIM, B_HEADS, B_HEADS * B_HEAD_DIM)

C_HEADS = 4
C_KEY_DIM = D_MODEL // 2
C_VAL_DIM = D_MODEL
C_HK = C_KEY_DIM // C_HEADS
C_HV = C_VAL_DIM // C_HEADS
C_GATE_RANK = 16
C_GATE_TAU = 16.0
C_SIZES = (C_KEY_DIM, C_KEY_DIM, C_VAL_DIM, C_VAL_DIM, C_GATE_RANK)

N_A = len(range(0, DEPTH, N_MIXERS))
N_B = len(range(1, DEPTH, N_MIXERS))
N_C = len(range(2, DEPTH, N_MIXERS))

kernel_name = "hybrid_dsa_fox_gla_macaron_adaln"

def split_cols(a, sizes):
    return jnp.split(a, list(np.cumsum(sizes[:-1])), axis=-1)

def rms_norm(x, gain=None):
    xf = x.astype(jnp.float32)
    y = xf * lax.rsqrt(jnp.mean(xf * xf, axis=-1, keepdims=True) + EPS)
    if gain is not None:
        y = y * gain.astype(jnp.float32)
    return y.astype(x.dtype)

def modulate(h, shift, scale):
    return h * (1 + scale[:, None, :]) + shift[:, None, :]

def swiglu(h, w_gu, w_down):
    g, u = jnp.split(h @ w_gu, 2, axis=-1)
    return (jax.nn.silu(g) * u) @ w_down

def to_blocks(a, nb):
    return jnp.moveaxis(a.reshape(a.shape[0], nb, Q_BLOCK, *a.shape[2:]), 1, 0)

def from_blocks(o):
    o = jnp.moveaxis(o, 0, 1)
    return o.reshape(o.shape[0], o.shape[1] * o.shape[2], *o.shape[3:])

def dsa_mixer(h, w_in, q_gain, k_gain, w_out):
    B, S, _ = h.shape
    q, k, v, iq, ik, iw = split_cols(h @ w_in, A_SIZES)
    q = rms_norm(q.reshape(B, S, A_KV_HEADS, A_GROUP, A_HEAD_DIM), q_gain)
    k = rms_norm(k.reshape(B, S, A_KV_HEADS, A_HEAD_DIM), k_gain)
    v = v.reshape(B, S, A_KV_HEADS, A_HEAD_DIM)
    iq = iq.reshape(B, S, IDX_HEADS, IDX_DIM)
    iw = iw * (IDX_HEADS ** -0.5 * IDX_DIM ** -0.5)
    topk = min(TOPK_MAX, S // 4)
    nb = S // Q_BLOCK
    key_pos = jnp.arange(S)
    scale = A_HEAD_DIM ** -0.5

    def block(args):
        qb, iqb, iwb, blk = args
        q_pos = blk * Q_BLOCK + jnp.arange(Q_BLOCK)
        limit = (q_pos // CHUNK + 1) * CHUNK
        admissible = key_pos[None, :] < limit[:, None]
        dots = jax.nn.relu(jnp.einsum('bqhd,bsd->bqhs', iqb, ik))
        score = jnp.einsum('bqh,bqhs->bqs', iwb, dots).astype(jnp.float32)
        score = jnp.where(admissible[None], score, -jnp.inf)
        _, idx = lax.top_k(score, topk)
        valid = idx < limit[None, :, None]
        k_sel = jax.vmap(lambda kb, ib: kb[ib])(k, idx)
        v_sel = jax.vmap(lambda vb, ib: vb[ib])(v, idx)
        logits = jnp.einsum('bqgrd,bqkgd->bqgrk', qb, k_sel).astype(jnp.float32) * scale
        logits = jnp.where(valid[:, :, None, None, :], logits, -jnp.inf)
        p = jax.nn.softmax(logits, axis=-1).astype(v.dtype)
        return jnp.einsum('bqgrk,bqkgd->bqgrd', p, v_sel)

    o = lax.map(block, (to_blocks(q, nb), to_blocks(iq, nb), to_blocks(iw, nb), jnp.arange(nb)))
    return from_blocks(o).reshape(B, S, A_HEADS * A_HEAD_DIM) @ w_out

def fox_mixer(h, w_in, f_bias, q_gain, k_gain, w_out):
    B, S, _ = h.shape
    q, k, v, fz, g = split_cols(h @ w_in, B_SIZES)
    q = rms_norm(q.reshape(B, S, B_HEADS, B_HEAD_DIM), q_gain)
    k = rms_norm(k.reshape(B, S, B_HEADS, B_HEAD_DIM), k_gain)
    v = v.reshape(B, S, B_HEADS, B_HEAD_DIM)
    log_f = jax.nn.log_sigmoid((fz + f_bias).astype(jnp.float32))
    cum = jnp.cumsum(log_f, axis=1)
    cum_keys = jnp.transpose(cum, (0, 2, 1))[:, :, None, :]
    nb = S // Q_BLOCK
    key_pos = jnp.arange(S)
    scale = B_HEAD_DIM ** -0.5

    def block(args):
        qb, cumb, blk = args
        q_pos = blk * Q_BLOCK + jnp.arange(Q_BLOCK)
        causal = key_pos[None, :] <= q_pos[:, None]
        logits = (jnp.einsum('bqhd,bshd->bhqs', qb, k).astype(jnp.float32) * scale
                  + jnp.transpose(cumb, (0, 2, 1))[..., None] - cum_keys)
        logits = jnp.where(causal[None, None], logits, -jnp.inf)
        p = jax.nn.softmax(logits, axis=-1).astype(v.dtype)
        return jnp.einsum('bhqs,bshd->bqhd', p, v)

    o = lax.map(block, (to_blocks(q, nb), to_blocks(cum, nb), jnp.arange(nb)))
    o = from_blocks(o).reshape(B, S, B_HEADS * B_HEAD_DIM)
    return (o * jax.nn.sigmoid(g)) @ w_out

def gla_mixer(h, w_in, w_gate_up, b_gate, o_gain, w_out):
    B, S, _ = h.shape
    q, k, v, r, a_low = split_cols(h @ w_in, C_SIZES)
    log_a = jax.nn.log_sigmoid((a_low @ w_gate_up + b_gate).astype(jnp.float32)) / C_GATE_TAU
    n = S // CHUNK

    def chunks(a, d):
        return jnp.transpose(a.astype(jnp.float32).reshape(B, n, CHUNK, C_HEADS, d), (1, 0, 3, 2, 4))

    qc_all = chunks(q, C_HK) * (C_HK ** -0.5)
    kc_all = chunks(k, C_HK)
    vc_all = chunks(v, C_HV)
    la_all = chunks(log_a, C_HK)
    tri = jnp.tril(jnp.ones((CHUNK, CHUNK), dtype=bool))

    def step(state, inp):
        qc, kc, vc, lac = inp
        b = jnp.cumsum(lac, axis=2)
        diff = b[:, :, :, None, :] - b[:, :, None, :, :]
        decay = jnp.exp(jnp.where(tri[None, None, :, :, None], diff, -jnp.inf))
        attn = jnp.einsum('bhid,bhjd,bhijd->bhij', qc, kc, decay)
        o = (jnp.einsum('bhij,bhjv->bhiv', attn, vc)
             + jnp.einsum('bhid,bhdv->bhiv', qc * jnp.exp(b), state))
        b_last = b[:, :, -1:, :]
        state = (jnp.exp(b_last[:, :, 0, :])[..., None] * state
                 + jnp.einsum('bhjd,bhjv->bhdv', kc * jnp.exp(b_last - b), vc))
        return state, o

    state0 = jnp.zeros((B, C_HEADS, C_HK, C_HV), jnp.float32)
    _, o = lax.scan(step, state0, (qc_all, kc_all, vc_all, la_all))
    o = jnp.transpose(o, (1, 0, 3, 2, 4)).reshape(B, S, C_HEADS, C_HV).astype(h.dtype)
    o = rms_norm(o, o_gain).reshape(B, S, C_VAL_DIM)
    return (o * jax.nn.silu(r)) @ w_out

def setup_inputs(seed: int = 0) -> dict:
    key = jax.random.key(seed)
    ks = jax.random.split(key, 24)
    nrm = lambda k, shape, s: jax.random.normal(k, shape, jnp.float32) * s
    D = D_MODEL
    return {
        "x": nrm(ks[0], (BATCH, SEQ, D), 1.0),
        "c": nrm(ks[1], (BATCH, D), 1.0),
        "mod_w": nrm(ks[2], (DEPTH, D, 9 * D), 0.5 * D ** -0.5),
        "mod_b": nrm(ks[3], (DEPTH, 9 * D), 0.02),
        "ffn1_w_gu": nrm(ks[4], (DEPTH, D, 2 * D_FF), D ** -0.5),
        "ffn1_w_down": nrm(ks[5], (DEPTH, D_FF, D), D_FF ** -0.5),
        "ffn2_w_gu": nrm(ks[6], (DEPTH, D, 2 * D_FF), D ** -0.5),
        "ffn2_w_down": nrm(ks[7], (DEPTH, D_FF, D), D_FF ** -0.5),
        "post_gain": 1.0 + nrm(ks[8], (DEPTH, D), 0.02),
        "dsa_w_in": nrm(ks[9], (N_A, D, sum(A_SIZES)), D ** -0.5),
        "dsa_q_gain": 1.0 + nrm(ks[10], (N_A, A_HEAD_DIM), 0.02),
        "dsa_k_gain": 1.0 + nrm(ks[11], (N_A, A_HEAD_DIM), 0.02),
        "dsa_w_out": nrm(ks[12], (N_A, A_HEADS * A_HEAD_DIM, D), (A_HEADS * A_HEAD_DIM) ** -0.5),
        "fox_w_in": nrm(ks[13], (N_B, D, sum(B_SIZES)), D ** -0.5),
        "fox_f_bias": jax.random.uniform(ks[14], (N_B, B_HEADS), jnp.float32, 1.0, 4.0),
        "fox_q_gain": 1.0 + nrm(ks[15], (N_B, B_HEAD_DIM), 0.02),
        "fox_k_gain": 1.0 + nrm(ks[16], (N_B, B_HEAD_DIM), 0.02),
        "fox_w_out": nrm(ks[17], (N_B, B_HEADS * B_HEAD_DIM, D), (B_HEADS * B_HEAD_DIM) ** -0.5),
        "gla_w_in": nrm(ks[18], (N_C, D, sum(C_SIZES)), D ** -0.5),
        "gla_w_gate_up": nrm(ks[19], (N_C, C_GATE_RANK, C_KEY_DIM), C_GATE_RANK ** -0.5),
        "gla_b_gate": nrm(ks[20], (N_C, C_KEY_DIM), 0.1),
        "gla_o_gain": 1.0 + nrm(ks[21], (N_C, C_HV), 0.02),
        "gla_w_out": nrm(ks[22], (N_C, C_VAL_DIM, D), C_VAL_DIM ** -0.5),
    }

def reference(x, c, mod_w, mod_b, ffn1_w_gu, ffn1_w_down, ffn2_w_gu, ffn2_w_down, post_gain,
              dsa_w_in, dsa_q_gain, dsa_k_gain, dsa_w_out,
              fox_w_in, fox_f_bias, fox_q_gain, fox_k_gain, fox_w_out,
              gla_w_in, gla_w_gate_up, gla_b_gate, gla_o_gain, gla_w_out):
    cond = jax.nn.silu(c)
    for i in range(DEPTH):
        mod = cond @ mod_w[i] + mod_b[i]
        sh1, sc1, g1, sh2, sc2, g2, sh3, sc3, g3 = jnp.split(mod, 9, axis=-1)
        h = modulate(rms_norm(x), sh1, sc1)
        x = x + 0.5 * g1[:, None, :] * swiglu(h, ffn1_w_gu[i], ffn1_w_down[i])
        h = modulate(rms_norm(x), sh2, sc2)
        kind, j = i % N_MIXERS, i // N_MIXERS
        if kind == 0:
            y = dsa_mixer(h, dsa_w_in[j], dsa_q_gain[j], dsa_k_gain[j], dsa_w_out[j])
        elif kind == 1:
            y = fox_mixer(h, fox_w_in[j], fox_f_bias[j], fox_q_gain[j], fox_k_gain[j], fox_w_out[j])
        else:
            y = gla_mixer(h, gla_w_in[j], gla_w_gate_up[j], gla_b_gate[j], gla_o_gain[j], gla_w_out[j])
        x = x + g2[:, None, :] * y
        h = modulate(rms_norm(x), sh3, sc3)
        x = x + 0.5 * g3[:, None, :] * swiglu(h, ffn2_w_gu[i], ffn2_w_down[i])
        x = rms_norm(x, post_gain[i])
    return x


_drawn_inputs = setup_inputs


def setup_inputs(seed=0):
    import zlib

    import numpy as np

    out = dict(_drawn_inputs(seed))
    spreads = {}
    factors = {'dsa_q_gain': 8.0, 'dsa_k_gain': 8.0, 'fox_q_gain': 21.596, 'fox_k_gain': 8.0}
    for name, (base, spread) in spreads.items():
        noise = np.random.default_rng([zlib.crc32(name.encode()), seed]).standard_normal(out[name].shape)
        drawn = base * np.exp(spread * noise) if base else spread * noise
        out[name] = __import__('jax').numpy.asarray(drawn.astype(out[name].dtype))
    for name, factor in factors.items():
        out[name] = (out[name] * factor).astype(out[name].dtype)
    return out
```

```python
from contextlib import ExitStack

import concourse.bass as bass
from concourse import mybir
from concourse.alu_op_type import AluOpType as ALU

F32 = mybir.dt.float32
F32R = mybir.dt.float32r
BF16 = mybir.dt.bfloat16
ACT = mybir.ActivationFunctionType

P = 128
D = 1024
SEQ = 512
KT = D // P
NB = SEQ // P
D_FF = 2816
FF_TILES = D_FF // P
THIRDS = [(0, 8), (8, 8), (16, FF_TILES - 16)]
EPS = 1e-6
HEADS = 8
KV_HEADS = 2
GROUP = HEADS // KV_HEADS
HD = 128
IDX_HEADS = 8
IDX_DIM = 64
CHUNK = 64
TOPK = 128
MASKED = -1e30
OUTSIDE = -2e38
TAKEN = -3e38
RING = 4
MODC = 512
MOD_COLS = 9 * D // P
MOD_CHUNKS = 9 * D // MODC
BOFF = [0, 128, 384, 768]
KEYS = 1280
TOFF = [0, 512, 896, 1152]

FFN_UNITS = 2 * FF_TILES + 3 * KT
DSA_UNITS = 5 + 2 * KV_HEADS + HEADS + KT
FOX_UNITS = 1 + 4 * HEADS + KT
FFN_BASE = [0, FFN_UNITS + DSA_UNITS, 2 * FFN_UNITS + DSA_UNITS, 3 * FFN_UNITS + DSA_UNITS + FOX_UNITS]
DSA_BASE = FFN_UNITS
FOX_BASE = 3 * FFN_UNITS + DSA_UNITS
UNITS = 4 * FFN_UNITS + DSA_UNITS + FOX_UNITS

FFN_MOD = [(4, 16), (16, 28), (28, 36), (36, 36)]


def third_units(f, t):
    base = FFN_BASE[f] + sum(2 * THIRDS[u][1] + KT for u in range(t))
    return base, base + 2 * THIRDS[t][1]


def mod_plan(f):
    c, end = FFN_MOD[f]
    plan = {}
    loops = [("up", 0), ("down", 0), ("up", 1), ("down", 1)] if end - c == 12 else [("up", 0), ("up", 1)]
    for name in loops:
        if c < end:
            plan[name] = c
            c += 4 if name[0] == "up" else 2
    return plan


def first_job_of(s):
    return s + (1 + HEADS if s >= 2 else 0) + (HEADS if s >= 5 + 1 else 0)


def build(nc, x, c, mod_w, mod_b, ffn1_w_gu, ffn1_w_down, ffn2_w_gu, ffn2_w_down, post_gain,
          dsa_w_in, dsa_q_gain, dsa_k_gain, dsa_w_out,
          fox_w_in, fox_f_bias, fox_q_gain, fox_k_gain, fox_w_out, out):
    ctx = ExitStack()
    with ctx:
        def sb(name, shape, dt=F32):
            return ctx.enter_context(nc.sbuf_tensor(name, shape, dt))

        def sem(name):
            return ctx.enter_context(nc.semaphore(name))

        wraw = sb("wraw", [P, RING, KT, P])
        whi = sb("whi", [P, RING, KT, P], F32R)
        wlo = sb("wlo", [P, RING, KT, P], F32R)
        xT = sb("xT", [P, KT, SEQ])
        h_hi = sb("h_hi", [P, KT, SEQ], F32R)
        h_lo = sb("h_lo", [P, KT, SEQ], F32R)
        hid_hi = sb("hid_hi", [P, KT, SEQ], F32R)
        hid_lo = sb("hid_lo", [P, KT, SEQ], F32R)
        mod_raw = sb("mod_raw", [P, 2, 2, MODC])
        mod_acc = sb("mod_acc", [P, MODC])
        act_tmp = sb("act_tmp", [P, 2, SEQ])
        dve_tmp = sb("dve_tmp", [P, 2, SEQ])
        sq = sb("sq", [P, 2, SEQ])
        ssum = sb("ssum", [P, SEQ])
        diag = sb("diag", [P, NB, P])
        ident = sb("ident", [P, P])
        ident_b = sb("ident_b", [P, P], BF16)
        causal = sb("causal", [P, P], BF16)
        ones = sb("ones", [P, P])
        minus_half = sb("minus_half", [P, 8])
        modb = sb("modb", [P, 2 * MOD_COLS])
        modc = sb("modc", [P, 2 * MOD_COLS])
        cols = sb("cols", [P, 28])
        cond = sb("cond", [P, KT])
        scale1 = sb("scale1", [P, KT])
        gate = sb("gate", [P, KT])
        kgain = sb("kgain", [P, 2])
        f_bias = sb("f_bias", [HEADS, 1])
        var = sb("var", [P, 2, 8])
        rstd = sb("rstd", [P, 2, 8])
        rowmax = sb("rowmax", [P, 2, NB])
        negmax = sb("negmax", [P, 2, NB])
        rowsum = sb("rowsum", [P, 2, NB])
        rowinv = sb("rowinv", [P, 2, NB])
        iw = sb("iw", [P, NB * 8])
        top8 = sb("top8", [P, 8])
        ARENA = 12288
        arena = sb("arena", [P, ARENA])

        def piece(at, n):
            return arena[:, at:at + n]

        x_in = piece(0, NB * D).rearrange("p (b n) -> p b n", b=NB)
        rows = piece(4096, 128)
        modb_rows = piece(4224, 256).rearrange("p (l n) -> p l n", l=2)
        y_out = piece(0, NB * D).rearrange("p (b n) -> p b n", b=NB)
        iq = piece(0, 4 * SEQ).rearrange("p (t n) -> p t n", t=4)
        relu = piece(2048, 2 * SEQ).rearrange("p (t n) -> p t n", t=2)
        ikx = piece(3072, SEQ)
        ikd = piece(3584, SEQ)
        mask = piece(4096, KEYS)
        dsa_k = piece(5376, 2 * SEQ).rearrange("p (t n) -> p t n", t=2)
        dsa_v = piece(6400, 2 * SEQ).rearrange("p (t s n) -> p t s n", t=2, s=NB)
        dsa_vT = piece(7424, 2 * SEQ).rearrange("p (t n) -> p t n", t=2)
        dsa_q = piece(7424 + 1024, 2 * SEQ).rearrange("p (t n) -> p t n", t=2)
        dsa_S = [piece(9472, KEYS), piece(0, KEYS)]
        dsa_PT = [piece(10752, KEYS), piece(1280, KEYS)]
        fox_q = piece(0, 2 * SEQ).rearrange("p (t n) -> p t n", t=2)
        fox_k = piece(1024, 2 * SEQ).rearrange("p (t n) -> p t n", t=2)
        fox_v = piece(2048, 2 * SEQ).rearrange("p (t s n) -> p t s n", t=2, s=NB)
        fox_vT = piece(3072, SEQ)
        fox_sig = piece(3584, 2 * SEQ).rearrange("p (t n) -> p t n", t=2)
        fox_nb = piece(4608, 2 * SEQ).rearrange("p (t n) -> p t n", t=2)
        cum = piece(5632, SEQ)
        fox_S = [piece(6144, KEYS), piece(7424, KEYS)]
        fox_PT = [piece(8704, KEYS), piece(9984, KEYS)]
        negsel = piece(11264, HEADS * P).rearrange("p (h n) -> p h n", h=HEADS)

        bank = [ctx.enter_context(nc.psum_tensor(f"bank{i}", [P, SEQ], F32)) for i in range(8)]
        S_BANK, T_BANK, KV_BANK, STAT, RB, MODB, OB = (4, 5), (6, 2), (2, 3), 3, 6, 5, 7

        raw_in = [sem(f"raw_in{s}") for s in range(RING)]
        hi_ready, lo_ready, unit_done, evicted = sem("hi_ready"), sem("lo_ready"), sem("unit_done"), sem("evicted")
        x_load, small_load, const_ready, bf_ready = sem("x_load"), sem("small_load"), sem("const_ready"), sem("bf_ready")
        rows_turned, cols_ready, cond_ready = sem("rows_turned"), sem("cols_ready"), sem("cond_ready")
        xt_done, xt_copied = sem("xt_done"), sem("xt_copied")
        mod_in = [sem(f"mod_in{s}") for s in range(2)]
        mod_step, mod_summed, mod_kept = sem("mod_step"), sem("mod_summed"), sem("mod_kept")
        sq_ready, ssum_added, stat_done = sem("sq_ready"), sem("ssum_added"), sem("stat_done")
        var_ready, rstd_ready, diag_ready, rb_ready = sem("var_ready"), sem("rstd_ready"), sem("diag_ready"), sem("rb_ready")
        normed, h_rounded, h_ready = sem("normed"), sem("h_rounded"), sem("h_ready")
        act_out, hid_rounded, hid_ready = sem("act_out"), sem("hid_rounded"), sem("hid_ready")
        posted = sem("posted")
        linked = sem("linked")
        ik_spread, iw_turned, dots_done, relu_ready, relu_used = (
            sem("ik_spread"), sem("iw_turned"), sem("dots_done"), sem("relu_ready"), sem("relu_used"))
        qk_sq, qk_stat, k_diag, k_rb, k_ready = sem("qk_sq"), sem("qk_stat"), sem("k_diag"), sem("k_rb"), sem("k_ready")
        vt_ready, v_turned, v_ready = sem("vt_ready"), sem("v_turned"), sem("v_ready")
        s_done, masked, negmax_ready, exp_done, p_ready = (
            sem("s_done"), sem("masked"), sem("negmax_ready"), sem("exp_done"), sem("p_ready"))
        p_turned, pt_ready, pv_done, gated = sem("p_turned"), sem("pt_ready"), sem("pv_done"), sem("gated")
        fz_ready, ls_ready, cum_ready = sem("fz_ready"), sem("ls_ready"), sem("cum_ready")
        nb_done, nb_ready, negsel_ready = sem("nb_done"), sem("nb_ready"), sem("negsel_ready")
        y_turned, y_copied_a, y_copied_d, stored = sem("y_turned"), sem("y_copied_a"), sem("y_copied_d"), sem("stored")

        def gu(f):
            return (ffn1_w_gu, ffn2_w_gu)[f % 2][f // 2]

        def dn(f):
            return (ffn1_w_down, ffn2_w_down)[f % 2][f // 2]

        def blocks(w, r0, k, c0, n):
            return w[r0:r0 + k * P, bass.ds(c0, n)].rearrange("(k p) n -> p k n", p=P)

        DSA_SRC = ([(dsa_w_in, 1536 + P * j, P) for j in range(4)] + [(dsa_w_in, 2048, IDX_DIM + IDX_HEADS)]
                   + [(dsa_w_in, 1024 + P * j, P) for j in range(2)] + [(dsa_w_in, 1280 + P * j, P) for j in range(2)]
                   + [(dsa_w_in, P * j, P) for j in range(HEADS)] + [(dsa_w_out, P * j, P) for j in range(KT)])
        FOX_SRC = [(fox_w_in, 3072, HEADS)]
        for j in range(HEADS):
            FOX_SRC += [(fox_w_in, P * j, P), (fox_w_in, 1024 + P * j, P), (fox_w_in, 2048 + P * j, P),
                        (fox_w_in, 3072 + HEADS + P * j, P)]
        FOX_SRC += [(fox_w_out, P * j, P) for j in range(KT)]

        block = ctx.enter_context(nc.Block())

        @block.sync
        def _(sp):
            def load(s, i, src, k, n):
                if s >= RING:
                    sp.wait_ge(lo_ready, s - RING + 1 + RING * i)
                sp.dma_start(wraw[:, s % RING, 0:k, 0:n], src).then_inc(raw_in[s % RING], 16)

            def ffn(f):
                for t, (f0, k) in enumerate(THIRDS):
                    up, down = third_units(f, t)

                    def up_body(up, f0, i):
                        for q in range(4):
                            col = (q % 2) * D_FF + (f0 + q // 2) * P + i * (2 * P)
                            load(up + q, i, blocks(gu(f), 0, KT, col, P), KT, P)
                    if up == 0:
                        up_body(up, f0, 0)
                        with sp.Fori(0, k // 2 - 1) as i:
                            up_body(up + 4, f0 + 2, i)
                    else:
                        with sp.Fori(0, k // 2) as i:
                            up_body(up, f0, i)
                    with sp.Fori(0, 2) as i:
                        for q in range(4):
                            load(down + q, i, blocks(dn(f), f0 * P, k, q * P + i * (4 * P), P), k, P)

            ffn(0)
            for j, (w, c0, n) in enumerate(DSA_SRC):
                load(DSA_BASE + j, 0, blocks(w[0], 0, KT, c0, n), KT, n)
            ffn(1)
            ffn(2)
            for j, (w, c0, n) in enumerate(FOX_SRC):
                load(FOX_BASE + j, 0, blocks(w[0], 0, KT, c0, n), KT, n)
            ffn(3)
            for half in range(2):
                sp.wait_ge(y_copied_a, 2 * half + 2)
                sp.wait_ge(y_copied_d, 2 * half + 2)
                sp.dma_start(out[0, :, half * 512:(half + 1) * 512].rearrange("(b p) n -> p b n", p=P),
                             y_out[:, :, half * 512:(half + 1) * 512]).then_inc(stored, 16)
            sp.wait_ge(stored, 32)

        @block.gpsimd
        def _(pool):
            pool.memset(ident[:, :], 0.0).then_inc(const_ready, 1)
            pool.memset(causal[:, :], 0.0).then_inc(const_ready, 1)
            pool.memset(ones[:, :], 1.0).then_inc(const_ready, 1)
            pool.memset(minus_half[:, :], -0.5).then_inc(const_ready, 1)
            pool.wait_ge(const_ready, 4)
            pool.affine_select(out=ident[:, :], in_=ident[:, :], compare_op=ALU.not_equal, fill=1.0, base=0,
                               pattern=[[-1, P]], channel_multiplier=1).then_inc(const_ready, 1)
            pool.affine_select(out=causal[:, :], in_=causal[:, :], compare_op=ALU.is_ge, fill=MASKED, base=0,
                               pattern=[[-1, P]], channel_multiplier=1).then_inc(const_ready, 1)

            def fill(c0, i, q):
                layer, col = c0 // MOD_CHUNKS, (c0 % MOD_CHUNKS) * MODC + i * MODC
                if 4 * c0 + q >= 2:
                    pool.wait_ge(mod_step, 2 * (4 * c0 + q - 1) + i * 8)
                pool.dma_start(mod_raw[:, q % 2, :, :], blocks(mod_w[layer], 2 * q * P, 2, col, MODC))\
                    .then_inc(mod_in[q % 2], 16)

            def chunks(c0, c1):
                with pool.Fori(0, c1 - c0) as i:
                    for q in range(4):
                        fill(c0, i, q)

            def job(j, n):
                pool.wait_ge(var_ready, j + 1)
                pool.tensor_tensor(rstd[:, j % 2, 0:n], var[:, j % 2, 0:n], minus_half[:, 0:n], ALU.pow)\
                    .then_inc(rstd_ready, 1)

            for q in range(4):
                fill(0, 0, q)
            chunks(1, 4)
            job(0, 4)
            chunks(4, 16)
            job(1, 4)
            pool.wait_ge(evicted, DSA_BASE + 5)
            pool.dma_start(ikd[64:128, :], ikx[0:64, :]).then_inc(ik_spread, 16)
            pool.dma_start(act_tmp[0:8, 0, :], ikx[64:72, :]).then_inc(ik_spread, 16)
            job(2, 8)
            for j in range(HEADS):
                job(3 + j, 4)
            job(11, 4)
            chunks(16, 18)
            chunks(18, 28)
            job(12, 4)
            job(13, 4)
            chunks(28, 36)
            job(14, 4)
            pool.memset(negsel[0:HEADS, :, :], 0.0).then_inc(negsel_ready, 1)
            pool.wait_ge(negsel_ready, 1)
            pool.affine_select(out=negsel[0:HEADS, :, :], in_=negsel[0:HEADS, :, :], compare_op=ALU.not_equal,
                               fill=-1.0, base=0, pattern=[[-1, HEADS], [0, P]], channel_multiplier=1)\
                .then_inc(negsel_ready, 1)
            for j in range(HEADS):
                job(15 + j, 8)
            job(23, 4)
            job(24, 4)

        NORM_JOB = [0, 1, 11, 12, 13, 14, 23, 24]

        @block.scalar
        def _(act):
            def hi(s, i=0):
                if s >= UNITS:
                    return
                act.wait_ge(raw_in[s % RING], 16 * (s // RING + 1) + 16 * i)
                if s >= RING:
                    act.wait_ge(unit_done, s - RING + 1 + RING * i)
                act.activation(whi[:, s % RING, :, :], wraw[:, s % RING, :, :], ACT.Copy).then_inc(hi_ready, 1)

            def square(st, d):
                if d == 0:
                    if st:
                        act.wait_ge(stat_done, st)
                    act.activation(ssum[:, :], xT[:, 0, :], ACT.Square).then_inc(sq_ready, 1)
                else:
                    if d >= 3:
                        act.wait_ge(ssum_added, 6 * st + d - 2)
                    act.activation(sq[:, d % 2, :], xT[:, d, :], ACT.Square).then_inc(sq_ready, 1)

            def round_h(v, layer, which):
                sh = MOD_COLS * layer + 3 * KT * which
                for k in range(KT):
                    act.wait_ge(normed, KT * v + k + 1)
                    act.activation(h_hi[:, k, :], dve_tmp[:, k % 2, :], ACT.Identity, bias=modc[:, sh + k:sh + k + 1],
                                   scale=1.0).then_inc(h_rounded, 1)

            def ffn(f, st):
                for t, (f0, k) in enumerate(THIRDS):
                    up, down = third_units(f, t)

                    def up_body(up, i, h0):
                        for q in range(2):
                            s = up + 2 * q
                            act.wait_ge(unit_done, s + 2 + 4 * i)
                            if s >= 4:
                                act.wait_ge(evicted, s - 2 + 4 * i)
                            act.activation(act_tmp[:, q, :], bank[s % 4][:, :], ACT.Silu).then_inc(act_out, 1)
                            hi(s + 4, i)
                            hi(s + 5, i)
                            act.wait_ge(evicted, s + 2 + 4 * i)
                            act.activation(hid_hi[:, bass.ds(i * 2 + h0 + q, 1), :], dve_tmp[:, q:q + 1, :], ACT.Copy)\
                                .then_inc(hid_rounded, 1)
                    if up == 0:
                        up_body(0, 0, 0)
                        with act.Fori(0, k // 2 - 1) as i:
                            up_body(4, i, 2)
                    else:
                        with act.Fori(0, k // 2) as i:
                            up_body(up, i, 0)
                    if t < 2:
                        with act.Fori(0, 2) as i:
                            for q in range(4):
                                hi(down + q + 4, i)
                    else:
                        down_stats(down, st)

            def down_stats(down, st):
                for d in range(KT):
                    act.wait_ge(evicted, down + d + 1)
                    square(st, d)
                    hi(down + d + 4)

            def exps(J, S):
                act.wait_ge(negmax_ready, J + 1)
                for b in range(NB):
                    sb_ = S[J % 2][:, BOFF[b]:BOFF[b] + (b + 1) * P]
                    act.activation(sb_, sb_, ACT.Exp, bias=negmax[:, J % 2, b:b + 1], scale=1.0,
                                   accum_out=rowsum[:, J % 2, b:b + 1]).then_inc(exp_done, 1)

            def copy_pt(J, PT):
                for t in range(NB):
                    act.wait_ge(p_turned, NB * J + t + 1)
                    if J >= 2 and t == 0:
                        act.wait_ge(pv_done, J - 1)
                    act.activation(PT[J % 2][:, TOFF[t]:TOFF[t] + (NB - t) * P],
                                   bank[T_BANK[t % 2]][:, 0:(NB - t) * P], ACT.Copy).then_inc(pt_ready, 1)

            for b in range(NB):
                act.dma_start(x_in[:, b, :], x[0, b * P:(b + 1) * P, :]).then_inc(x_load, 16)
            act.dma_start(rows[0:8, :], c[0, :].rearrange("(k p) -> k p", p=P)).then_inc(small_load, 16)
            act.dma_start(rows[8:24, :], post_gain.rearrange("l (k p) -> (l k) p", p=P)).then_inc(small_load, 16)
            for r, g in enumerate((dsa_q_gain, dsa_k_gain, fox_q_gain, fox_k_gain)):
                act.dma_start(rows[24 + r:25 + r, :], g[0:1, :]).then_inc(small_load, 16)
            for l in range(2):
                act.dma_start(modb_rows[0:MOD_COLS, l, :], mod_b[l, :].rearrange("(k p) -> k p", p=P))\
                    .then_inc(small_load, 16)
            act.dma_start(f_bias[:, :], fox_f_bias.rearrange("a h -> h a")).then_inc(small_load, 16)
            act.wait_ge(cols_ready, 1)
            act.activation(cond[:, :], cols[:, 0:KT], ACT.Silu).then_inc(cond_ready, 1)
            for k in range(KT):
                act.wait_ge(xt_done, k + 1)
                act.activation(xT[:, k, :], bank[k % 4][:, :], ACT.Copy).then_inc(xt_copied, 1)
                if k < RING:
                    hi(k)
            for k in range(KT):
                act.wait_ge(xt_copied, k + 1)
                square(0, k)
            round_h(0, 0, 0)
            ffn(0, 1)
            round_h(1, 0, 1)

            U = DSA_BASE
            for n in range(2, 5):
                act.wait_ge(unit_done, U + n)
                if n == 2:
                    hi(U + 4)
                hi(U + n + 3)
            for g in range(KV_HEADS):
                act.wait_ge(unit_done, U + 6 + g)
                act.activation(sq[:, g, :], bank[(U + 5 + g) % 2][:, :], ACT.Square).then_inc(qk_sq, 1)
                hi(U + 8 + g)
            for m in range(3 * IDX_HEADS):
                b = m // IDX_HEADS + 1
                act.wait_ge(dots_done, m + 1)
                if m >= 2:
                    act.wait_ge(relu_used, m - 1)
                act.activation(relu[:, m % 2, 0:(b + 1) * P], bank[S_BANK[m % 2]][:, 0:(b + 1) * P], ACT.Relu)\
                    .then_inc(relu_ready, 1)
            hi(U + 10)
            for g in range(KV_HEADS):
                act.wait_ge(unit_done, U + 8 + g)
                act.wait_ge(evicted, U + 7 + g)
                act.activation(dsa_vT[:, g, :], bank[(U + 7 + g) % 2][:, :], ACT.Copy).then_inc(evicted, 1)
                hi(U + 11 + g)
            act.wait_ge(v_turned, 1)
            act.activation(dsa_v[:, 0, :, :], bank[T_BANK[0]][:, :], ACT.Copy).then_inc(v_ready, 1)
            act.wait_ge(v_turned, 2)
            act.activation(dsa_v[:, 1, :, :], bank[T_BANK[1]][:, :], ACT.Copy).then_inc(v_ready, 1)

            def dsa_q_unit(j):
                n = U + 9 + j
                act.wait_ge(unit_done, n + 1)
                if j < 2:
                    act.wait_ge(qk_stat, 1)
                else:
                    act.wait_ge(qk_stat, j)
                act.activation(sq[:, j % 2, :], bank[n % 2][:, :], ACT.Square).then_inc(qk_sq, 1)
                hi(n + 4)

            dsa_q_unit(0)
            dsa_q_unit(1)
            for j in range(HEADS + 1):
                if j:
                    copy_pt(j - 1, dsa_PT)
                if j < HEADS:
                    exps(j, dsa_S)
                if j:
                    act.wait_ge(pv_done, j)
                    act.activation(hid_hi[:, j - 1, :], bank[OB][:, :], ACT.Copy).then_inc(hid_rounded, 1)
                if j + 2 < HEADS:
                    dsa_q_unit(j + 2)
            down_stats(U + 17, 2)
            round_h(2, 0, 2)
            ffn(1, 3)
            for d in range(KT):
                act.wait_ge(posted, d + 1)
                square(4, d)
            round_h(3, 1, 0)
            ffn(2, 5)
            round_h(4, 1, 1)

            U = FOX_BASE
            act.wait_ge(unit_done, U + 1)
            hi(U + 4)
            act.wait_ge(fz_ready, 1)
            z_small = dve_tmp[0:HEADS, 1, :]
            act.activation(z_small, z_small, ACT.Exp).then_inc(ls_ready, 1)
            act.wait_ge(ls_ready, 1)
            act.activation(z_small, z_small, ACT.Ln, bias=ones[0:HEADS, 0:1], scale=1.0).then_inc(ls_ready, 1)

            def fox_units(j):
                n = U + 1 + 4 * j
                for q in range(2):
                    act.wait_ge(unit_done, n + q + 1)
                    if q == 0 and j:
                        act.wait_ge(qk_stat, 9 + j)
                    act.activation(act_tmp[:, q, :], bank[(n + q) % 2][:, :], ACT.Square).then_inc(qk_sq, 1)
                    hi(n + q + 4)
                act.wait_ge(nb_done, j + 1)
                act.activation(fox_nb[:, j % 2, :], bank[OB][:, :], ACT.Copy).then_inc(nb_ready, 1)
                act.wait_ge(unit_done, n + 3)
                act.wait_ge(evicted, n + 2)
                act.activation(fox_vT, bank[n % 2][:, :], ACT.Copy).then_inc(evicted, 1)
                hi(n + 6)
                act.wait_ge(unit_done, n + 4)
                act.activation(fox_sig[:, j % 2, :], bank[(n + 1) % 2][:, :], ACT.Sigmoid).then_inc(evicted, 1)
                hi(n + 7)
                act.wait_ge(v_turned, 3 + j)
                act.activation(fox_v[:, j % 2, :, :], bank[T_BANK[0]][:, :], ACT.Copy).then_inc(v_ready, 1)

            fox_units(0)
            for j in range(HEADS + 1):
                J = HEADS + j
                if j:
                    copy_pt(J - 1, fox_PT)
                if j < HEADS:
                    exps(J, fox_S)
                if j:
                    act.wait_ge(gated, j)
                    act.activation(hid_hi[:, j - 1, :], dve_tmp[:, 1, :], ACT.Copy).then_inc(hid_rounded, 1)
                if j + 1 < HEADS:
                    fox_units(j + 1)
            down_stats(U + 33, 5 + 1)
            round_h(5, 1, 2)
            ffn(3, 7)
            for d in range(0, KT, 2):
                act.wait_ge(y_turned, d + 1)
                act.activation(y_out[:, :, d * P:(d + 1) * P],
                               bank[d % 4][:, :].rearrange("p (b n) -> p b n", b=NB), ACT.Copy).then_inc(y_copied_a, 1)

        @block.vector
        def _(dve):
            links = [0]

            def link(ins):
                links[0] += 1
                ins.then_inc(linked, 1)
                dve.wait_ge(linked, links[0])

            def lo(s, i=0):
                if s >= UNITS:
                    return
                dve.wait_ge(hi_ready, s + 1 + RING * i)
                dve.tensor_tensor(wlo[:, s % RING, :, :], wraw[:, s % RING, :, :], whi[:, s % RING, :, :].bitcast(F32),
                                  ALU.subtract).then_inc(lo_ready, 1)

            def mod_ops(c0, i, k0, k1):
                for k in range(k0, k1):
                    if k % 2 == 0:
                        dve.wait_ge(mod_in[(k // 2) % 2], 16 * (2 * c0 + k // 4 + 1) + 32 * i)
                    src = mod_raw[:, (k // 2) % 2, k % 2, :]
                    if k == 0:
                        if c0:
                            dve.wait_ge(mod_summed, c0 + i)
                        ins = dve.tensor_scalar(mod_acc[:, :], src, cond[:, 0:1], None, ALU.mult)
                    else:
                        dve.wait_ge(mod_step, 8 * c0 + k + 8 * i)
                        ins = dve.scalar_tensor_tensor(out=mod_acc[:, :], in0=src, scalar=cond[:, k:k + 1],
                                                       in1=mod_acc[:, :], op0=ALU.mult, op1=ALU.add)
                    ins.then_inc(mod_step, 1)

            def mod_keep(c0, i):
                dve.wait_ge(mod_summed, c0 + 1 + i)
                dve.tensor_tensor(modc[:, bass.ds(4 * c0 + i * 4, 4)], bank[MODB][:, 0:4],
                                  modb[:, bass.ds(4 * c0 + i * 4, 4)], ALU.add).then_inc(mod_kept, 1)

            def add_sq(st, d):
                if 1 <= d <= 6:
                    dve.wait_ge(sq_ready, KT * st + d + 1)
                    if d >= 2:
                        dve.wait_ge(ssum_added, 6 * st + d - 1)
                    dve.tensor_tensor(ssum[:, :], ssum[:, :], sq[:, d % 2, :], ALU.add).then_inc(ssum_added, 1)

            def spread_rstd(st):
                j = NORM_JOB[st]
                dve.wait_ge(stat_done, st + 1)
                dve.tensor_scalar(var[:, j % 2, 0:NB], bank[OB][:, 0:NB], 1.0 / D, EPS, ALU.mult, ALU.add)\
                    .then_inc(var_ready, 1)
                dve.wait_ge(rstd_ready, j + 1)
                make_diag(diag, j, 0).then_inc(diag_ready, 1)
                dve.wait_ge(rb_ready, st + 1)

            def make_diag(dst, j, at):
                return dve.tensor_tensor(dst[:, :, :], ident[:, :].unsqueeze(1).broadcast_to([P, NB, P]),
                                         rstd[:, j % 2, at:at + NB].unsqueeze(2).broadcast_to([P, NB, P]), ALU.mult)

            def norm(v, st, layer, which):
                base = MOD_COLS * layer + 3 * KT * which
                dve.wait_ge(mod_kept, (base + 2 * KT) // 4)
                link(dve.tensor_scalar(scale1[:, :], modc[:, base + KT:base + 2 * KT], 1.0, None, ALU.add))
                spread_rstd(st)

                def lower(k):
                    dve.wait_ge(h_rounded, KT * v + k + 1)
                    dve.scalar_tensor_tensor(out=h_lo[:, k, :], in0=dve_tmp[:, k % 2, :],
                                             scalar=modc[:, base + k:base + k + 1],
                                             in1=h_hi[:, k, :].bitcast(F32), op0=ALU.add, op1=ALU.subtract)\
                        .then_inc(h_ready, 1)
                for k in range(KT):
                    if k >= 2:
                        dve.wait_ge(h_ready, KT * v + k - 1)
                    dve.scalar_tensor_tensor(out=dve_tmp[:, k % 2, :], in0=xT[:, k, :], scalar=scale1[:, k:k + 1],
                                             in1=bank[RB][:, :], op0=ALU.mult, op1=ALU.mult).then_inc(normed, 1)
                    if k:
                        lower(k - 1)
                lower(KT - 1)

            def make_gate(layer, which):
                base = MOD_COLS * layer + 3 * KT * which + 2 * KT
                dve.wait_ge(mod_kept, (base + KT) // 4)
                link(dve.tensor_scalar(gate[:, :], modc[:, base:base + KT], 0.5, None, ALU.mult))

            def add_x(s, d, i, g):
                dve.wait_ge(unit_done, s + 1 + 4 * i)
                dve.scalar_tensor_tensor(out=xT[:, bass.ds(i * 4 + d, 1), :], in0=bank[s % 4][:, :].unsqueeze(1),
                                         scalar=g[:, bass.ds(i * 4 + d, 1)], in1=xT[:, bass.ds(i * 4 + d, 1), :],
                                         op0=ALU.mult, op1=ALU.add).then_inc(evicted, 1)

            def down_stats(down, st, g):
                for d in range(KT):
                    add_sq(st, d - 1)
                    add_x(down + d, d, 0, g)
                    lo(down + d + 4)

            def ffn(f, st):
                plan = mod_plan(f)
                for t, (f0, k) in enumerate(THIRDS):
                    up, down = third_units(f, t)
                    tile0 = HID_BASE[("ffn", f)] + f0
                    pair0 = PAIR_BASE[f] + f0
                    mod_up, mod_down = plan.get(("up", t)), plan.get(("down", t))

                    def up_body(i):
                        for q in range(2):
                            s = up + 2 * q
                            if mod_up is not None:
                                mod_ops(mod_up, i, 4 * q, 4 * q + 4)
                            dve.wait_ge(act_out, pair0 + q + 1 + 2 * i)
                            dve.tensor_tensor(dve_tmp[:, q, :], act_tmp[:, q, :], bank[(s + 1) % 4][:, :], ALU.mult)\
                                .then_inc(evicted, 2)
                            lo(s + 4, i)
                            dve.wait_ge(hid_rounded, tile0 + q + 1 + 2 * i)
                            dve.tensor_tensor(hid_lo[:, bass.ds(i * 2 + q, 1), :], dve_tmp[:, q:q + 1, :],
                                              hid_hi[:, bass.ds(i * 2 + q, 1), :].bitcast(F32), ALU.subtract)\
                                .then_inc(hid_ready, 1)
                            lo(s + 5, i)
                        if mod_up is not None:
                            mod_keep(mod_up, i)
                    with dve.Fori(0, k // 2) as i:
                        up_body(i)
                    if t == 0:
                        make_gate(f // 2, 2 * (f % 2))
                    if t < 2:
                        with dve.Fori(0, 2) as i:
                            for q in range(4):
                                if mod_down is not None:
                                    mod_ops(mod_down, i, 2 * q, 2 * q + 2)
                                add_x(down + q, q, i, gate)
                                lo(down + q + 4, i)
                            if mod_down is not None:
                                mod_keep(mod_down, i)
                    else:
                        down_stats(down, st, gate)

            def post(st, layer):
                spread_rstd(st)
                for d in range(KT):
                    at = 8 + KT * layer + d
                    dve.scalar_tensor_tensor(out=xT[:, d, :], in0=xT[:, d, :], scalar=cols[:, at:at + 1],
                                             in1=bank[RB][:, :], op0=ALU.mult, op1=ALU.mult).then_inc(posted, 1)

            def mask_rows(J, S, b, bias, scale):
                dve.wait_ge(s_done, NB * J + b + 1)
                if J >= 2 and b == 0:
                    dve.wait_ge(p_turned, NB * (J - 1))
                w = (b + 1) * P
                dve.tensor_tensor_reduce(out=S[J % 2][:, BOFF[b]:BOFF[b] + w], in0=bank[S_BANK[b % 2]][:, 0:w],
                                         in1=bias, scale=scale, scalar=-3e38, op0=ALU.add, op1=ALU.max,
                                         accum_out=rowmax[:, J % 2, b:b + 1]).then_inc(masked, 1)

            def negate_max(J):
                dve.wait_ge(masked, NB * (J + 1))
                dve.tensor_scalar(negmax[:, J % 2, :], rowmax[:, J % 2, :], -1.0, None, ALU.mult)\
                    .then_inc(negmax_ready, 1)

            def normalise(J, S):
                dve.wait_ge(exp_done, NB * (J + 1))
                link(dve.reciprocal(rowinv[:, J % 2, :], rowsum[:, J % 2, :]))
                for b in range(NB):
                    sb_ = S[J % 2][:, BOFF[b]:BOFF[b] + (b + 1) * P]
                    dve.tensor_scalar(sb_, sb_, rowinv[:, J % 2, b:b + 1], None, ALU.mult).then_inc(p_ready, 1)

            dve.wait_ge(const_ready, 6)
            dve.tensor_copy(ident_b[:, :], ident[:, :]).then_inc(bf_ready, 1)
            dve.wait_ge(rows_turned, 1)
            dve.tensor_copy(modb[:, :], bank[4][:, 32:32 + 2 * MOD_COLS])
            dve.tensor_copy(cols[:, :], bank[4][:, 0:28]).then_inc(cols_ready, 1)
            dve.wait_ge(cols_ready, 1)
            dve.tensor_scalar(kgain[:, 0:1], cols[:, 25:26], float(HD) ** 0.5, None, ALU.mult)
            link(dve.tensor_scalar(kgain[:, 1:2], cols[:, 27:28], float(HD) ** 0.5, None, ALU.mult))
            dve.wait_ge(cond_ready, 1)
            for ch in range(4):
                mod_ops(ch, 0, 0, 8)
                mod_keep(ch, 0)
                lo(ch)
            for d in range(KT):
                add_sq(0, d)
            norm(0, 0, 0, 0)
            ffn(0, 1)
            norm(1, 1, 0, 1)

            U = DSA_BASE
            for n in range(4):
                dve.wait_ge(unit_done, U + max(n + 1, 2))
                dve.tensor_copy(iq[:, n, :], bank[(U + n) % 2][:, :]).then_inc(evicted, 1)
                lo(U + 4 + n)
            dve.wait_ge(unit_done, U + 5)
            dve.tensor_copy(ikx[0:72, :], bank[(U + 4) % 2][0:72, :]).then_inc(evicted, 1)
            for g in range(KV_HEADS):
                dve.wait_ge(qk_sq, g + 1)
                dve.tensor_scalar(dsa_k[:, g, :], bank[(U + 5 + g) % 2][:, :], kgain[:, 0:1], None, ALU.mult)\
                    .then_inc(evicted, 1)
                lo(U + 8 + g)
            dve.wait_ge(iw_turned, 1)
            link(dve.tensor_scalar(iw[:, :], bank[T_BANK[0]][:, 0:NB * 8], float(IDX_HEADS * IDX_DIM) ** -0.5, None,
                                   ALU.mult))
            for m in range(3 * IDX_HEADS):
                b, head = m // IDX_HEADS + 1, m % IDX_HEADS
                dve.wait_ge(relu_ready, m + 1)
                w, at = (b + 1) * P, 8 * b + head
                sc = mask[:, BOFF[b]:BOFF[b] + w]
                if head == 0:
                    ins = dve.tensor_scalar(sc, relu[:, m % 2, 0:w], iw[:, at:at + 1], None, ALU.mult)
                else:
                    dve.wait_ge(relu_used, m)
                    ins = dve.scalar_tensor_tensor(out=sc, in0=relu[:, m % 2, 0:w], scalar=iw[:, at:at + 1], in1=sc,
                                                   op0=ALU.mult, op1=ALU.add)
                ins.then_inc(relu_used, 1)
            lo(U + 10)
            dve.wait_ge(qk_stat, 1)
            dve.tensor_scalar(var[:, 0, :], bank[STAT][:, 0:8], 1.0, HD * EPS, ALU.mult, ALU.add).then_inc(var_ready, 1)
            dve.wait_ge(rstd_ready, 3)
            for g in range(KV_HEADS):
                if g:
                    dve.wait_ge(k_rb, 1)
                make_diag(diag, 2, NB * g).then_inc(k_diag, 1)
                dve.wait_ge(k_rb, g + 1)
                dve.tensor_tensor(dsa_k[:, g, :], dsa_k[:, g, :], bank[KV_BANK[0]][:, :], ALU.mult).then_inc(k_ready, 1)

            def top_k(b):
                w = (b + 1) * P
                sc = mask[:, BOFF[b]:BOFF[b] + w]
                link(dve.memset(mask[0:CHUNK, BOFF[b] + w - CHUNK:BOFF[b] + w], OUTSIDE))
                for r in range(TOPK // 8):
                    link(dve.max(top8[:, :], sc))
                    link(dve.match_replace(out=sc, in_to_replace=top8[:, :], in_values=sc, imm_value=TAKEN))
                link(dve.tensor_scalar(sc, sc, (TAKEN + OUTSIDE) / 2, MASKED, ALU.is_gt, ALU.mult))

            def dsa_q_unit(j):
                n = U + 9 + j
                dve.wait_ge(qk_sq, 3 + j)
                dve.tensor_scalar(dsa_q[:, j % 2, :], bank[n % 2][:, :], cols[:, 24:25], None, ALU.mult)\
                    .then_inc(evicted, 1)
                lo(n + 4)

            def dsa_q_var(j):
                dve.wait_ge(qk_stat, 2 + j)
                dve.tensor_scalar(var[:, (3 + j) % 2, 0:NB], bank[STAT][:, 0:NB], 1.0, HD * EPS, ALU.mult, ALU.add)\
                    .then_inc(var_ready, 1)

            link(dve.memset(mask[:, 0:P], 0.0))
            link(dve.memset(mask[0:CHUNK, P - CHUNK:P], MASKED))
            top_k(1)
            lo(U + 11)
            lo(U + 12)
            dsa_q_unit(0)
            top_k(2)
            dsa_q_var(0)
            dsa_q_unit(1)
            top_k(3)
            dsa_q_var(1)
            for j in range(HEADS + 1):
                if j < HEADS:
                    dve.wait_ge(rstd_ready, 4 + j)
                    for b in range(NB):
                        mask_rows(j, dsa_S, b, mask[:, BOFF[b]:BOFF[b] + (b + 1) * P], rstd[:, (3 + j) % 2, b:b + 1])
                    negate_max(j)
                    normalise(j, dsa_S)
                if j:
                    dve.wait_ge(hid_rounded, HID_BASE["dsa"] + j)
                    dve.tensor_tensor(hid_lo[:, j - 1, :], bank[OB][:, :], hid_hi[:, j - 1, :].bitcast(F32),
                                      ALU.subtract).then_inc(hid_ready, 1)
                if j + 2 < HEADS:
                    dsa_q_unit(j + 2)
                    dsa_q_var(j + 2)
            down_stats(U + 17, 2, modc[:, 5 * KT:6 * KT])
            norm(2, 2, 0, 2)
            ffn(1, 3)
            post(3, 0)
            for d in range(KT):
                add_sq(4, d)
            norm(3, 4, 1, 0)
            ffn(2, 5)
            norm(4, 5, 1, 1)

            U = FOX_BASE
            z, z_small = dve_tmp[0:HEADS, 0, :], dve_tmp[0:HEADS, 1, :]
            dve.wait_ge(unit_done, U + 1)
            dve.memset(sq[0:HEADS, 0, :], 1.0)
            dve.tensor_scalar(z, bank[U % 2][0:HEADS, :], f_bias[:, 0:1], None, ALU.add).then_inc(evicted, 1)
            dve.wait_ge(evicted, U + 1)
            dve.scalar_tensor_tensor(out=z_small, in0=z, scalar=-1.0, in1=z, op0=ALU.mult, op1=ALU.min)\
                .then_inc(fz_ready, 1)
            lo(U + 4)
            dve.wait_ge(ls_ready, 2)
            link(dve.scalar_tensor_tensor(out=z, in0=z, scalar=0.0, in1=z_small, op0=ALU.min, op1=ALU.subtract))
            dve.tensor_tensor_scan(cum[0:HEADS, :], sq[0:HEADS, 0, :], z, 0.0, ALU.mult, ALU.add)\
                .then_inc(cum_ready, 1)
            dve.wait_ge(cum_ready, 1)

            def fox_units(j):
                n, par = U + 1 + 4 * j, j % 2
                for q, (dst, g) in enumerate(((fox_q, cols[:, 26:27]), (fox_k, kgain[:, 1:2]))):
                    dve.wait_ge(qk_sq, 11 + 2 * j + q)
                    dve.tensor_scalar(dst[:, par, :], bank[(n + q) % 2][:, :], g, None, ALU.mult).then_inc(evicted, 1)
                    lo(n + q + 4)
                dve.wait_ge(qk_stat, 10 + j)
                dve.tensor_scalar(var[:, (15 + j) % 2, :], bank[STAT][:, 0:8], 1.0, HD * EPS, ALU.mult, ALU.add)\
                    .then_inc(var_ready, 1)
                dve.wait_ge(rstd_ready, 16 + j)
                make_diag(diag, 15 + j, 0).then_inc(k_diag, 1)
                dve.wait_ge(k_rb, 3 + 2 * j)
                dve.tensor_tensor(fox_q[:, par, :], fox_q[:, par, :], bank[KV_BANK[0]][:, :], ALU.mult)
                make_diag(diag, 15 + j, NB).then_inc(k_diag, 1)
                dve.wait_ge(k_rb, 4 + 2 * j)
                dve.tensor_tensor(fox_k[:, par, :], fox_k[:, par, :], bank[KV_BANK[1]][:, :], ALU.mult)\
                    .then_inc(k_ready, 1)
                lo(n + 6)
                lo(n + 7)

            fox_units(0)
            for j in range(HEADS + 1):
                J = HEADS + j
                if j < HEADS:
                    dve.wait_ge(nb_ready, j + 1)
                    for b in range(NB):
                        mask_rows(J, fox_S, b, fox_nb[:, j % 2, 0:(b + 1) * P], 1.0)
                    negate_max(J)
                    normalise(J, fox_S)
                if j:
                    dve.wait_ge(pv_done, J)
                    dve.wait_ge(hid_ready, HID_BASE["fox"] + j - 1)
                    dve.tensor_tensor(dve_tmp[:, 1, :], bank[OB][:, :], fox_sig[:, (j - 1) % 2, :], ALU.mult)\
                        .then_inc(gated, 1)
                    dve.wait_ge(hid_rounded, HID_BASE["fox"] + j)
                    dve.tensor_tensor(hid_lo[:, j - 1, :], dve_tmp[:, 1, :], hid_hi[:, j - 1, :].bitcast(F32),
                                      ALU.subtract).then_inc(hid_ready, 1)
                if j + 1 < HEADS:
                    fox_units(j + 1)
            down_stats(U + 33, 6, modc[:, MOD_COLS + 5 * KT:MOD_COLS + 6 * KT])
            norm(5, 6, 1, 2)
            ffn(3, 7)
            post(7, 1)
            for d in range(1, KT, 2):
                dve.wait_ge(y_turned, d + 1)
                dve.tensor_copy(y_out[:, :, d * P:(d + 1) * P],
                                bank[d % 4][:, :].rearrange("p (b n) -> p b n", b=NB)).then_inc(y_copied_d, 1)

        @block.tensor
        def _(pe):
            def three(dst, s, k, hi_, lo_, first, last):
                w = s % RING
                pe.matmul(dst, whi[:, w, k, :], hi_, start=first, stop=False)
                pe.matmul(dst, whi[:, w, k, :], lo_, start=False, stop=False)
                return pe.matmul(dst, wlo[:, w, k, :], hi_, start=False, stop=last)

            def unit(s, i, dst, K, A_hi, A_lo, free, ready=None):
                pe.wait_ge(lo_ready, s + 1 + RING * i)
                if free > 0 or not isinstance(i, int):
                    pe.wait_ge(evicted, free + RING * i)
                for k in range(K):
                    if ready is not None:
                        pe.wait_ge(hid_ready, ready + k + 1)
                    ins = three(dst, s, k, A_hi[:, k, :], A_lo[:, k, :], k == 0, k == K - 1)
                ins.then_inc(unit_done, 1)

            def pair(s, i, banks, free, v=None):
                pe.wait_ge(lo_ready, s + 2 + RING * i)
                if s > 2 or not isinstance(i, int):
                    pe.wait_ge(evicted, free + RING * i)
                for k in range(KT):
                    if v is not None:
                        pe.wait_ge(h_ready, KT * v + k + 1)
                    for q in range(2):
                        ins = three(bank[banks[q]][:, :], s + q, k, h_hi[:, k, :], h_lo[:, k, :], k == 0, k == KT - 1)
                ins.then_inc(unit_done, 2)

            def mod_sum(c0, i):
                pe.wait_ge(mod_step, 8 * (c0 + 1) + 8 * i)
                if c0:
                    pe.wait_ge(mod_kept, c0 + i)
                for q in range(4):
                    ins = pe.matmul(bank[MODB][:, q:q + 1], mod_acc[:, q * P:(q + 1) * P], ones[:, 0:1], start=True,
                                    stop=True)
                ins.then_inc(mod_summed, 1)

            def stat(st):
                pe.wait_ge(ssum_added, 6 * (st + 1))
                pe.wait_ge(sq_ready, KT * (st + 1))
                for b in range(NB):
                    pe.matmul(bank[OB][:, b:b + 1], ssum[:, b * P:(b + 1) * P], ones[:, 0:1], start=True, stop=False)
                    ins = pe.matmul(bank[OB][:, b:b + 1], sq[:, 1, b * P:(b + 1) * P], ones[:, 0:1], start=False,
                                    stop=True)
                ins.then_inc(stat_done, 1)
                pe.wait_ge(diag_ready, st + 1)
                pe.matmul(bank[RB][:, :], ones[:, :], diag[:, :, :], start=True, stop=True).then_inc(rb_ready, 1)

            def ffn(f, v):
                plan = mod_plan(f)
                for t, (f0, k) in enumerate(THIRDS):
                    up, down = third_units(f, t)
                    mod_up, mod_down = plan.get(("up", t)), plan.get(("down", t))

                    def up_body(i, first):
                        for q in range(2):
                            s = up + 2 * q
                            pair(s, i, (s % 4, (s + 1) % 4), s - 2, v if first and q == 0 else None)
                        if mod_up is not None:
                            mod_sum(mod_up, i)
                    if t == 0:
                        up_body(0, True)
                        up += 4
                        if mod_up is not None:
                            mod_up += 1
                        with pe.Fori(0, k // 2 - 1) as i:
                            up_body(i, False)
                    else:
                        with pe.Fori(0, k // 2) as i:
                            up_body(i, False)
                    tile0 = HID_BASE[("ffn", f)] + f0

                    def down_body(i, q0, n):
                        for q in range(q0, n):
                            s = down + q
                            unit(s, i, bank[s % 4][:, :], k, hid_hi, hid_lo, s - 3, tile0 if q == 0 and t == 2 else None)
                    if t < 2:
                        pe.wait_ge(hid_ready, tile0 + k)
                        with pe.Fori(0, 2) as i:
                            down_body(i, 0, 4)
                            if mod_down is not None:
                                mod_sum(mod_down, i)
                    else:
                        down_body(0, 0, KT)

            def turn_p(J, S, t):
                if t == 0:
                    pe.wait_ge(p_ready, NB * (J + 1))
                if J or t >= 2:
                    pe.wait_ge(pt_ready, NB * J + t - 1)
                for b in range(t, NB):
                    ins = pe.transpose(bank[T_BANK[t % 2]][:, (b - t) * P:(b - t + 1) * P],
                                       S[J % 2][:, BOFF[b] + t * P:BOFF[b] + (t + 1) * P], ident[:, :])
                ins.then_inc(p_turned, 1)

            def pv(J, PT, V):
                pe.wait_ge(pt_ready, NB * (J + 1))
                for t in range(NB):
                    ins = pe.matmul(bank[OB][:, t * P:SEQ], V[:, t, :], PT[J % 2][:, TOFF[t]:TOFF[t] + (NB - t) * P],
                                    start=(t == 0), stop=(t == NB - 1))
                ins.then_inc(pv_done, 1)

            pe.wait_ge(small_load, 16 * 9)
            pe.wait_ge(const_ready, 6)
            pe.transpose(bank[4][:, 0:28], rows[0:28, :], ident[0:28, 0:28])
            for l in range(2):
                ins = pe.transpose(bank[4][:, 32 + MOD_COLS * l:32 + MOD_COLS * (l + 1)], modb_rows[0:MOD_COLS, l, :],
                                   ident[0:MOD_COLS, 0:MOD_COLS])
            ins.then_inc(rows_turned, 1)
            pe.wait_ge(x_load, 16 * NB)
            for k in range(KT):
                if k >= 4:
                    pe.wait_ge(xt_copied, k - 3)
                for b in range(NB):
                    ins = pe.transpose(bank[k % 4][:, b * P:(b + 1) * P], x_in[:, b, k * P:(k + 1) * P], ident[:, :])
                ins.then_inc(xt_done, 1)
            for ch in range(4):
                mod_sum(ch, 0)
            stat(0)
            ffn(0, 0)
            stat(1)

            U = DSA_BASE
            pair(U, 0, (U % 2, (U + 1) % 2), U, 1)
            for n in range(2, 7):
                unit(U + n, 0, bank[(U + n) % 2][:, :], KT, h_hi, h_lo, U + n - 1)
            pe.wait_ge(ik_spread, 32)
            for b in range(NB):
                ins = pe.transpose(bank[T_BANK[0]][:, 8 * b:8 * b + 8], act_tmp[0:8, 0, b * P:(b + 1) * P],
                                   ident[0:8, 0:8])
            ins.then_inc(iw_turned, 1)
            for m in range(3 * IDX_HEADS):
                b, head = m // IDX_HEADS + 1, m % IDX_HEADS
                if m >= 2:
                    pe.wait_ge(relu_ready, m - 1)
                r = 64 * (head % 2)
                ik = ikx if head % 2 == 0 else ikd
                pe.matmul(bank[S_BANK[m % 2]][:, 0:(b + 1) * P], iq[r:r + 64, head // 2, b * P:(b + 1) * P],
                          ik[r:r + 64, 0:(b + 1) * P], start=True, stop=True).then_inc(dots_done, 1)
            pe.wait_ge(qk_sq, 2)
            for g in range(KV_HEADS):
                for b in range(NB):
                    ins = pe.matmul(bank[STAT][:, NB * g + b:NB * g + b + 1], sq[:, g, b * P:(b + 1) * P],
                                    ones[:, 0:1], start=True, stop=True)
            ins.then_inc(qk_stat, 1)
            unit(U + 7, 0, bank[(U + 7) % 2][:, :], KT, h_hi, h_lo, U + 6)
            pe.wait_ge(k_diag, 1)
            pe.matmul(bank[KV_BANK[0]][:, :], ones[:, :], diag[:, :, :], start=True, stop=True).then_inc(k_rb, 1)
            unit(U + 8, 0, bank[(U + 8) % 2][:, :], KT, h_hi, h_lo, U + 7)
            pe.wait_ge(k_diag, 2)
            pe.wait_ge(k_ready, 1)
            pe.matmul(bank[KV_BANK[0]][:, :], ones[:, :], diag[:, :, :], start=True, stop=True).then_inc(k_rb, 1)
            pe.wait_ge(evicted, U + 9)
            pe.wait_ge(k_ready, 2)
            for g in range(KV_HEADS):
                for b in range(NB):
                    ins = pe.transpose(bank[T_BANK[g]][:, b * P:(b + 1) * P], dsa_vT[:, g, b * P:(b + 1) * P],
                                       ident[:, :])
                ins.then_inc(v_turned, 1)

            def dsa_q_unit(j):
                n = U + 9 + j
                unit(n, 0, bank[n % 2][:, :], KT, h_hi, h_lo, n - 1)
                pe.wait_ge(qk_sq, 3 + j)
                pe.wait_ge(var_ready, 3 + j)
                for b in range(NB):
                    ins = pe.matmul(bank[STAT][:, b:b + 1], sq[:, j % 2, b * P:(b + 1) * P], ones[:, 0:1], start=True,
                                    stop=True)
                ins.then_inc(qk_stat, 1)

            def dsa_score(j, b):
                if j or b >= 2:
                    pe.wait_ge(masked, NB * j + b - 1)
                pe.matmul(bank[S_BANK[b % 2]][:, 0:(b + 1) * P], dsa_q[:, j % 2, b * P:(b + 1) * P],
                          dsa_k[:, j // GROUP, 0:(b + 1) * P], start=True, stop=True).then_inc(s_done, 1)

            dsa_q_unit(0)
            dsa_q_unit(1)
            pe.wait_ge(v_ready, 2)
            for j in range(HEADS + 1):
                for b in range(NB):
                    if j < HEADS:
                        if b == 0:
                            pe.wait_ge(evicted, U + 10 + j)
                        dsa_score(j, b)
                    if j:
                        turn_p(j - 1, dsa_S, b)
                if j:
                    if j >= 2:
                        pe.wait_ge(hid_ready, HID_BASE["dsa"] + j - 1)
                    pv(j - 1, dsa_PT, dsa_v[:, (j - 1) // GROUP, :, :])
                if j + 2 < HEADS:
                    dsa_q_unit(j + 2)
            for d in range(KT):
                s = U + 17 + d
                unit(s, 0, bank[s % 4][:, :], KT, hid_hi, hid_lo, s - 1, HID_BASE["dsa"] if d == 0 else None)
            stat(2)
            ffn(1, 2)
            stat(3)
            stat(4)
            ffn(2, 3)
            stat(5)

            U = FOX_BASE
            pe.wait_ge(h_ready, KT * 5)
            unit(U, 0, bank[U % 2][:, :], KT, h_hi, h_lo, U)

            def fox_units(j):
                n, par = U + 1 + 4 * j, j % 2
                unit(n, 0, bank[n % 2][:, :], KT, h_hi, h_lo, n - 1)
                if j == 0:
                    pe.wait_ge(cum_ready, 1)
                    pe.wait_ge(negsel_ready, 2)
                else:
                    pe.wait_ge(nb_ready, j)
                    if j > 1:
                        pe.wait_ge(gated, j - 1)
                pe.matmul(bank[OB][:, :], negsel[0:HEADS, j, :], cum[0:HEADS, :], start=True, stop=True)\
                    .then_inc(nb_done, 1)
                unit(n + 1, 0, bank[(n + 1) % 2][:, :], KT, h_hi, h_lo, n)
                pe.wait_ge(qk_sq, 12 + 2 * j)
                if j:
                    pe.wait_ge(k_ready, 2 + j)
                for q in range(2):
                    for b in range(NB):
                        ins = pe.matmul(bank[STAT][:, NB * q + b:NB * q + b + 1], act_tmp[:, q, b * P:(b + 1) * P],
                                        ones[:, 0:1], start=True, stop=True)
                ins.then_inc(qk_stat, 1)
                unit(n + 2, 0, bank[n % 2][:, :], KT, h_hi, h_lo, n + 1)
                for q in range(2):
                    pe.wait_ge(k_diag, 3 + 2 * j + q)
                    pe.matmul(bank[KV_BANK[q]][:, :], ones[:, :], diag[:, :, :], start=True, stop=True)\
                        .then_inc(k_rb, 1)
                unit(n + 3, 0, bank[(n + 1) % 2][:, :], KT, h_hi, h_lo, n + 2)
                pe.wait_ge(evicted, n + 3)
                for b in range(NB):
                    ins = pe.transpose(bank[T_BANK[0]][:, b * P:(b + 1) * P], fox_vT[:, b * P:(b + 1) * P], ident[:, :])
                ins.then_inc(v_turned, 1)

            def fox_score(j, b):
                J = HEADS + j
                pe.wait_ge(masked, NB * J + b - 1)
                w = (b + 1) * P
                dst = bank[S_BANK[b % 2]]
                pe.matmul(dst[:, 0:w], fox_q[:, j % 2, b * P:w], fox_k[:, j % 2, 0:w], start=True, stop=False)
                pe.matmul(dst[:, b * P:w], ident_b[:, :], causal[:, :], start=False, stop=True).then_inc(s_done, 1)

            pe.wait_ge(bf_ready, 1)
            fox_units(0)
            for j in range(HEADS + 1):
                J = HEADS + j
                for b in range(NB):
                    if j < HEADS:
                        if b == 0:
                            pe.wait_ge(k_ready, 3 + j)
                        fox_score(j, b)
                    if j:
                        if b == 0:
                            pe.wait_ge(v_ready, 2 + min(j + 1, HEADS))
                        turn_p(J - 1, fox_S, b)
                if j:
                    pe.wait_ge(nb_ready, min(j + 1, HEADS))
                    if j >= 2:
                        pe.wait_ge(gated, j - 1)
                    pv(J - 1, fox_PT, fox_v[:, (j - 1) % 2, :, :])
                if j + 1 < HEADS:
                    if j:
                        pe.wait_ge(gated, j)
                    fox_units(j + 1)
            for d in range(KT):
                s = U + 33 + d
                unit(s, 0, bank[s % 4][:, :], KT, hid_hi, hid_lo, s - 1, HID_BASE["fox"] if d == 0 else None)
            stat(6)
            ffn(3, 5)
            stat(7)
            for d in range(KT):
                pe.wait_ge(posted, KT + d + 1)
                if d >= 4:
                    pe.wait_ge((y_copied_a, y_copied_d)[d % 2], d // 2 - 1)
                for b in range(NB):
                    ins = pe.transpose(bank[d % 4][:, b * P:(b + 1) * P], xT[:, d, b * P:(b + 1) * P], ident[:, :])
                ins.then_inc(y_turned, 1)


HID_BASE = {("ffn", 0): 0, "dsa": 22, ("ffn", 1): 30, ("ffn", 2): 52, "fox": 74, ("ffn", 3): 82}
PAIR_BASE = [0, 22, 44, 66]

_INS = ['x', 'c', 'mod_w', 'mod_b', 'ffn1_w_gu', 'ffn1_w_down', 'ffn2_w_gu', 'ffn2_w_down', 'post_gain',
        'dsa_w_in', 'dsa_q_gain', 'dsa_k_gain', 'dsa_w_out',
        'fox_w_in', 'fox_f_bias', 'fox_q_gain', 'fox_k_gain', 'fox_w_out']


def kernel(**inputs):
    import numpy as _np
    import concourse.bacc as _bacc
    from concourse import mybir as _mybir
    from concourse.bass_utils import run_bass_kernel_spmd as _run

    nc = _bacc.Bacc("TRN2", target_bir_lowering=False, num_devices=1)
    arrays, args = {}, []
    for name in _INS:
        a = _np.ascontiguousarray(inputs[name])
        arrays[f"in_{name}_dram"] = a
        args.append(nc.dram_tensor(f"in_{name}_dram", a.shape, _mybir.dt.from_np(a.dtype), kind="ExternalInput").ap())
    args.append(nc.dram_tensor("out_0_dram", (1, SEQ, D), _mybir.dt.float32, kind="ExternalOutput").ap())
    build(nc, *args)
    r = _run(nc, [arrays], core_ids=[0])
    return r.results[0]["out_0_dram"]
```

```python
from contextlib import ExitStack

import concourse.bass as bass
from concourse import mybir
from concourse.alu_op_type import AluOpType as ALU

F32 = mybir.dt.float32
F32R = mybir.dt.float32r
BF16 = mybir.dt.bfloat16
ACT = mybir.ActivationFunctionType

P = 128
D = 1024
SEQ = 512
KT = D // P
NB = SEQ // P
D_FF = 2816
FF_TILES = D_FF // P
THIRDS = [(0, 8), (8, 8), (16, FF_TILES - 16)]
EPS = 1e-6
HEADS = 8
KV_HEADS = 2
GROUP = HEADS // KV_HEADS
HD = 128
IDX_HEADS = 8
IDX_DIM = 64
CHUNK = 64
TOPK = 128
MASKED = -1e30
OUTSIDE = -2e38
TAKEN = -3e38
RING = 4
MODC = 512
MOD_COLS = 9 * D // P
MOD_CHUNKS = 9 * D // MODC
BOFF = [0, 128, 384, 768]
KEYS = 1280
TOFF = [0, 512, 896, 1152]

FFN_UNITS = 2 * FF_TILES + 3 * KT
DSA_UNITS = 5 + 2 * KV_HEADS + HEADS + KT
FOX_UNITS = 1 + 4 * HEADS + KT
FFN_BASE = [0, FFN_UNITS + DSA_UNITS, 2 * FFN_UNITS + DSA_UNITS, 3 * FFN_UNITS + DSA_UNITS + FOX_UNITS]
DSA_BASE = FFN_UNITS
FOX_BASE = 3 * FFN_UNITS + DSA_UNITS
UNITS = 4 * FFN_UNITS + DSA_UNITS + FOX_UNITS

FFN_MOD = [(4, 16), (16, 28), (28, 36), (36, 36)]


def third_units(f, t):
    base = FFN_BASE[f] + sum(2 * THIRDS[u][1] + KT for u in range(t))
    return base, base + 2 * THIRDS[t][1]


def mod_plan(f):
    c, end = FFN_MOD[f]
    plan = {}
    loops = [("up", 0), ("down", 0), ("up", 1), ("down", 1)] if end - c == 12 else [("up", 0), ("up", 1)]
    for name in loops:
        if c < end:
            plan[name] = c
            c += 4 if name[0] == "up" else 2
    return plan


def build(nc, x, c, mod_w, mod_b, ffn1_w_gu, ffn1_w_down, ffn2_w_gu, ffn2_w_down, post_gain,
          dsa_w_in, dsa_q_gain, dsa_k_gain, dsa_w_out,
          fox_w_in, fox_f_bias, fox_q_gain, fox_k_gain, fox_w_out, out):
    ctx = ExitStack()
    with ctx:
        def sb(name, shape, dt=F32):
            return ctx.enter_context(nc.sbuf_tensor(name, shape, dt))

        def sem(name):
            return ctx.enter_context(nc.semaphore(name))

        wraw = sb("wraw", [P, RING, KT, P])
        whi = sb("whi", [P, RING, KT, P], F32R)
        wlo = sb("wlo", [P, RING, KT, P], F32R)
        xT = sb("xT", [P, KT, SEQ])
        h_hi = sb("h_hi", [P, KT, SEQ], F32R)
        h_lo = sb("h_lo", [P, KT, SEQ], F32R)
        hid_hi = sb("hid_hi", [P, KT, SEQ], F32R)
        hid_lo = sb("hid_lo", [P, KT, SEQ], F32R)
        mod_raw = sb("mod_raw", [P, 2, 2, MODC])
        mod_acc = sb("mod_acc", [P, MODC])
        act_tmp = sb("act_tmp", [P, 2, SEQ])
        dve_tmp = sb("dve_tmp", [P, 2, SEQ])
        sq = sb("sq", [P, 2, SEQ])
        ssum = sb("ssum", [P, SEQ])
        diag = sb("diag", [P, NB, P])
        ident = sb("ident", [P, P])
        ident_b = sb("ident_b", [P, P], BF16)
        causal = sb("causal", [P, P], BF16)
        ones = sb("ones", [P, P])
        minus_half = sb("minus_half", [P, NB * HEADS])
        modb = sb("modb", [P, 2 * MOD_COLS])
        modc = sb("modc", [P, 2 * MOD_COLS])
        cols = sb("cols", [P, 28])
        cond = sb("cond", [P, KT])
        scale1 = sb("scale1", [P, KT])
        gate = sb("gate", [P, KT])
        kgain = sb("kgain", [P, 2])
        f_bias = sb("f_bias", [HEADS, 1])
        var = sb("var", [P, 2, NB * HEADS])
        rstd = sb("rstd", [P, 2, NB * HEADS])
        rowmax = sb("rowmax", [P, 2, NB])
        negmax = sb("negmax", [P, 2, NB])
        rowsum = sb("rowsum", [P, 2, NB])
        rowinv = sb("rowinv", [P, 2, NB])
        iw = sb("iw", [P, NB * 8])
        top8 = sb("top8", [P, 8])
        qk = sb("qk", [P, 4, SEQ], F32R)
        ARENA = 10240
        arena = sb("arena", [P, ARENA])

        def piece(at, n):
            return arena[:, at:at + n]

        x_in = piece(0, NB * D).rearrange("p (b n) -> p b n", b=NB)
        rows = piece(4096, 128)
        modb_rows = piece(4224, 256).rearrange("p (l n) -> p l n", l=2)
        y_out = piece(0, NB * D).rearrange("p (b n) -> p b n", b=NB)
        mod_slots = ([piece(4608 + 1024 * s, 2 * MODC).rearrange("p (a n) -> p a n", a=2) for s in range(5)]
                     + [mod_raw[:, s, :, :] for s in range(2)])
        iq = piece(0, 4 * SEQ).rearrange("p (t n) -> p t n", t=4)
        relu = piece(2048, 2 * SEQ).rearrange("p (t n) -> p t n", t=2)
        ikx = piece(3072, SEQ)
        ikd = piece(3584, SEQ)
        mask = piece(4096, KEYS)
        dsa_k = piece(5376, 2 * SEQ).rearrange("p (t n) -> p t n", t=2)
        dsa_v = piece(6400, 2 * SEQ).rearrange("p (t s n) -> p t s n", t=2, s=NB)
        dsa_vT = piece(7424, 2 * SEQ).rearrange("p (t n) -> p t n", t=2)
        dsa_S = [piece(8448, KEYS), piece(0, KEYS)]
        dsa_PT = piece(1280, KEYS)
        fox_qk = piece(0, 2 * SEQ).rearrange("p (t n) -> p t n", t=2)
        fox_v = piece(1024, 2 * SEQ).rearrange("p (t s n) -> p t s n", t=2, s=NB)
        fox_vT = piece(2048, SEQ)
        fox_sig = piece(2560, 2 * SEQ).rearrange("p (t n) -> p t n", t=2)
        fox_nb = piece(3584, 2 * SEQ).rearrange("p (t n) -> p t n", t=2)
        cum = piece(4608, SEQ)
        fox_S = [piece(5120, KEYS), piece(6400, KEYS)]
        fox_PT = piece(7680, KEYS)
        negsel = piece(8960, HEADS * P).rearrange("p (h n) -> p h n", h=HEADS)
        diag_tmp = dve_tmp[:, 0, :].rearrange("p (b n) -> p b n", b=NB)
        diag_k = sq[:, 0, :].rearrange("p (b n) -> p b n", b=NB)

        bank = [ctx.enter_context(nc.psum_tensor(f"bank{i}", [P, SEQ], F32)) for i in range(8)]
        S_BANK, T_BANK, KV_BANK, STAT, RB, MODB, OB, VB = (4, 5), (6, 2), (2, 3), 3, 6, 5, 7, 4
        K_BANK = (2, 6)

        raw_in = [sem(f"raw_in{s}") for s in range(RING)]
        hi_ready, lo_ready, unit_done, evicted = sem("hi_ready"), sem("lo_ready"), sem("unit_done"), sem("evicted")
        x_load, small_load, const_ready, bf_ready = sem("x_load"), sem("small_load"), sem("const_ready"), sem("bf_ready")
        rows_turned, cols_ready, cond_ready = sem("rows_turned"), sem("cols_ready"), sem("cond_ready")
        xt_done, xt_copied = sem("xt_done"), sem("xt_copied")
        mod_in = [sem(f"mod_in{s}") for s in range(2)]
        mod_first = [sem(f"mod_first{s}") for s in range(7)]
        mod_step, mod_summed, mod_kept = sem("mod_step"), sem("mod_summed"), sem("mod_kept")
        sq_ready, ssum_added, stat_done = sem("sq_ready"), sem("ssum_added"), sem("stat_done")
        var_ready, rstd_ready, diag_ready, rb_ready = sem("var_ready"), sem("rstd_ready"), sem("diag_ready"), sem("rb_ready")
        normed, h_rounded, h_ready = sem("normed"), sem("h_rounded"), sem("h_ready")
        act_out, hid_rounded, hid_ready = sem("act_out"), sem("hid_rounded"), sem("hid_ready")
        posted = sem("posted")
        linked = sem("linked")
        ik_spread, iw_turned, dots_done, relu_ready, relu_used = (
            sem("ik_spread"), sem("iw_turned"), sem("dots_done"), sem("relu_ready"), sem("relu_used"))
        qk_sq, qk_stat, k_diag, k_rb, k_ready = sem("qk_sq"), sem("qk_stat"), sem("k_diag"), sem("k_rb"), sem("k_ready")
        v_turned, v_ready = sem("v_turned"), sem("v_ready")
        q_rounded, qk_normed, qk_rounded = sem("q_rounded"), sem("qk_normed"), sem("qk_rounded")
        s_done, masked, negmax_ready, exp_done, p_ready = (
            sem("s_done"), sem("masked"), sem("negmax_ready"), sem("exp_done"), sem("p_ready"))
        p_turned, pt_ready, pv_done, gated = sem("p_turned"), sem("pt_ready"), sem("pv_done"), sem("gated")
        fz_ready, ls_ready, cum_ready = sem("fz_ready"), sem("ls_ready"), sem("cum_ready")
        nb_done, nb_ready, negsel_ready = sem("nb_done"), sem("nb_ready"), sem("negsel_ready")
        y_turned, y_copied_a, y_copied_d, stored = sem("y_turned"), sem("y_copied_a"), sem("y_copied_d"), sem("stored")

        def gu(f):
            return (ffn1_w_gu, ffn2_w_gu)[f % 2][f // 2]

        def dn(f):
            return (ffn1_w_down, ffn2_w_down)[f % 2][f // 2]

        def blocks(w, r0, k, c0, n):
            return w[r0:r0 + k * P, bass.ds(c0, n)].rearrange("(k p) n -> p k n", p=P)

        DSA_SRC = ([(dsa_w_in, 1536 + P * j, P) for j in range(4)] + [(dsa_w_in, 2048, IDX_DIM + IDX_HEADS)]
                   + [(dsa_w_in, 1024 + P * j, P) for j in range(2)] + [(dsa_w_in, 1280, P)]
                   + [(dsa_w_in, P * j, P) for j in range(HEADS)] + [(dsa_w_in, 1280 + P, P)]
                   + [(dsa_w_out, P * j, P) for j in range(KT)])
        FOX_SRC = [(fox_w_in, 3072, HEADS)]
        for j in range(HEADS):
            FOX_SRC += [(fox_w_in, P * j, P), (fox_w_in, 1024 + P * j, P), (fox_w_in, 2048 + P * j, P),
                        (fox_w_in, 3072 + HEADS + P * j, P)]
        FOX_SRC += [(fox_w_out, P * j, P) for j in range(KT)]

        block = ctx.enter_context(nc.Block())

        @block.sync
        def _(sp):
            def load(s, i, src, k, n):
                if s >= RING:
                    sp.wait_ge(lo_ready, s - RING + 1 + RING * i)
                sp.dma_start(wraw[:, s % RING, 0:k, 0:n], src).then_inc(raw_in[s % RING], 16)

            def ffn(f):
                for t, (f0, k) in enumerate(THIRDS):
                    up, down = third_units(f, t)

                    def up_body(up, f0, i):
                        for q in range(4):
                            col = (q % 2) * D_FF + (f0 + q // 2) * P + i * (2 * P)
                            load(up + q, i, blocks(gu(f), 0, KT, col, P), KT, P)
                    if up == 0:
                        up_body(up, f0, 0)
                        for m in range(7, 16):
                            first_fill(m)
                        with sp.Fori(0, k // 2 - 1) as i:
                            up_body(up + 4, f0 + 2, i)
                    else:
                        with sp.Fori(0, k // 2) as i:
                            up_body(up, f0, i)
                    with sp.Fori(0, 2) as i:
                        for q in range(4):
                            load(down + q, i, blocks(dn(f), f0 * P, k, q * P + i * (4 * P), P), k, P)

            def first_fill(f):
                if f >= 7:
                    sp.wait_ge(mod_step, 2 * (f - 6))
                sp.dma_start(mod_slots[f % 7], blocks(mod_w[0], 2 * (f % 4) * P, 2, (f // 4) * MODC, MODC))\
                    .then_inc(mod_first[f % 7], 16)

            for f in range(7):
                first_fill(f)
            ffn(0)
            for j, (w, c0, n) in enumerate(DSA_SRC):
                load(DSA_BASE + j, 0, blocks(w[0], 0, KT, c0, n), KT, n)
            ffn(1)
            ffn(2)
            for j, (w, c0, n) in enumerate(FOX_SRC):
                load(FOX_BASE + j, 0, blocks(w[0], 0, KT, c0, n), KT, n)
            ffn(3)
            for half in range(2):
                sp.wait_ge(y_copied_a, 2 * half + 2)
                sp.wait_ge(y_copied_d, 2 * half + 2)
                sp.dma_start(out[0, :, half * 512:(half + 1) * 512].rearrange("(b p) n -> p b n", p=P),
                             y_out[:, :, half * 512:(half + 1) * 512]).then_inc(stored, 16)
            sp.wait_ge(stored, 32)

        @block.gpsimd
        def _(pool):
            pool.memset(ident[:, :], 0.0).then_inc(const_ready, 1)
            pool.memset(causal[:, :], 0.0).then_inc(const_ready, 1)
            pool.memset(ones[:, :], 1.0).then_inc(const_ready, 1)
            pool.memset(minus_half[:, :], -0.5).then_inc(const_ready, 1)
            pool.wait_ge(const_ready, 4)
            pool.affine_select(out=ident[:, :], in_=ident[:, :], compare_op=ALU.not_equal, fill=1.0, base=0,
                               pattern=[[-1, P]], channel_multiplier=1).then_inc(const_ready, 1)
            pool.affine_select(out=causal[:, :], in_=causal[:, :], compare_op=ALU.is_ge, fill=MASKED, base=0,
                               pattern=[[-1, P]], channel_multiplier=1).then_inc(const_ready, 1)

            def fill(c0, i, q):
                layer, col = c0 // MOD_CHUNKS, (c0 % MOD_CHUNKS) * MODC + i * MODC
                if 4 * c0 + q >= 18:
                    pool.wait_ge(mod_step, 2 * (4 * c0 + q - 1) + i * 8)
                pool.dma_start(mod_raw[:, q % 2, :, :], blocks(mod_w[layer], 2 * q * P, 2, col, MODC))\
                    .then_inc(mod_in[q % 2], 16)

            def chunks(c0, c1):
                with pool.Fori(0, c1 - c0) as i:
                    for q in range(4):
                        fill(c0, i, q)

            def job(j, n):
                pool.wait_ge(var_ready, j + 1)
                pool.tensor_tensor(rstd[:, j % 2, 0:n], var[:, j % 2, 0:n], minus_half[:, 0:n], ALU.pow)\
                    .then_inc(rstd_ready, 1)

            job(0, 4)
            pool.wait_ge(mod_step, 32)
            for q in range(4):
                fill(4, 0, q)
            chunks(5, 16)
            job(1, 4)
            pool.wait_ge(evicted, DSA_BASE + 5)
            pool.dma_start(ikd[64:128, :], ikx[0:64, :]).then_inc(ik_spread, 16)
            pool.dma_start(act_tmp[0:8, 0, :], ikx[64:72, :]).then_inc(ik_spread, 16)
            job(2, 8)
            job(3, NB * HEADS)
            job(4, 4)
            chunks(16, 18)
            chunks(18, 28)
            job(5, 4)
            job(6, 4)
            chunks(28, 36)
            job(7, 4)
            pool.memset(negsel[0:HEADS, :, :], 0.0).then_inc(negsel_ready, 1)
            pool.wait_ge(negsel_ready, 1)
            pool.affine_select(out=negsel[0:HEADS, :, :], in_=negsel[0:HEADS, :, :], compare_op=ALU.not_equal,
                               fill=-1.0, base=0, pattern=[[-1, HEADS], [0, P]], channel_multiplier=1)\
                .then_inc(negsel_ready, 1)
            for j in range(HEADS):
                job(8 + j, 8)
            job(16, 4)
            job(17, 4)

        NORM_JOB = [0, 1, 4, 5, 6, 7, 16, 17]

        @block.scalar
        def _(act):
            def hi(s, i=0):
                if s >= UNITS:
                    return
                act.wait_ge(raw_in[s % RING], 16 * (s // RING + 1) + 16 * i)
                if s >= RING:
                    act.wait_ge(unit_done, s - RING + 1 + RING * i)
                act.activation(whi[:, s % RING, :, :], wraw[:, s % RING, :, :], ACT.Copy).then_inc(hi_ready, 1)

            def square(st, d):
                if d == 0:
                    if st:
                        act.wait_ge(stat_done, st)
                    act.activation(ssum[:, :], xT[:, 0, :], ACT.Square).then_inc(sq_ready, 1)
                else:
                    if d >= 3:
                        act.wait_ge(ssum_added, 6 * st + d - 2)
                    act.activation(sq[:, d % 2, :], xT[:, d, :], ACT.Square).then_inc(sq_ready, 1)

            def round_h(v, layer, which):
                sh = MOD_COLS * layer + 3 * KT * which
                for k in range(KT):
                    act.wait_ge(normed, KT * v + k + 1)
                    act.activation(h_hi[:, k, :], dve_tmp[:, k % 2, :], ACT.Identity, bias=modc[:, sh + k:sh + k + 1],
                                   scale=1.0).then_inc(h_rounded, 1)

            def ffn(f, st):
                for t, (f0, k) in enumerate(THIRDS):
                    up, down = third_units(f, t)

                    def up_body(up, i, h0):
                        for q in range(2):
                            s = up + 2 * q
                            act.wait_ge(unit_done, s + 2 + 4 * i)
                            if s >= 4:
                                act.wait_ge(evicted, s - 2 + 4 * i)
                            act.activation(act_tmp[:, q, :], bank[s % 4][:, :], ACT.Silu).then_inc(act_out, 1)
                            hi(s + 4, i)
                            hi(s + 5, i)
                            act.wait_ge(evicted, s + 2 + 4 * i)
                            act.activation(hid_hi[:, bass.ds(i * 2 + h0 + q, 1), :], dve_tmp[:, q:q + 1, :], ACT.Copy)\
                                .then_inc(hid_rounded, 1)
                    if up == 0:
                        up_body(0, 0, 0)
                        with act.Fori(0, k // 2 - 1) as i:
                            up_body(4, i, 2)
                    else:
                        with act.Fori(0, k // 2) as i:
                            up_body(up, i, 0)
                    if t < 2:
                        with act.Fori(0, 2) as i:
                            for q in range(4):
                                hi(down + q + 4, i)
                    else:
                        down_stats(down, st)

            def down_stats(down, st):
                for d in range(KT):
                    act.wait_ge(evicted, down + d + 1)
                    square(st, d)
                    hi(down + d + 4)

            def exps(J, S):
                act.wait_ge(negmax_ready, J + 1)
                for b in range(NB):
                    sb_ = S[J % 2][:, BOFF[b]:BOFF[b] + (b + 1) * P]
                    act.activation(sb_, sb_, ACT.Exp, bias=negmax[:, J % 2, b:b + 1], scale=1.0,
                                   accum_out=rowsum[:, J % 2, b:b + 1]).then_inc(exp_done, 1)

            def copy_pt(J, PT):
                for t in range(NB):
                    act.wait_ge(p_turned, NB * J + t + 1)
                    if J and t == 0:
                        act.wait_ge(pv_done, J)
                    act.activation(PT[:, TOFF[t]:TOFF[t] + (NB - t) * P],
                                   bank[T_BANK[t % 2]][:, 0:(NB - t) * P], ACT.Copy).then_inc(pt_ready, 1)

            act.dma_start(rows[0:8, :], c[0, :].rearrange("(k p) -> k p", p=P)).then_inc(small_load, 16)
            act.dma_start(rows[8:24, :], post_gain.rearrange("l (k p) -> (l k) p", p=P)).then_inc(small_load, 16)
            for r, g in enumerate((dsa_q_gain, dsa_k_gain, fox_q_gain, fox_k_gain)):
                act.dma_start(rows[24 + r:25 + r, :], g[0:1, :]).then_inc(small_load, 16)
            for l in range(2):
                act.dma_start(modb_rows[0:MOD_COLS, l, :], mod_b[l, :].rearrange("(k p) -> k p", p=P))\
                    .then_inc(small_load, 16)
            act.dma_start(f_bias[:, :], fox_f_bias.rearrange("a h -> h a")).then_inc(small_load, 16)
            for b in range(NB):
                act.dma_start(x_in[:, b, :], x[0, b * P:(b + 1) * P, :]).then_inc(x_load, 16)
            act.wait_ge(cols_ready, 1)
            act.activation(cond[:, :], cols[:, 0:KT], ACT.Silu).then_inc(cond_ready, 1)
            for k in range(KT):
                act.wait_ge(xt_done, k + 1)
                act.activation(xT[:, k, :], bank[k % 4][:, :], ACT.Copy).then_inc(xt_copied, 1)
                if k < RING:
                    hi(k)
            for k in range(KT):
                act.wait_ge(xt_copied, k + 1)
                square(0, k)
            round_h(0, 0, 0)
            ffn(0, 1)
            round_h(1, 0, 1)

            U = DSA_BASE
            for n in range(2, 5):
                act.wait_ge(unit_done, U + n)
                if n == 2:
                    hi(U + 4)
                hi(U + n + 3)
            for g in range(KV_HEADS):
                act.wait_ge(unit_done, U + 6 + g)
                act.activation(sq[:, g, :], bank[(U + 5 + g) % 2][:, :], ACT.Square).then_inc(qk_sq, 1)
                hi(U + 8 + g)
            for m in range(3 * IDX_HEADS):
                b = m // IDX_HEADS + 1
                act.wait_ge(dots_done, m + 1)
                if m >= 2:
                    act.wait_ge(relu_used, m - 1)
                act.activation(relu[:, m % 2, 0:(b + 1) * P], bank[S_BANK[m % 2]][:, 0:(b + 1) * P], ACT.Relu)\
                    .then_inc(relu_ready, 1)
            hi(U + 10)

            def dsa_v_unit(g, n):
                act.wait_ge(unit_done, n + 1)
                act.wait_ge(evicted, n)
                act.activation(dsa_vT[:, g, :], bank[n % 2][:, :], ACT.Copy).then_inc(evicted, 1)
                hi(n + 4)

            dsa_v_unit(0, U + 7)
            for g in range(KV_HEADS):
                act.wait_ge(qk_normed, g + 1)
                act.activation(qk[:, g, :], dsa_k[:, g, :], ACT.Copy).then_inc(qk_rounded, 1)
            for j in range(HEADS):
                n = U + 8 + j
                act.wait_ge(unit_done, n + 1)
                act.wait_ge(qk_stat, max(j, 1))
                act.activation(sq[:, j % 2, :], bank[n % 2][:, :], ACT.Square).then_inc(qk_sq, 1)
                act.activation(hid_hi[:, j, :], bank[n % 2][:, :], ACT.Copy, scale=cols[:, 24:25]).then_inc(q_rounded, 1)
                hi(n + 4)
            dsa_v_unit(1, U + 16)
            for g in range(KV_HEADS):
                act.wait_ge(v_turned, g + 1)
                act.activation(dsa_v[:, g, :, :], bank[T_BANK[g]][:, :], ACT.Copy).then_inc(v_ready, 1)
            for j in range(HEADS + 1):
                if j:
                    copy_pt(j - 1, dsa_PT)
                if j < HEADS:
                    exps(j, dsa_S)
                if j:
                    act.wait_ge(pv_done, j)
                    act.activation(hid_hi[:, j - 1, :], bank[OB][:, :], ACT.Copy).then_inc(hid_rounded, 1)
            down_stats(U + 17, 2)
            round_h(2, 0, 2)
            ffn(1, 3)
            for d in range(KT):
                act.wait_ge(posted, d + 1)
                square(4, d)
            round_h(3, 1, 0)
            ffn(2, 5)
            round_h(4, 1, 1)

            U = FOX_BASE
            act.wait_ge(unit_done, U + 1)
            hi(U + 4)
            act.wait_ge(fz_ready, 1)
            z_small = dve_tmp[0:HEADS, 1, :]
            act.activation(z_small, z_small, ACT.Exp).then_inc(ls_ready, 1)
            act.wait_ge(ls_ready, 1)
            act.activation(z_small, z_small, ACT.Ln, bias=ones[0:HEADS, 0:1], scale=1.0).then_inc(ls_ready, 1)

            def fox_units(j):
                n = U + 1 + 4 * j
                for q in range(2):
                    act.wait_ge(unit_done, n + q + 1)
                    if q == 0 and j:
                        act.wait_ge(qk_stat, 9 + j)
                    act.activation(act_tmp[:, q, :], bank[(n + q) % 2][:, :], ACT.Square).then_inc(qk_sq, 1)
                    hi(n + q + 4)
                act.wait_ge(nb_done, j + 1)
                act.activation(fox_nb[:, j % 2, :], bank[OB][:, :], ACT.Copy).then_inc(nb_ready, 1)
                act.wait_ge(unit_done, n + 3)
                act.wait_ge(evicted, n + 2)
                act.activation(fox_vT, bank[n % 2][:, :], ACT.Copy).then_inc(evicted, 1)
                hi(n + 6)
                for q in range(2):
                    act.wait_ge(qk_normed, 3 + 2 * j + q)
                    act.activation(qk[:, q, :], fox_qk[:, q, :], ACT.Copy).then_inc(qk_rounded, 1)
                act.wait_ge(unit_done, n + 4)
                act.activation(fox_sig[:, j % 2, :], bank[(n + 1) % 2][:, :], ACT.Sigmoid).then_inc(evicted, 1)
                hi(n + 7)
                act.wait_ge(v_turned, 3 + j)
                act.activation(fox_v[:, j % 2, :, :], bank[VB][:, :], ACT.Copy).then_inc(v_ready, 1)

            fox_units(0)
            for j in range(HEADS + 1):
                J = HEADS + j
                if j:
                    copy_pt(J - 1, fox_PT)
                if j < HEADS:
                    exps(J, fox_S)
                if j:
                    act.wait_ge(gated, j)
                    act.activation(hid_hi[:, j - 1, :], dve_tmp[:, 1, :], ACT.Copy).then_inc(hid_rounded, 1)
                if j + 1 < HEADS:
                    fox_units(j + 1)
            down_stats(U + 33, 5 + 1)
            round_h(5, 1, 2)
            ffn(3, 7)
            for d in range(0, KT, 2):
                act.wait_ge(y_turned, d + 1)
                act.activation(y_out[:, :, d * P:(d + 1) * P],
                               bank[d % 4][:, :].rearrange("p (b n) -> p b n", b=NB), ACT.Copy).then_inc(y_copied_a, 1)

        @block.vector
        def _(dve):
            links = [0]

            def link(ins):
                links[0] += 1
                ins.then_inc(linked, 1)
                dve.wait_ge(linked, links[0])

            def lo(s, i=0):
                if s >= UNITS:
                    return
                dve.wait_ge(hi_ready, s + 1 + RING * i)
                dve.tensor_tensor(wlo[:, s % RING, :, :], wraw[:, s % RING, :, :], whi[:, s % RING, :, :].bitcast(F32),
                                  ALU.subtract).then_inc(lo_ready, 1)

            def mod_ops(c0, i, k0, k1):
                for k in range(k0, k1):
                    if c0 < 4:
                        f = 4 * c0 + k // 2
                        if k % 2 == 0:
                            dve.wait_ge(mod_first[f % 7], 16 * (f // 7 + 1))
                        src = mod_slots[f % 7][:, k % 2, :]
                    else:
                        if k % 2 == 0:
                            dve.wait_ge(mod_in[(k // 2) % 2], 16 * (2 * (c0 - 4) + k // 4 + 1) + 32 * i)
                        src = mod_raw[:, (k // 2) % 2, k % 2, :]
                    if k == 0:
                        if c0:
                            dve.wait_ge(mod_summed, c0 + i)
                        ins = dve.tensor_scalar(mod_acc[:, :], src, cond[:, 0:1], None, ALU.mult)
                    else:
                        dve.wait_ge(mod_step, 8 * c0 + k + 8 * i)
                        ins = dve.scalar_tensor_tensor(out=mod_acc[:, :], in0=src, scalar=cond[:, k:k + 1],
                                                       in1=mod_acc[:, :], op0=ALU.mult, op1=ALU.add)
                    ins.then_inc(mod_step, 1)

            def mod_keep(c0, i):
                dve.wait_ge(mod_summed, c0 + 1 + i)
                dve.tensor_tensor(modc[:, bass.ds(4 * c0 + i * 4, 4)], bank[MODB][:, 0:4],
                                  modb[:, bass.ds(4 * c0 + i * 4, 4)], ALU.add).then_inc(mod_kept, 1)

            def add_sq(st, d):
                if 1 <= d <= 6:
                    dve.wait_ge(sq_ready, KT * st + d + 1)
                    if d >= 2:
                        dve.wait_ge(ssum_added, 6 * st + d - 1)
                    dve.tensor_tensor(ssum[:, :], ssum[:, :], sq[:, d % 2, :], ALU.add).then_inc(ssum_added, 1)

            def spread_rstd(st):
                j = NORM_JOB[st]
                dve.wait_ge(stat_done, st + 1)
                dve.tensor_scalar(var[:, j % 2, 0:NB], bank[OB][:, 0:NB], 1.0 / D, EPS, ALU.mult, ALU.add)\
                    .then_inc(var_ready, 1)
                dve.wait_ge(rstd_ready, j + 1)
                make_diag(diag, j, 0).then_inc(diag_ready, 1)
                dve.wait_ge(rb_ready, st + 1)

            def make_diag(dst, j, at):
                return dve.tensor_tensor(dst[:, :, :], ident[:, :].unsqueeze(1).broadcast_to([P, NB, P]),
                                         rstd[:, j % 2, at:at + NB].unsqueeze(2).broadcast_to([P, NB, P]), ALU.mult)

            def norm(v, st, layer, which):
                base = MOD_COLS * layer + 3 * KT * which
                dve.wait_ge(mod_kept, (base + 2 * KT) // 4)
                link(dve.tensor_scalar(scale1[:, :], modc[:, base + KT:base + 2 * KT], 1.0, None, ALU.add))
                if st:
                    spread_rstd(st)

                def lower(k):
                    dve.wait_ge(h_rounded, KT * v + k + 1)
                    dve.scalar_tensor_tensor(out=h_lo[:, k, :], in0=dve_tmp[:, k % 2, :],
                                             scalar=modc[:, base + k:base + k + 1],
                                             in1=h_hi[:, k, :].bitcast(F32), op0=ALU.add, op1=ALU.subtract)\
                        .then_inc(h_ready, 1)
                for k in range(KT):
                    if k >= 2:
                        dve.wait_ge(h_ready, KT * v + k - 1)
                    dve.scalar_tensor_tensor(out=dve_tmp[:, k % 2, :], in0=xT[:, k, :], scalar=scale1[:, k:k + 1],
                                             in1=bank[RB][:, :], op0=ALU.mult, op1=ALU.mult).then_inc(normed, 1)
                    if k:
                        lower(k - 1)
                lower(KT - 1)

            def make_gate(layer, which):
                base = MOD_COLS * layer + 3 * KT * which + 2 * KT
                dve.wait_ge(mod_kept, (base + KT) // 4)
                link(dve.tensor_scalar(gate[:, :], modc[:, base:base + KT], 0.5, None, ALU.mult))

            def add_x(s, d, i, g):
                dve.wait_ge(unit_done, s + 1 + 4 * i)
                dve.scalar_tensor_tensor(out=xT[:, bass.ds(i * 4 + d, 1), :], in0=bank[s % 4][:, :].unsqueeze(1),
                                         scalar=g[:, bass.ds(i * 4 + d, 1)], in1=xT[:, bass.ds(i * 4 + d, 1), :],
                                         op0=ALU.mult, op1=ALU.add).then_inc(evicted, 1)

            def down_stats(down, st, g):
                for d in range(KT):
                    add_sq(st, d - 1)
                    add_x(down + d, d, 0, g)
                    lo(down + d + 4)

            def ffn(f, st):
                plan = mod_plan(f)
                for t, (f0, k) in enumerate(THIRDS):
                    up, down = third_units(f, t)
                    tile0 = HID_BASE[("ffn", f)] + f0
                    pair0 = PAIR_BASE[f] + f0
                    mod_up, mod_down = plan.get(("up", t)), plan.get(("down", t))

                    def up_body(i):
                        for q in range(2):
                            s = up + 2 * q
                            if mod_up is not None:
                                mod_ops(mod_up, i, 4 * q, 4 * q + 4)
                            dve.wait_ge(act_out, pair0 + q + 1 + 2 * i)
                            dve.tensor_tensor(dve_tmp[:, q, :], act_tmp[:, q, :], bank[(s + 1) % 4][:, :], ALU.mult)\
                                .then_inc(evicted, 2)
                            lo(s + 4, i)
                            dve.wait_ge(hid_rounded, tile0 + q + 1 + 2 * i)
                            dve.tensor_tensor(hid_lo[:, bass.ds(i * 2 + q, 1), :], dve_tmp[:, q:q + 1, :],
                                              hid_hi[:, bass.ds(i * 2 + q, 1), :].bitcast(F32), ALU.subtract)\
                                .then_inc(hid_ready, 1)
                            lo(s + 5, i)
                        if mod_up is not None:
                            mod_keep(mod_up, i)
                    with dve.Fori(0, k // 2) as i:
                        up_body(i)
                    if t == 0:
                        make_gate(f // 2, 2 * (f % 2))
                    if t < 2:
                        with dve.Fori(0, 2) as i:
                            for q in range(4):
                                if mod_down is not None:
                                    mod_ops(mod_down, i, 2 * q, 2 * q + 2)
                                add_x(down + q, q, i, gate)
                                lo(down + q + 4, i)
                            if mod_down is not None:
                                mod_keep(mod_down, i)
                    else:
                        down_stats(down, st, gate)

            def post(st, layer):
                spread_rstd(st)
                for d in range(KT):
                    at = 8 + KT * layer + d
                    dve.scalar_tensor_tensor(out=xT[:, d, :], in0=xT[:, d, :], scalar=cols[:, at:at + 1],
                                             in1=bank[RB][:, :], op0=ALU.mult, op1=ALU.mult).then_inc(posted, 1)

            def mask_rows(J, S, b, bias, scale):
                dve.wait_ge(s_done, NB * J + b + 1)
                if J >= 2 and b == 0:
                    dve.wait_ge(p_turned, NB * (J - 1))
                w = (b + 1) * P
                dve.tensor_tensor_reduce(out=S[J % 2][:, BOFF[b]:BOFF[b] + w], in0=bank[S_BANK[b % 2]][:, 0:w],
                                         in1=bias, scale=scale, scalar=-3e38, op0=ALU.add, op1=ALU.max,
                                         accum_out=rowmax[:, J % 2, b:b + 1]).then_inc(masked, 1)

            def negate_max(J):
                dve.wait_ge(masked, NB * (J + 1))
                dve.tensor_scalar(negmax[:, J % 2, :], rowmax[:, J % 2, :], -1.0, None, ALU.mult)\
                    .then_inc(negmax_ready, 1)

            def normalise(J, S):
                dve.wait_ge(exp_done, NB * (J + 1))
                link(dve.reciprocal(rowinv[:, J % 2, :], rowsum[:, J % 2, :]))
                for b in range(NB):
                    sb_ = S[J % 2][:, BOFF[b]:BOFF[b] + (b + 1) * P]
                    dve.tensor_scalar(sb_, sb_, rowinv[:, J % 2, b:b + 1], None, ALU.mult).then_inc(p_ready, 1)

            dve.wait_ge(const_ready, 6)
            dve.tensor_copy(ident_b[:, :], ident[:, :]).then_inc(bf_ready, 1)
            dve.wait_ge(rows_turned, 1)
            dve.tensor_copy(modb[:, :], bank[4][:, 32:32 + 2 * MOD_COLS])
            dve.tensor_copy(cols[:, :], bank[4][:, 0:28]).then_inc(cols_ready, 1)
            dve.wait_ge(cols_ready, 1)
            dve.tensor_scalar(kgain[:, 0:1], cols[:, 25:26], float(HD) ** 0.5, None, ALU.mult)
            link(dve.tensor_scalar(kgain[:, 1:2], cols[:, 27:28], float(HD) ** 0.5, None, ALU.mult))
            dve.wait_ge(cond_ready, 1)
            for ch in range(4):
                mod_ops(ch, 0, 0, 8)
                mod_keep(ch, 0)
                lo(ch)
                if ch == 1:
                    for d in range(KT):
                        add_sq(0, d)
                    spread_rstd(0)
            norm(0, 0, 0, 0)
            ffn(0, 1)
            norm(1, 1, 0, 1)

            U = DSA_BASE
            for n in range(4):
                dve.wait_ge(unit_done, U + max(n + 1, 2))
                dve.tensor_copy(iq[:, n, :], bank[(U + n) % 2][:, :]).then_inc(evicted, 1)
                lo(U + 4 + n)
            dve.wait_ge(unit_done, U + 5)
            dve.tensor_copy(ikx[0:72, :], bank[(U + 4) % 2][0:72, :]).then_inc(evicted, 1)
            for g in range(KV_HEADS):
                dve.wait_ge(qk_sq, g + 1)
                dve.tensor_scalar(dsa_k[:, g, :], bank[(U + 5 + g) % 2][:, :], kgain[:, 0:1], None, ALU.mult)\
                    .then_inc(evicted, 1)
                lo(U + 8 + g)
            dve.wait_ge(iw_turned, 1)
            link(dve.tensor_scalar(iw[:, :], bank[T_BANK[0]][:, 0:NB * 8], float(IDX_HEADS * IDX_DIM) ** -0.5, None,
                                   ALU.mult))
            for m in range(3 * IDX_HEADS):
                b, head = m // IDX_HEADS + 1, m % IDX_HEADS
                dve.wait_ge(relu_ready, m + 1)
                w, at = (b + 1) * P, 8 * b + head
                sc = mask[:, BOFF[b]:BOFF[b] + w]
                if head == 0:
                    ins = dve.tensor_scalar(sc, relu[:, m % 2, 0:w], iw[:, at:at + 1], None, ALU.mult)
                else:
                    dve.wait_ge(relu_used, m)
                    ins = dve.scalar_tensor_tensor(out=sc, in0=relu[:, m % 2, 0:w], scalar=iw[:, at:at + 1], in1=sc,
                                                   op0=ALU.mult, op1=ALU.add)
                ins.then_inc(relu_used, 1)
            lo(U + 10)
            link(dve.memset(mask[:, 0:P], 0.0))
            link(dve.memset(mask[0:CHUNK, P - CHUNK:P], MASKED))
            dve.wait_ge(qk_stat, 1)
            dve.tensor_scalar(var[:, 0, 0:8], bank[STAT][:, 0:8], 1.0, HD * EPS, ALU.mult, ALU.add)\
                .then_inc(var_ready, 1)

            def top_k(b, r0, r1):
                w = (b + 1) * P
                sc = mask[:, BOFF[b]:BOFF[b] + w]
                if r0 == 0:
                    link(dve.memset(mask[0:CHUNK, BOFF[b] + w - CHUNK:BOFF[b] + w], OUTSIDE))
                for r in range(r0, r1):
                    link(dve.max(top8[:, :], sc))
                    link(dve.match_replace(out=sc, in_to_replace=top8[:, :], in_values=sc, imm_value=TAKEN))
                if r1 == TOPK // 8:
                    link(dve.tensor_scalar(sc, sc, (TAKEN + OUTSIDE) / 2, MASKED, ALU.is_gt, ALU.mult))

            top_k(1, 0, 4)
            dve.wait_ge(rstd_ready, 3)
            for g in range(KV_HEADS):
                make_diag((diag, diag_tmp)[g], 2, NB * g).then_inc(k_diag, 1)
            for g in range(KV_HEADS):
                dve.wait_ge(k_rb, g + 1)
                dve.tensor_tensor(dsa_k[:, g, :], dsa_k[:, g, :], bank[K_BANK[g]][:, :], ALU.mult)\
                    .then_inc(qk_normed, 1)
            for g in range(KV_HEADS):
                dve.wait_ge(qk_rounded, g + 1)
                dve.tensor_tensor(qk[:, 2 + g, :], dsa_k[:, g, :], qk[:, g, :].bitcast(F32), ALU.subtract)\
                    .then_inc(k_ready, 1)
            lo(U + 11)
            pieces = [(1, 4, 10), (1, 10, 16), (2, 0, 5), (2, 5, 10), (2, 10, 16), (3, 0, 4), (3, 4, 8), (3, 8, 12),
                      (3, 12, 16)]
            for j in range(HEADS):
                top_k(*pieces[j])
                n = U + 8 + j
                dve.wait_ge(q_rounded, j + 1)
                dve.scalar_tensor_tensor(out=hid_lo[:, j, :], in0=bank[n % 2][:, :], scalar=cols[:, 24:25],
                                         in1=hid_hi[:, j, :].bitcast(F32), op0=ALU.mult, op1=ALU.subtract)\
                    .then_inc(evicted, 1)
                lo(n + 4)
            top_k(*pieces[HEADS])
            dve.wait_ge(qk_stat, 1 + HEADS)
            dve.tensor_scalar(var[:, 1, :], bank[STAT][:, 0:NB * HEADS], 1.0, HD * EPS, ALU.mult, ALU.add)\
                .then_inc(var_ready, 1)
            lo(U + 20)
            dve.wait_ge(rstd_ready, 4)
            for j in range(HEADS + 1):
                if j < HEADS:
                    for b in range(NB):
                        mask_rows(j, dsa_S, b, mask[:, BOFF[b]:BOFF[b] + (b + 1) * P], rstd[:, 1, NB * j + b:NB * j + b + 1])
                    negate_max(j)
                if j:
                    dve.wait_ge(hid_rounded, HID_BASE["dsa"] + j)
                    dve.tensor_tensor(hid_lo[:, j - 1, :], bank[OB][:, :], hid_hi[:, j - 1, :].bitcast(F32),
                                      ALU.subtract).then_inc(hid_ready, 1)
                if j < HEADS:
                    normalise(j, dsa_S)
            down_stats(U + 17, 2, modc[:, 5 * KT:6 * KT])
            norm(2, 2, 0, 2)
            ffn(1, 3)
            post(3, 0)
            for d in range(KT):
                add_sq(4, d)
            norm(3, 4, 1, 0)
            ffn(2, 5)
            norm(4, 5, 1, 1)

            U = FOX_BASE
            z, z_small = dve_tmp[0:HEADS, 0, :], dve_tmp[0:HEADS, 1, :]
            dve.wait_ge(unit_done, U + 1)
            dve.memset(sq[0:HEADS, 0, :], 1.0)
            dve.tensor_scalar(z, bank[U % 2][0:HEADS, :], f_bias[:, 0:1], None, ALU.add).then_inc(evicted, 1)
            dve.wait_ge(evicted, U + 1)
            dve.scalar_tensor_tensor(out=z_small, in0=z, scalar=-1.0, in1=z, op0=ALU.mult, op1=ALU.min)\
                .then_inc(fz_ready, 1)
            lo(U + 4)
            dve.wait_ge(ls_ready, 2)
            link(dve.scalar_tensor_tensor(out=z, in0=z, scalar=0.0, in1=z_small, op0=ALU.min, op1=ALU.subtract))
            dve.tensor_tensor_scan(cum[0:HEADS, :], sq[0:HEADS, 0, :], z, 0.0, ALU.mult, ALU.add)\
                .then_inc(cum_ready, 1)
            dve.wait_ge(cum_ready, 1)

            def fox_units(j):
                n = U + 1 + 4 * j
                for q, g in enumerate((cols[:, 26:27], kgain[:, 1:2])):
                    dve.wait_ge(qk_sq, 11 + 2 * j + q)
                    if j:
                        dve.wait_ge(k_ready, 2 + 2 * j)
                    dve.tensor_scalar(fox_qk[:, q, :], bank[(n + q) % 2][:, :], g, None, ALU.mult).then_inc(evicted, 1)
                    lo(n + q + 4)
                dve.wait_ge(qk_stat, 10 + j)
                dve.tensor_scalar(var[:, j % 2, 0:8], bank[STAT][:, 0:8], 1.0, HD * EPS, ALU.mult, ALU.add)\
                    .then_inc(var_ready, 1)
                dve.wait_ge(rstd_ready, 9 + j)
                make_diag(diag, 8 + j, 0).then_inc(k_diag, 1)
                make_diag(diag_k, 8 + j, NB).then_inc(k_diag, 1)
                for q in range(2):
                    dve.wait_ge(k_rb, 3 + 2 * j + q)
                    dve.tensor_tensor(fox_qk[:, q, :], fox_qk[:, q, :], bank[KV_BANK[q]][:, :], ALU.mult)\
                        .then_inc(qk_normed, 1)
                for q in range(2):
                    dve.wait_ge(qk_rounded, 3 + 2 * j + q)
                    dve.tensor_tensor(qk[:, 2 + q, :], fox_qk[:, q, :], qk[:, q, :].bitcast(F32), ALU.subtract)\
                        .then_inc(k_ready, 1)
                lo(n + 6)
                lo(n + 7)

            fox_units(0)
            for j in range(HEADS + 1):
                J = HEADS + j
                if j < HEADS:
                    dve.wait_ge(nb_ready, j + 1)
                    for b in range(NB):
                        mask_rows(J, fox_S, b, fox_nb[:, j % 2, 0:(b + 1) * P], 1.0)
                    negate_max(J)
                if j:
                    dve.wait_ge(pv_done, J)
                    dve.wait_ge(hid_ready, HID_BASE["fox"] + j - 1)
                    dve.tensor_tensor(dve_tmp[:, 1, :], bank[OB][:, :], fox_sig[:, (j - 1) % 2, :], ALU.mult)\
                        .then_inc(gated, 1)
                    dve.wait_ge(hid_rounded, HID_BASE["fox"] + j)
                    dve.tensor_tensor(hid_lo[:, j - 1, :], dve_tmp[:, 1, :], hid_hi[:, j - 1, :].bitcast(F32),
                                      ALU.subtract).then_inc(hid_ready, 1)
                if j < HEADS:
                    normalise(J, fox_S)
                if j + 1 < HEADS:
                    fox_units(j + 1)
            down_stats(U + 33, 6, modc[:, MOD_COLS + 5 * KT:MOD_COLS + 6 * KT])
            norm(5, 6, 1, 2)
            ffn(3, 7)
            post(7, 1)
            for d in range(1, KT, 2):
                dve.wait_ge(y_turned, d + 1)
                dve.tensor_copy(y_out[:, :, d * P:(d + 1) * P],
                                bank[d % 4][:, :].rearrange("p (b n) -> p b n", b=NB)).then_inc(y_copied_d, 1)

        @block.tensor
        def _(pe):
            def three(dst, s, k, hi_, lo_, first, last):
                w = s % RING
                pe.matmul(dst, whi[:, w, k, :], hi_, start=first, stop=False)
                pe.matmul(dst, whi[:, w, k, :], lo_, start=False, stop=False)
                return pe.matmul(dst, wlo[:, w, k, :], hi_, start=False, stop=last)

            def unit(s, i, dst, K, A_hi, A_lo, free, ready=None):
                pe.wait_ge(lo_ready, s + 1 + RING * i)
                if free > 0 or not isinstance(i, int):
                    pe.wait_ge(evicted, free + RING * i)
                for k in range(K):
                    if ready is not None:
                        pe.wait_ge(hid_ready, ready + k + 1)
                    ins = three(dst, s, k, A_hi[:, k, :], A_lo[:, k, :], k == 0, k == K - 1)
                ins.then_inc(unit_done, 1)

            def pair(s, i, banks, free, v=None):
                pe.wait_ge(lo_ready, s + 2 + RING * i)
                if s > 2 or not isinstance(i, int):
                    pe.wait_ge(evicted, free + RING * i)
                for k in range(KT):
                    if v is not None:
                        pe.wait_ge(h_ready, KT * v + k + 1)
                    for q in range(2):
                        ins = three(bank[banks[q]][:, :], s + q, k, h_hi[:, k, :], h_lo[:, k, :], k == 0, k == KT - 1)
                ins.then_inc(unit_done, 2)

            def mod_sum(c0, i):
                pe.wait_ge(mod_step, 8 * (c0 + 1) + 8 * i)
                if c0:
                    pe.wait_ge(mod_kept, c0 + i)
                for q in range(4):
                    ins = pe.matmul(bank[MODB][:, q:q + 1], mod_acc[:, q * P:(q + 1) * P], ones[:, 0:1], start=True,
                                    stop=True)
                ins.then_inc(mod_summed, 1)

            def stat(st):
                pe.wait_ge(ssum_added, 6 * (st + 1))
                pe.wait_ge(sq_ready, KT * (st + 1))
                for b in range(NB):
                    pe.matmul(bank[OB][:, b:b + 1], ssum[:, b * P:(b + 1) * P], ones[:, 0:1], start=True, stop=False)
                    ins = pe.matmul(bank[OB][:, b:b + 1], sq[:, 1, b * P:(b + 1) * P], ones[:, 0:1], start=False,
                                    stop=True)
                ins.then_inc(stat_done, 1)
                pe.wait_ge(diag_ready, st + 1)
                pe.matmul(bank[RB][:, :], ones[:, :], diag[:, :, :], start=True, stop=True).then_inc(rb_ready, 1)

            def ffn(f, v):
                plan = mod_plan(f)
                for t, (f0, k) in enumerate(THIRDS):
                    up, down = third_units(f, t)
                    mod_up, mod_down = plan.get(("up", t)), plan.get(("down", t))

                    def up_body(i, first):
                        for q in range(2):
                            s = up + 2 * q
                            pair(s, i, (s % 4, (s + 1) % 4), s - 2, v if first and q == 0 else None)
                        if mod_up is not None:
                            mod_sum(mod_up, i)
                    if t == 0:
                        up_body(0, True)
                        up += 4
                        if mod_up is not None:
                            mod_up += 1
                        with pe.Fori(0, k // 2 - 1) as i:
                            up_body(i, False)
                    else:
                        with pe.Fori(0, k // 2) as i:
                            up_body(i, False)
                    tile0 = HID_BASE[("ffn", f)] + f0

                    def down_body(i, q0, n):
                        for q in range(q0, n):
                            s = down + q
                            unit(s, i, bank[s % 4][:, :], k, hid_hi, hid_lo, s - 3, tile0 if q == 0 else None)
                    if t < 2:
                        with pe.Fori(0, 2) as i:
                            down_body(i, 0, 4)
                            if mod_down is not None:
                                mod_sum(mod_down, i)
                    else:
                        down_body(0, 0, KT)

            def turn_p(J, S, t):
                if t == 0:
                    pe.wait_ge(p_ready, NB * (J + 1))
                if J or t >= 2:
                    pe.wait_ge(pt_ready, NB * J + t - 1)
                for b in range(t, NB):
                    ins = pe.transpose(bank[T_BANK[t % 2]][:, (b - t) * P:(b - t + 1) * P],
                                       S[J % 2][:, BOFF[b] + t * P:BOFF[b] + (t + 1) * P], ident[:, :])
                ins.then_inc(p_turned, 1)

            def pv(J, PT, V):
                pe.wait_ge(pt_ready, NB * (J + 1))
                for t in range(NB):
                    ins = pe.matmul(bank[OB][:, t * P:SEQ], V[:, t, :], PT[:, TOFF[t]:TOFF[t] + (NB - t) * P],
                                    start=(t == 0), stop=(t == NB - 1))
                ins.then_inc(pv_done, 1)

            pe.wait_ge(small_load, 16 * 9)
            pe.wait_ge(const_ready, 6)
            pe.transpose(bank[4][:, 0:28], rows[0:28, :], ident[0:28, 0:28])
            for l in range(2):
                ins = pe.transpose(bank[4][:, 32 + MOD_COLS * l:32 + MOD_COLS * (l + 1)], modb_rows[0:MOD_COLS, l, :],
                                   ident[0:MOD_COLS, 0:MOD_COLS])
            ins.then_inc(rows_turned, 1)
            pe.wait_ge(x_load, 16 * NB)
            for k in range(KT):
                if k >= 4:
                    pe.wait_ge(xt_copied, k - 3)
                for b in range(NB):
                    ins = pe.transpose(bank[k % 4][:, b * P:(b + 1) * P], x_in[:, b, k * P:(k + 1) * P], ident[:, :])
                ins.then_inc(xt_done, 1)
            for ch in range(4):
                mod_sum(ch, 0)
                if ch == 1:
                    stat(0)
            ffn(0, 0)
            stat(1)

            U = DSA_BASE
            pair(U, 0, (U % 2, (U + 1) % 2), U, 1)
            for n in range(2, 7):
                unit(U + n, 0, bank[(U + n) % 2][:, :], KT, h_hi, h_lo, U + n - 1)
            pe.wait_ge(ik_spread, 32)
            for b in range(NB):
                ins = pe.transpose(bank[T_BANK[0]][:, 8 * b:8 * b + 8], act_tmp[0:8, 0, b * P:(b + 1) * P],
                                   ident[0:8, 0:8])
            ins.then_inc(iw_turned, 1)
            for m in range(3 * IDX_HEADS):
                b, head = m // IDX_HEADS + 1, m % IDX_HEADS
                if m >= 2:
                    pe.wait_ge(relu_ready, m - 1)
                r = 64 * (head % 2)
                ik = ikx if head % 2 == 0 else ikd
                pe.matmul(bank[S_BANK[m % 2]][:, 0:(b + 1) * P], iq[r:r + 64, head // 2, b * P:(b + 1) * P],
                          ik[r:r + 64, 0:(b + 1) * P], start=True, stop=True).then_inc(dots_done, 1)
            pe.wait_ge(qk_sq, 2)
            for g in range(KV_HEADS):
                for b in range(NB):
                    ins = pe.matmul(bank[STAT][:, NB * g + b:NB * g + b + 1], sq[:, g, b * P:(b + 1) * P],
                                    ones[:, 0:1], start=True, stop=True)
            ins.then_inc(qk_stat, 1)
            unit(U + 7, 0, bank[(U + 7) % 2][:, :], KT, h_hi, h_lo, U + 6)

            def dsa_q_stat(j):
                pe.wait_ge(qk_sq, 3 + j)
                if j == 0:
                    pe.wait_ge(var_ready, 3)
                for b in range(NB):
                    ins = pe.matmul(bank[STAT][:, NB * j + b:NB * j + b + 1], sq[:, j % 2, b * P:(b + 1) * P],
                                    ones[:, 0:1], start=True, stop=True)
                ins.then_inc(qk_stat, 1)

            for j in range(HEADS):
                n = U + 8 + j
                unit(n, 0, bank[n % 2][:, :], KT, h_hi, h_lo, n - 1)
                if j:
                    dsa_q_stat(j - 1)
                if j == 0:
                    for g in range(KV_HEADS):
                        pe.wait_ge(k_diag, g + 1)
                        pe.matmul(bank[K_BANK[g]][:, :], ones[:, :], (diag, diag_tmp)[g][:, :, :], start=True,
                                  stop=True).then_inc(k_rb, 1)
            unit(U + 16, 0, bank[(U + 16) % 2][:, :], KT, h_hi, h_lo, U + 15)
            dsa_q_stat(HEADS - 1)
            pe.wait_ge(evicted, U + 17)
            for g in range(KV_HEADS):
                for b in range(NB):
                    ins = pe.transpose(bank[T_BANK[g]][:, b * P:(b + 1) * P], dsa_vT[:, g, b * P:(b + 1) * P],
                                       ident[:, :])
                ins.then_inc(v_turned, 1)

            def score(dst, q_hi, q_lo, k_hi, k_lo, last):
                pe.matmul(dst, q_hi, k_hi, start=True, stop=False)
                pe.matmul(dst, q_hi, k_lo, start=False, stop=False)
                return pe.matmul(dst, q_lo, k_hi, start=False, stop=last)

            def dsa_score(j, b):
                if j or b >= 2:
                    pe.wait_ge(masked, NB * j + b - 1)
                w, g = (b + 1) * P, j // GROUP
                score(bank[S_BANK[b % 2]][:, 0:w], hid_hi[:, j, b * P:w], hid_lo[:, j, b * P:w], qk[:, g, 0:w],
                      qk[:, 2 + g, 0:w], True).then_inc(s_done, 1)

            def heads(j, score_of, turn_of, pv_of):
                order = [(0, 0), (0, 1), (1, 0), (0, 2), (1, 1), (0, 3), (1, 2), (2, 0), (1, 3)]
                for kind, b in order:
                    if kind == 0 and j:
                        turn_of(b)
                    if kind == 1 and j < HEADS:
                        score_of(b)
                    if kind == 2 and j:
                        pv_of()

            pe.wait_ge(v_ready, 2)
            for j in range(HEADS + 1):
                def pv_of():
                    if j >= 2:
                        pe.wait_ge(hid_ready, HID_BASE["dsa"] + j - 1)
                    pv(j - 1, dsa_PT, dsa_v[:, (j - 1) // GROUP, :, :])
                heads(j, lambda b: dsa_score(j, b), lambda t: turn_p(j - 1, dsa_S, t), pv_of)
            for d in range(KT):
                s = U + 17 + d
                unit(s, 0, bank[s % 4][:, :], KT, hid_hi, hid_lo, s - 1, HID_BASE["dsa"] if d == 0 else None)
            stat(2)
            ffn(1, 2)
            stat(3)
            stat(4)
            ffn(2, 3)
            stat(5)

            U = FOX_BASE
            pe.wait_ge(h_ready, KT * 5)
            unit(U, 0, bank[U % 2][:, :], KT, h_hi, h_lo, U)

            def fox_units(j):
                n = U + 1 + 4 * j
                unit(n, 0, bank[n % 2][:, :], KT, h_hi, h_lo, n - 1)
                unit(n + 1, 0, bank[(n + 1) % 2][:, :], KT, h_hi, h_lo, n)
                if j == 0:
                    pe.wait_ge(cum_ready, 1)
                    pe.wait_ge(negsel_ready, 2)
                if j > 1:
                    pe.wait_ge(gated, j - 1)
                pe.matmul(bank[OB][:, :], negsel[0:HEADS, j, :], cum[0:HEADS, :], start=True, stop=True)\
                    .then_inc(nb_done, 1)
                pe.wait_ge(qk_sq, 12 + 2 * j)
                for q in range(2):
                    for b in range(NB):
                        ins = pe.matmul(bank[STAT][:, NB * q + b:NB * q + b + 1], act_tmp[:, q, b * P:(b + 1) * P],
                                        ones[:, 0:1], start=True, stop=True)
                ins.then_inc(qk_stat, 1)
                unit(n + 2, 0, bank[n % 2][:, :], KT, h_hi, h_lo, n + 1)
                for q in range(2):
                    pe.wait_ge(k_diag, 3 + 2 * j + q)
                    pe.matmul(bank[KV_BANK[q]][:, :], ones[:, :], (diag, diag_k)[q][:, :, :], start=True, stop=True)\
                        .then_inc(k_rb, 1)
                unit(n + 3, 0, bank[(n + 1) % 2][:, :], KT, h_hi, h_lo, n + 2)
                pe.wait_ge(evicted, n + 3)
                if j:
                    pe.wait_ge(masked, NB * (HEADS + j))
                for b in range(NB):
                    ins = pe.transpose(bank[VB][:, b * P:(b + 1) * P], fox_vT[:, b * P:(b + 1) * P], ident[:, :])
                ins.then_inc(v_turned, 1)

            def fox_score(j, b):
                if b == 0:
                    pe.wait_ge(k_ready, 4 + 2 * j)
                    pe.wait_ge(v_ready, 3 + j)
                pe.wait_ge(masked, NB * (HEADS + j) + b - 1)
                w = (b + 1) * P
                dst = bank[S_BANK[b % 2]]
                score(dst[:, 0:w], qk[:, 0, b * P:w], qk[:, 2, b * P:w], qk[:, 1, 0:w], qk[:, 3, 0:w], False)
                pe.matmul(dst[:, b * P:w], ident_b[:, :], causal[:, :], start=False, stop=True).then_inc(s_done, 1)

            pe.wait_ge(bf_ready, 1)
            fox_units(0)
            for j in range(HEADS + 1):
                J = HEADS + j

                def pv_of():
                    pe.wait_ge(nb_ready, min(j + 1, HEADS))
                    if j >= 2:
                        pe.wait_ge(gated, j - 1)
                    pv(J - 1, fox_PT, fox_v[:, (j - 1) % 2, :, :])

                def turn_of(t):
                    if t == 1:
                        pe.wait_ge(qk_normed, 3 + 2 * min(j, HEADS - 1))
                    turn_p(J - 1, fox_S, t)
                heads(j, lambda b: fox_score(j, b), turn_of, pv_of)
                if j + 1 < HEADS:
                    if j:
                        pe.wait_ge(gated, j)
                    fox_units(j + 1)
            for d in range(KT):
                s = U + 33 + d
                unit(s, 0, bank[s % 4][:, :], KT, hid_hi, hid_lo, s - 1, HID_BASE["fox"] if d == 0 else None)
            stat(6)
            ffn(3, 5)
            stat(7)
            for d in range(KT):
                pe.wait_ge(posted, KT + d + 1)
                if d >= 4:
                    pe.wait_ge((y_copied_a, y_copied_d)[d % 2], d // 2 - 1)
                for b in range(NB):
                    ins = pe.transpose(bank[d % 4][:, b * P:(b + 1) * P], xT[:, d, b * P:(b + 1) * P], ident[:, :])
                ins.then_inc(y_turned, 1)


HID_BASE = {("ffn", 0): 0, "dsa": 22, ("ffn", 1): 30, ("ffn", 2): 52, "fox": 74, ("ffn", 3): 82}
PAIR_BASE = [0, 22, 44, 66]

_INS = ['x', 'c', 'mod_w', 'mod_b', 'ffn1_w_gu', 'ffn1_w_down', 'ffn2_w_gu', 'ffn2_w_down', 'post_gain',
        'dsa_w_in', 'dsa_q_gain', 'dsa_k_gain', 'dsa_w_out',
        'fox_w_in', 'fox_f_bias', 'fox_q_gain', 'fox_k_gain', 'fox_w_out']


def kernel(**inputs):
    import numpy as _np
    import concourse.bacc as _bacc
    from concourse import mybir as _mybir
    from concourse.bass_utils import run_bass_kernel_spmd as _run

    nc = _bacc.Bacc("TRN2", target_bir_lowering=False, num_devices=1)
    arrays, args = {}, []
    for name in _INS:
        a = _np.ascontiguousarray(inputs[name])
        arrays[f"in_{name}_dram"] = a
        args.append(nc.dram_tensor(f"in_{name}_dram", a.shape, _mybir.dt.from_np(a.dtype), kind="ExternalInput").ap())
    args.append(nc.dram_tensor("out_0_dram", (1, SEQ, D), _mybir.dt.float32, kind="ExternalOutput").ap())
    build(nc, *args)
    r = _run(nc, [arrays], core_ids=[0])
    return r.results[0]["out_0_dram"]
```

```python
from contextlib import ExitStack

import concourse.bass as bass
from concourse import mybir
from concourse.alu_op_type import AluOpType as ALU

F32 = mybir.dt.float32
F32R = mybir.dt.float32r
BF16 = mybir.dt.bfloat16
ACT = mybir.ActivationFunctionType

P = 128
D = 1024
SEQ = 512
KT = D // P
NB = SEQ // P
D_FF = 2816
FF_TILES = D_FF // P
THIRDS = [(0, 8), (8, 8), (16, FF_TILES - 16)]
EPS = 1e-6
HEADS = 8
KV_HEADS = 2
GROUP = HEADS // KV_HEADS
HD = 128
IDX_HEADS = 8
IDX_DIM = 64
CHUNK = 64
EARLY = 6
TOPK = 128
MASKED = -1e30
OUTSIDE = -2e38
TAKEN = -3e38
RING = 4
MODC = 512
MOD_COLS = 9 * D // P
MOD_CHUNKS = 9 * D // MODC
FIRST_CHUNKS = (0, 2, 1, 3)
PE_CHUNKS = 2
PE_TILES = 2
BOFF = [0, 128, 384, 768]
KEYS = 1280
TOFF = [0, 512, 896, 1152]

FFN_UNITS = 2 * FF_TILES + 3 * KT
DSA_UNITS = 5 + 2 * KV_HEADS + HEADS + KT
FOX_UNITS = 1 + 4 * HEADS + KT
FFN_BASE = [0, FFN_UNITS + DSA_UNITS, 2 * FFN_UNITS + DSA_UNITS, 3 * FFN_UNITS + DSA_UNITS + FOX_UNITS]
DSA_BASE = FFN_UNITS
FOX_BASE = 3 * FFN_UNITS + DSA_UNITS
UNITS = 4 * FFN_UNITS + DSA_UNITS + FOX_UNITS

FFN_MOD = [(4, 16), (16, 28), (28, 36), (36, 36)]


def third_units(f, t):
    base = FFN_BASE[f] + sum(2 * THIRDS[u][1] + KT for u in range(t))
    return base, base + 2 * THIRDS[t][1]


def mod_plan(f):
    c, end = FFN_MOD[f]
    plan = {}
    loops = [("up", 0), ("down", 0), ("up", 1), ("down", 1)] if end - c == 12 else [("up", 0), ("up", 1)]
    for name in loops:
        if c < end:
            plan[name] = c
            c += 4 if name[0] == "up" else 2
    return plan


def build(nc, x, c, mod_w, mod_b, ffn1_w_gu, ffn1_w_down, ffn2_w_gu, ffn2_w_down, post_gain,
          dsa_w_in, dsa_q_gain, dsa_k_gain, dsa_w_out,
          fox_w_in, fox_f_bias, fox_q_gain, fox_k_gain, fox_w_out, out):
    ctx = ExitStack()
    with ctx:
        def sb(name, shape, dt=F32):
            return ctx.enter_context(nc.sbuf_tensor(name, shape, dt))

        def sem(name):
            return ctx.enter_context(nc.semaphore(name))

        wraw = sb("wraw", [P, RING, KT, P])
        whi = sb("whi", [P, RING, KT, P], F32R)
        wlo = sb("wlo", [P, RING, KT, P], F32R)
        xT = sb("xT", [P, KT, SEQ])
        h_hi = sb("h_hi", [P, KT, SEQ], F32R)
        h_lo = sb("h_lo", [P, KT, SEQ], F32R)
        hid_hi = sb("hid_hi", [P, KT, SEQ], F32R)
        hid_lo = sb("hid_lo", [P, KT, SEQ], F32R)
        mod_raw = sb("mod_raw", [P, 2, 2, MODC])
        mod_acc = sb("mod_acc", [P, MODC])
        act_tmp = sb("act_tmp", [P, 2, SEQ])
        dve_tmp = sb("dve_tmp", [P, 2, SEQ])
        sq = sb("sq", [P, 2, SEQ])
        ssum = sb("ssum", [P, SEQ])
        ident = sb("ident", [P, P])
        gain_scale = sb("gain_scale", [P, KT])
        gain_sums = sb("gain_sums", [P, NB])
        ident_r = sb("ident_r", [P, P], F32R)
        ident_b = sb("ident_b", [P, P], BF16)
        causal = sb("causal", [P, P], BF16)
        ones = sb("ones", [P, P])
        minus_half = sb("minus_half", [P, NB * HEADS])
        modb = sb("modb", [P, 2 * MOD_COLS])
        modc = sb("modc", [P, 2 * MOD_COLS])
        cols = sb("cols", [P, 28])
        cond = sb("cond", [P, KT])
        scale1 = sb("scale1", [P, KT])
        gate = sb("gate", [P, KT])
        kgain = sb("kgain", [P, 2])
        f_bias = sb("f_bias", [HEADS, 1])
        var = sb("var", [P, 2, NB * HEADS])
        rstd = sb("rstd", [P, 2, NB * HEADS])
        root = sb("root", [P, 2, 2, 2 * NB], F32R)
        rowmax = sb("rowmax", [P, 4, NB])
        negmax = sb("negmax", [P, 4, NB])
        rowsum = sb("rowsum", [P, 4, NB])
        rowinv = sb("rowinv", [P, 4, NB])
        iw = sb("iw", [P, NB * 8])
        top8 = sb("top8", [P, 8])
        qk = sb("qk", [P, 4, SEQ], F32R)
        pt_hi = sb("pt_hi", [P, KEYS], F32R)
        pt_lo = sb("pt_lo", [P, KEYS], F32R)
        v_hi = sb("v_hi", [P, 2, NB, P], F32R)
        v_lo = sb("v_lo", [P, 2, NB, P], F32R)
        ARENA = 6400
        arena = sb("arena", [P, ARENA])

        def piece(at, n):
            return arena[:, at:at + n]

        x_in = piece(0, NB * D).rearrange("p (b n) -> p b n", b=NB)
        rows = piece(4096, 128)
        modb_rows = piece(4224, 256).rearrange("p (l n) -> p l n", l=2)
        y_out = piece(0, NB * D).rearrange("p (b n) -> p b n", b=NB)
        mod_row = [ssum[0:1, :], sq[0:1, 0, :]]
        first_acc = [mod_acc, piece(4480, MODC)]

        def tiles_of(x):
            return x.rearrange("p (a n) -> p a n", a=2)

        wraw_slot = [wraw[:, s, :, :].rearrange("p (a k) n -> p a (k n)", a=2) for s in range(RING)]
        x_slot = [tiles_of(piece(2 * MODC * s, 2 * MODC)) for s in range(NB)]
        raw_slot = [mod_raw[:, s, :, :] for s in range(2)]
        spare_slot = tiles_of(piece(4992, 2 * MODC))
        mod_slots = (raw_slot + [wraw_slot[2], wraw_slot[3]]
                     + [wraw_slot[0], wraw_slot[1], act_tmp[:, :, :], spare_slot]
                     + [dve_tmp[:, :, :]] + x_slot
                     + [raw_slot[1], act_tmp[:, :, :], spare_slot])
        mask = piece(0, KEYS)
        ik_hi, ik_lo = hid_hi[:, 4, :], hid_lo[:, 4, :]
        relu = piece(3328, 2 * SEQ).rearrange("p (t n) -> p t n", t=2)
        ikx = piece(4352, SEQ)
        ikd = piece(4864, SEQ)
        dsa_k = piece(5376, 2 * SEQ).rearrange("p (t n) -> p t n", t=2)
        dsa_vT = piece(1280, 2 * SEQ).rearrange("p (t n) -> p t n", t=2)
        dsa_S = [piece(KEYS * (1 + n), KEYS) for n in range(4)]
        gain_sum, gain_sq = piece(0, SEQ), piece(SEQ, 2 * SEQ).rearrange("p (t n) -> p t n", t=2)
        fox_qk = piece(0, 2 * SEQ).rearrange("p (t n) -> p t n", t=2)
        fox_vT = piece(1024, SEQ)
        fox_sig = piece(1536, 2 * SEQ).rearrange("p (t n) -> p t n", t=2)
        fox_nb = piece(2560, 2 * SEQ).rearrange("p (t n) -> p t n", t=2)
        fox_S = [piece(3584, KEYS), piece(4864, KEYS)]
        cum = piece(4864, SEQ)
        cum_hi, cum_lo = hid_hi[0:HEADS, KT - 1, :], hid_lo[0:HEADS, KT - 1, :]

        bank = [ctx.enter_context(nc.psum_tensor(f"bank{i}", [P, SEQ], F32)) for i in range(8)]
        S_BANK, T_BANK, KV_BANK, STAT, RB, MODB, OB, VB = (4, 5), (6, 2), (2, 3), 3, 6, 5, 7, 4
        K_BANK = (2, 6)

        raw_in = [sem(f"raw_in{s}") for s in range(RING)]
        hi_ready, lo_ready, unit_done, evicted = sem("hi_ready"), sem("lo_ready"), sem("unit_done"), sem("evicted")
        x_load, small_load, const_ready, bf_ready = sem("x_load"), sem("small_load"), sem("const_ready"), sem("bf_ready")
        rows_turned, cols_ready, cond_ready = sem("rows_turned"), sem("cols_ready"), sem("cond_ready")
        xt_done, xt_copied = sem("xt_done"), sem("xt_copied")
        mod_in = [sem(f"mod_in{s}") for s in range(2)]
        mod_first = [sem(f"mod_first{s}") for s in range(16)]
        c_load, c_turned, mod_direct, row_ready, mod_rest = (
            sem("c_load"), sem("c_turned"), sem("mod_direct"), sem("row_ready"), sem("mod_rest"))
        mod_step, mod_summed, mod_kept = sem("mod_step"), sem("mod_summed"), sem("mod_kept")
        sq_ready, ssum_added, stat_done = sem("sq_ready"), sem("ssum_added"), sem("stat_done")
        var_ready, rstd_ready, root_ready, rb_ready = sem("var_ready"), sem("rstd_ready"), sem("root_ready"), sem("rb_ready")
        normed, h_rounded, h_ready = sem("normed"), sem("h_rounded"), sem("h_ready")
        act_out, hid_rounded, hid_ready = sem("act_out"), sem("hid_rounded"), sem("hid_ready")
        posted = sem("posted")
        linked = sem("linked")
        iq_rounded, ik_rounded, ik_split = sem("iq_rounded"), sem("ik_rounded"), sem("ik_split")
        ik_spread, iw_turned, dots_done, relu_ready, relu_used = (
            sem("ik_spread"), sem("iw_turned"), sem("dots_done"), sem("relu_ready"), sem("relu_used"))
        qk_sq, qk_stat, k_rb, k_ready = sem("qk_sq"), sem("qk_stat"), sem("k_rb"), sem("k_ready")
        v_turned, v_rounded, v_ready = sem("v_turned"), sem("v_rounded"), sem("v_ready")
        q_rounded, q_split, qk_normed, qk_rounded = sem("q_rounded"), sem("q_split"), sem("qk_normed"), sem("qk_rounded")
        s_done, masked, negmax_ready, exp_done, p_ready = (
            sem("s_done"), sem("masked"), sem("negmax_ready"), sem("exp_done"), sem("p_ready"))
        p_turned, pt_rounded, pt_ready = sem("p_turned"), sem("pt_rounded"), sem("pt_ready")
        pv_done, gated = sem("pv_done"), sem("gated")
        fz_ready, ls_ready, cum_ready = sem("fz_ready"), sem("ls_ready"), sem("cum_ready")
        nb_done, nb_ready = sem("nb_done"), sem("nb_ready")
        gsq_ready, gsum_added = sem("gsq_ready"), sem("gsum_added")
        y_turned, y_copied_a, y_copied_d, stored = sem("y_turned"), sem("y_copied_a"), sem("y_copied_d"), sem("stored")

        def gu(f):
            return (ffn1_w_gu, ffn2_w_gu)[f % 2][f // 2]

        def dn(f):
            return (ffn1_w_down, ffn2_w_down)[f % 2][f // 2]

        def blocks(w, r0, k, c0, n):
            return w[r0:r0 + k * P, bass.ds(c0, n)].rearrange("(k p) n -> p k n", p=P)

        DSA_SRC = ([(dsa_w_in, 1536 + P * j, P) for j in range(4)] + [(dsa_w_in, 2048, IDX_DIM + IDX_HEADS)]
                   + [(dsa_w_in, 1024 + P * j, P) for j in range(2)] + [(dsa_w_in, 1280, P)]
                   + [(dsa_w_in, P * j, P) for j in range(HEADS)] + [(dsa_w_in, 1280 + P, P)]
                   + [(dsa_w_out, P * j, P) for j in range(KT)])
        FOX_SRC = [(fox_w_in, 3072, HEADS)]
        for j in range(HEADS):
            FOX_SRC += [(fox_w_in, P * j, P), (fox_w_in, 1024 + P * j, P), (fox_w_in, 2048 + P * j, P),
                        (fox_w_in, 3072 + HEADS + P * j, P)]
        FOX_SRC += [(fox_w_out, P * j, P) for j in range(KT)]

        block = ctx.enter_context(nc.Block())

        @block.sync
        def _(sp):
            def load(s, i, src, k, n):
                if s >= RING:
                    sp.wait_ge(lo_ready, s - RING + 1 + RING * i)
                sp.dma_start(wraw[:, s % RING, 0:k, 0:n], src).then_inc(raw_in[s % RING], 16)

            def ffn(f):
                for t, (f0, k) in enumerate(THIRDS):
                    up, down = third_units(f, t)

                    def up_body(up, f0, i):
                        for q in range(4):
                            col = (q % 2) * D_FF + (f0 + q // 2) * P + i * (2 * P)
                            load(up + q, i, blocks(gu(f), 0, KT, col, P), KT, P)
                    if up == 0:
                        load(0, 0, blocks(gu(f), 0, KT, 0, P), KT, P)
                        load(1, 0, blocks(gu(f), 0, KT, D_FF, P), KT, P)
                        sp.wait_ge(mod_step, 8)
                        load(2, 0, blocks(gu(f), 0, KT, P, P), KT, P)
                        load(3, 0, blocks(gu(f), 0, KT, D_FF + P, P), KT, P)
                        with sp.Fori(0, k // 2 - 1) as i:
                            up_body(up + 4, f0 + 2, i)
                    else:
                        with sp.Fori(0, k // 2) as i:
                            up_body(up, f0, i)
                    with sp.Fori(0, 2) as i:
                        for q in range(4):
                            load(down + q, i, blocks(dn(f), f0 * P, k, q * P + i * (4 * P), P), k, P)

            for b in range(NB):
                sp.dma_start(x_in[:, b, :], x[0, b * P:(b + 1) * P, :]).then_inc(x_load, 16)
            for f in range(16):
                if f == 9:
                    sp.wait_ge(xt_done, KT)
                if f == 13:
                    sp.wait_ge(mod_step, 4)
                if f == 14:
                    sp.wait_ge(mod_direct, 1)
                sp.dma_start(mod_slots[f], blocks(mod_w[0], 2 * (f % 4) * P, 2, FIRST_CHUNKS[f // 4] * MODC, MODC))\
                    .then_inc(mod_first[f], 16)
            ffn(0)
            for j, (w, c0, n) in enumerate(DSA_SRC):
                load(DSA_BASE + j, 0, blocks(w[0], 0, KT, c0, n), KT, n)
            ffn(1)
            ffn(2)
            for j, (w, c0, n) in enumerate(FOX_SRC):
                load(FOX_BASE + j, 0, blocks(w[0], 0, KT, c0, n), KT, n)
            ffn(3)
            for part in range(KT // 2):
                sp.wait_ge(y_copied_a, part + 1)
                sp.wait_ge(y_copied_d, part + 1)
                cols_ = slice(part * 2 * P, (part + 1) * 2 * P)
                sp.dma_start(out[0, :, cols_].rearrange("(b p) n -> p b n", p=P), y_out[:, :, cols_])\
                    .then_inc(stored, 16)
            sp.wait_ge(stored, 16 * KT // 2)

        @block.gpsimd
        def _(pool):
            pool.memset(ident[:, :], 0.0).then_inc(const_ready, 1)
            pool.memset(causal[:, :], 0.0).then_inc(const_ready, 1)
            pool.memset(ones[:, :], 1.0).then_inc(const_ready, 1)
            pool.memset(minus_half[:, :], -0.5).then_inc(const_ready, 1)
            pool.wait_ge(const_ready, 4)
            pool.affine_select(out=ident[:, :], in_=ident[:, :], compare_op=ALU.not_equal, fill=1.0, base=0,
                               pattern=[[-1, P]], channel_multiplier=1).then_inc(const_ready, 1)
            pool.affine_select(out=causal[:, :], in_=causal[:, :], compare_op=ALU.is_ge, fill=MASKED, base=0,
                               pattern=[[-1, P]], channel_multiplier=1).then_inc(const_ready, 1)

            def fill(c0, i, q):
                layer, col = c0 // MOD_CHUNKS, (c0 % MOD_CHUNKS) * MODC + i * MODC
                if 4 * c0 + q >= 18:
                    pool.wait_ge(mod_step, 2 * (4 * (c0 - PE_CHUNKS) + q - 1) + i * 8)
                pool.dma_start(mod_raw[:, q % 2, :, :], blocks(mod_w[layer], 2 * q * P, 2, col, MODC))\
                    .then_inc(mod_in[q % 2], 16)

            def chunks(c0, c1):
                with pool.Fori(0, c1 - c0) as i:
                    for q in range(4):
                        fill(c0, i, q)

            def job(j, n, at=0):
                pool.wait_ge(var_ready, j + 1)
                pool.tensor_tensor(rstd[:, j % 2, at:at + n], var[:, j % 2, at:at + n], minus_half[:, 0:n], ALU.pow)\
                    .then_inc(rstd_ready, 1)

            job(0, 4)
            pool.wait_ge(mod_step, 16)
            pool.wait_ge(mod_rest, 2)
            for q in range(4):
                fill(4, 0, q)
            chunks(5, 16)
            job(1, 4)
            pool.wait_ge(evicted, DSA_BASE + 5)
            pool.dma_start(ikd[64:128, :], ikx[0:64, :]).then_inc(ik_spread, 16)
            pool.dma_start(act_tmp[0:8, 0, :], ikx[64:72, :]).then_inc(ik_spread, 16)
            job(2, 8)

            def lo(n):
                pool.wait_ge(hi_ready, n + 1)
                pool.tensor_tensor(wlo[:, n % RING, :, :], wraw[:, n % RING, :, :],
                                   whi[:, n % RING, :, :].bitcast(F32), ALU.subtract).then_inc(lo_ready, 1)

            pool.wait_ge(lo_ready, DSA_BASE + 12)
            for j in range(HEADS):
                if j == HEADS - 1:
                    job(3, NB * EARLY)
                pool.wait_ge(q_rounded, j + 1)
                pool.tensor_tensor(hid_lo[:, j, :], act_tmp[:, j % 2, :], hid_hi[:, j, :].bitcast(F32), ALU.subtract)\
                    .then_inc(q_split, 1)
                lo(DSA_BASE + 12 + j)
            job(4, NB * (HEADS - EARLY), NB * EARLY)
            job(5, 4)
            chunks(16, 18)
            chunks(18, 28)
            job(6, 4)
            job(7, 4)
            chunks(28, 36)
            job(8, 4)
            for j in range(HEADS):
                job(9 + j, 8)
            job(17, 4)
            job(18, 4)

        NORM_JOB = [0, 1, 5, 6, 7, 8, 17, 18]

        SUMS_BEFORE = [0, 1, 2, 3, 3, 4, 5, 6]
        POST_RB = 4
        ROOTS_BEFORE = [0, 1, 3, 4, 5, 6, 15, 16]

        LAST_UNIT = {st: down + KT + 3 for st, down in (
            (1, third_units(0, 2)[1]), (2, DSA_BASE + 17), (3, third_units(1, 2)[1]), (5, third_units(2, 2)[1]),
            (6, FOX_BASE + 33), (7, third_units(3, 2)[1]))}

        @block.scalar
        def _(act):
            def hi(s, i=0):
                if s >= UNITS:
                    return
                act.wait_ge(raw_in[s % RING], 16 * (s // RING + 1) + 16 * i)
                if s >= RING:
                    act.wait_ge(unit_done, s - RING + 1 + RING * i)
                act.activation(whi[:, s % RING, :, :], wraw[:, s % RING, :, :], ACT.Copy).then_inc(hi_ready, 1)

            def square(st, d):
                if d == 0:
                    if st:
                        act.wait_ge(stat_done, SUMS_BEFORE[st])
                    act.activation(ssum[:, :], xT[:, 0, :], ACT.Square).then_inc(sq_ready, 1)
                else:
                    if d >= 3:
                        act.wait_ge(ssum_added, 6 * SUMS_BEFORE[st] + d - 2)
                    act.activation(sq[:, d % 2, :], xT[:, d, :], ACT.Square).then_inc(sq_ready, 1)

            def round_h(v, layer, which):
                sh = MOD_COLS * layer + 3 * KT * which
                for k in range(KT):
                    act.wait_ge(normed, KT * v + k + 1)
                    act.activation(h_hi[:, k, :], dve_tmp[:, k % 2, :], ACT.Identity, bias=modc[:, sh + k:sh + k + 1],
                                   scale=1.0).then_inc(h_rounded, 1)

            def ffn(f, st):
                for t, (f0, k) in enumerate(THIRDS):
                    up, down = third_units(f, t)

                    def up_body(up, i, h0):
                        for q in range(2):
                            s = up + 2 * q
                            act.wait_ge(unit_done, s + 2 + 4 * i)
                            if s >= 4:
                                act.wait_ge(evicted, s - 2 + 4 * i)
                            act.activation(act_tmp[:, q, :], bank[s % 4][:, :], ACT.Silu).then_inc(act_out, 1)
                            hi(s + 4, i)
                            hi(s + 5, i)
                            act.wait_ge(evicted, s + 2 + 4 * i)
                            act.activation(hid_hi[:, bass.ds(i * 2 + h0 + q, 1), :], dve_tmp[:, q:q + 1, :], ACT.Copy)\
                                .then_inc(hid_rounded, 1)
                    if up == 0:
                        up_body(0, 0, 0)
                        with act.Fori(0, k // 2 - 1) as i:
                            up_body(4, i, 2)
                    else:
                        with act.Fori(0, k // 2) as i:
                            up_body(up, i, 0)
                    if t < 2:
                        with act.Fori(0, 2) as i:
                            for q in range(4):
                                hi(down + q + 4, i)
                    else:
                        down_stats(down, st)

            def gain_square(d):
                if d >= 3:
                    act.wait_ge(gsum_added, d - 2)
                dst = gain_sum if d == 0 else gain_sq[:, d % 2, :]
                act.activation(dst, xT[:, d, :], ACT.Square, scale=cols[:, 8 + d:9 + d]).then_inc(gsq_ready, 1)

            def down_stats(down, st):
                for d in range(KT):
                    act.wait_ge(evicted, down + d + 1)
                    square(st, d)
                    if st == 3:
                        gain_square(d)
                    hi(down + d + 4)

            def exps(J, S, b):
                act.wait_ge(negmax_ready, J + 1)
                slot = J % len(S)
                sb_ = S[slot][:, BOFF[b]:BOFF[b] + (b + 1) * P]
                act.activation(sb_, sb_, ACT.Exp, bias=negmax[:, slot, b:b + 1], scale=1.0,
                               accum_out=rowsum[:, slot, b:b + 1]).then_inc(exp_done, 1)

            def round_pt(J, t):
                act.wait_ge(p_turned, NB * J + t + 1)
                if J and t == 0:
                    act.wait_ge(pv_done, J)
                act.activation(pt_hi[:, TOFF[t]:TOFF[t] + (NB - t) * P],
                               bank[T_BANK[t % 2]][:, 0:(NB - t) * P], ACT.Copy).then_inc(pt_rounded, 1)

            act.dma_start(rows[0:8, :], c[0, :].rearrange("(k p) -> k p", p=P)).then_inc(c_load, 16)
            act.wait_ge(c_turned, 1)
            act.activation(cond[:, :], bank[RB][:, 0:KT], ACT.Silu).then_inc(cond_ready, 1)
            act.dma_start(rows[8:24, :], post_gain.rearrange("l (k p) -> (l k) p", p=P)).then_inc(small_load, 16)
            for r, g in enumerate((dsa_q_gain, dsa_k_gain, fox_q_gain, fox_k_gain)):
                act.dma_start(rows[24 + r:25 + r, :], g[0:1, :]).then_inc(small_load, 16)
            for l in range(2):
                act.dma_start(modb_rows[0:MOD_COLS, l, :], mod_b[l, :].rearrange("(k p) -> k p", p=P))\
                    .then_inc(small_load, 16)
            act.dma_start(f_bias[:, :], fox_f_bias.rearrange("a h -> h a")).then_inc(small_load, 16)
            for k in range(KT):
                act.wait_ge(xt_done, k + 1)
                act.activation(xT[:, k, :], bank[k % 4][:, :], ACT.Copy).then_inc(xt_copied, 1)
            for k in range(KT):
                act.wait_ge(xt_copied, k + 1)
                square(0, k)
            act.wait_ge(stat_done, 1)
            for r in range(PE_CHUNKS):
                act.wait_ge(mod_direct, r + 1)
                act.activation(mod_row[r], bank[r][0:1, :], ACT.Copy).then_inc(row_ready, 1)
            hi(0)
            hi(1)
            round_h(0, 0, 0)
            hi(2)
            hi(3)
            ffn(0, 1)
            round_h(1, 0, 1)

            U = DSA_BASE
            for n in range(4):
                act.wait_ge(unit_done, U + max(n + 1, 2))
                act.activation(hid_hi[:, n, :], bank[(U + n) % 2][:, :], ACT.Copy).then_inc(iq_rounded, 1)
                hi(U + n + 4)
            for g in range(KV_HEADS):
                act.wait_ge(unit_done, U + 6 + g)
                act.activation(sq[:, g, :], bank[(U + 5 + g) % 2][:, :], ACT.Square).then_inc(qk_sq, 1)
                hi(U + 8 + g)
            act.wait_ge(ik_spread, 32)
            for r, src in ((0, ikx), (64, ikd)):
                act.activation(ik_hi[r:r + 64, :], src[r:r + 64, :], ACT.Copy).then_inc(ik_rounded, 1)
            hi(U + 10)

            def dsa_v_unit(g, n):
                act.wait_ge(unit_done, n + 1)
                act.wait_ge(evicted, n)
                act.activation(dsa_vT[:, g, :], bank[n % 2][:, :], ACT.Copy).then_inc(evicted, 1)
                hi(n + 4)

            dsa_v_unit(0, U + 7)
            for m in range(3 * IDX_HEADS):
                b = m // IDX_HEADS + 1
                act.wait_ge(dots_done, m + 1)
                if m >= 2:
                    act.wait_ge(relu_used, m - 1)
                act.activation(relu[:, m % 2, 0:(b + 1) * P], bank[S_BANK[m % 2]][:, 0:(b + 1) * P], ACT.Relu)\
                    .then_inc(relu_ready, 1)
            for j in range(HEADS):
                if j == 2:
                    for g in range(KV_HEADS):
                        act.wait_ge(qk_normed, g + 1)
                        act.activation(qk[:, g, :], dsa_k[:, g, :], ACT.Copy).then_inc(qk_rounded, 1)
                n = U + 8 + j
                act.wait_ge(unit_done, n + 1)
                act.wait_ge(qk_stat, max(j, 1))
                act.activation(sq[:, j % 2, :], bank[n % 2][:, :], ACT.Square).then_inc(qk_sq, 1)
                if j >= 2:
                    act.wait_ge(q_split, j - 1)
                act.activation(act_tmp[:, j % 2, :], bank[n % 2][:, :], ACT.Copy, scale=cols[:, 24:25])\
                    .then_inc(evicted, 1)
                act.wait_ge(evicted, n + 1)
                act.activation(hid_hi[:, j, :], act_tmp[:, j % 2, :], ACT.Copy).then_inc(q_rounded, 1)
                hi(n + 4)
            dsa_v_unit(1, U + 16)
            for g in range(KV_HEADS):
                act.wait_ge(v_turned, g + 1)
                act.activation(v_hi[:, g, :, :], bank[T_BANK[g]][:, :], ACT.Copy).then_inc(v_rounded, 1)
            for j in range(HEADS + 3):
                for b in range(NB):
                    if j >= 3:
                        round_pt(j - 3, b)
                    if 1 <= j <= HEADS:
                        exps(j - 1, dsa_S, b)
                if j >= 3:
                    act.wait_ge(pv_done, j - 2)
                    act.activation(hid_hi[:, j - 3, :], bank[OB][:, :], ACT.Copy).then_inc(hid_rounded, 1)
            down_stats(U + 17, 2)
            round_h(2, 0, 2)
            ffn(1, 3)
            round_h(3, 1, 0)
            ffn(2, 5)
            round_h(4, 1, 1)

            U = FOX_BASE
            act.wait_ge(unit_done, U + 1)
            hi(U + 4)
            act.wait_ge(fz_ready, 1)
            z_small = dve_tmp[0:HEADS, 1, :]
            act.activation(z_small, z_small, ACT.Exp).then_inc(ls_ready, 1)
            act.wait_ge(ls_ready, 1)
            act.activation(z_small, z_small, ACT.Ln, bias=ones[0:HEADS, 0:1], scale=1.0).then_inc(ls_ready, 1)

            def fox_units(j):
                n = U + 1 + 4 * j
                for q in range(2):
                    act.wait_ge(unit_done, n + q + 1)
                    if q == 0 and j:
                        act.wait_ge(qk_stat, 9 + j)
                    act.activation(act_tmp[:, q, :], bank[(n + q) % 2][:, :], ACT.Square).then_inc(qk_sq, 1)
                    hi(n + q + 4)
                act.wait_ge(nb_done, j + 1)
                act.activation(fox_nb[:, j % 2, :], bank[OB][:, :], ACT.Copy).then_inc(nb_ready, 1)
                act.wait_ge(unit_done, n + 3)
                act.wait_ge(evicted, n + 2)
                act.activation(fox_vT, bank[n % 2][:, :], ACT.Copy).then_inc(evicted, 1)
                for q in range(2):
                    act.wait_ge(qk_normed, 3 + 2 * j + q)
                    act.activation(qk[:, q, :], fox_qk[:, q, :], ACT.Copy).then_inc(qk_rounded, 1)
                act.wait_ge(v_turned, 3 + j)
                act.activation(v_hi[:, j % 2, :, :], bank[VB][:, :], ACT.Copy).then_inc(v_rounded, 1)
                hi(n + 6)
                act.wait_ge(unit_done, n + 4)
                act.activation(fox_sig[:, j % 2, :], bank[(n + 1) % 2][:, :], ACT.Sigmoid).then_inc(evicted, 1)
                if j == 0:
                    hi(n + 7)

            fox_units(0)
            for j in range(HEADS + 1):
                J = HEADS + j
                if j:
                    for t in range(NB):
                        round_pt(J - 1, t)
                    if j < HEADS:
                        hi(U + 1 + 4 * j + 7)
                if j < HEADS:
                    for b in range(NB):
                        exps(J, fox_S, b)
                if j:
                    act.wait_ge(gated, j)
                    act.activation(hid_hi[:, j - 1, :], dve_tmp[:, 1, :], ACT.Copy).then_inc(hid_rounded, 1)
                if j + 1 < HEADS:
                    fox_units(j + 1)
            down_stats(U + 33, 5 + 1)
            round_h(5, 1, 2)
            ffn(3, 7)
            for d in range(0, KT, 2):
                act.wait_ge(y_turned, d + 1)
                act.activation(y_out[:, :, d * P:(d + 1) * P],
                               bank[d % 4][:, :].rearrange("p (b n) -> p b n", b=NB), ACT.Copy).then_inc(y_copied_a, 1)

        @block.vector
        def _(dve):
            links = [0]

            def link(ins):
                links[0] += 1
                ins.then_inc(linked, 1)
                dve.wait_ge(linked, links[0])

            def lo(s, i=0):
                if s >= UNITS:
                    return
                dve.wait_ge(hi_ready, s + 1 + RING * i)
                dve.tensor_tensor(wlo[:, s % RING, :, :], wraw[:, s % RING, :, :], whi[:, s % RING, :, :].bitcast(F32),
                                  ALU.subtract).then_inc(lo_ready, 1)

            def mod_add(acc, src, k, done):
                if k == 0:
                    ins = dve.tensor_scalar(acc, src, cond[:, 0:1], None, ALU.mult)
                else:
                    dve.wait_ge(mod_step, done)
                    ins = dve.scalar_tensor_tensor(out=acc, in0=src, scalar=cond[:, k:k + 1], in1=acc, op0=ALU.mult,
                                                   op1=ALU.add)
                ins.then_inc(mod_step, 1)

            def mod_ops(c0, i, k0, k1):
                for k in range(k0, k1):
                    if k % 2 == 0:
                        dve.wait_ge(mod_in[(k // 2) % 2], 16 * (2 * (c0 - 4) + k // 4 + 1) + 32 * i)
                    if k == 0:
                        dve.wait_ge(mod_summed, c0 + i)
                    mod_add(mod_acc[:, :], mod_raw[:, (k // 2) % 2, k % 2, :], k, 8 * (c0 - PE_CHUNKS) + k + 8 * i)

            def first_ops(ch):
                for k in range(KT):
                    f = 4 * FIRST_CHUNKS.index(ch) + k // 2
                    if k % 2 == 0:
                        dve.wait_ge(mod_first[f], 16)
                    mod_add(first_acc[ch][:, 0:MODC], mod_slots[f][:, k % 2, :], k, 8 * ch + k)

            def mod_keep(c0, i):
                dve.wait_ge(mod_summed, c0 + 1 + i)
                dve.tensor_tensor(modc[:, bass.ds(4 * c0 + i * 4, 4)], bank[MODB][:, 0:4],
                                  modb[:, bass.ds(4 * c0 + i * 4, 4)], ALU.add).then_inc(mod_kept, 1)

            def add_sq(st, d):
                if 1 <= d <= 6:
                    dve.wait_ge(sq_ready, KT * SUMS_BEFORE[st] + d + 1)
                    if d >= 2:
                        dve.wait_ge(ssum_added, 6 * SUMS_BEFORE[st] + d - 1)
                    dve.tensor_tensor(ssum[:, :], ssum[:, :], sq[:, d % 2, :], ALU.add).then_inc(ssum_added, 1)

            def split_roots(j, n):
                dve.wait_ge(rstd_ready, j + 1)
                link(dve.tensor_copy(root[:, j % 2, 0, 0:n], rstd[:, j % 2, 0:n]))
                dve.tensor_tensor(root[:, j % 2, 1, 0:n], rstd[:, j % 2, 0:n], root[:, j % 2, 0, 0:n].bitcast(F32),
                                  ALU.subtract).then_inc(root_ready, 1)

            def spread_rstd(st):
                j = NORM_JOB[st]
                dve.wait_ge(stat_done, SUMS_BEFORE[st] + 1)
                dve.tensor_scalar(var[:, j % 2, 0:NB], bank[OB][:, 0:NB], 1.0 / D, EPS, ALU.mult, ALU.add)\
                    .then_inc(var_ready, 1)
                if st:
                    lo(LAST_UNIT[st])
                split_roots(j, NB)
                dve.wait_ge(rb_ready, st + 1)

            def spread_both():
                j, n = NORM_JOB[3] % 2, NORM_JOB[4] % 2
                dve.wait_ge(stat_done, 4)
                link(dve.tensor_scalar(gain_sums[:, :], bank[OB][:, NB:2 * NB], 1.0 / D, None, ALU.mult))
                dve.tensor_scalar(var[:, j, 0:NB], bank[OB][:, 0:NB], 1.0 / D, EPS, ALU.mult, ALU.add)\
                    .then_inc(var_ready, 1)
                lo(LAST_UNIT[3])
                dve.wait_ge(rstd_ready, NORM_JOB[3] + 1)
                link(dve.tensor_tensor(gain_sums[:, :], gain_sums[:, :], rstd[:, j, 0:NB], ALU.mult))
                link(dve.tensor_tensor(gain_sums[:, :], gain_sums[:, :], rstd[:, j, 0:NB], ALU.mult))
                dve.tensor_scalar(var[:, n, 0:NB], gain_sums[:, :], EPS, None, ALU.add).then_inc(var_ready, 1)
                split_roots(NORM_JOB[3], NB)
                dve.wait_ge(rstd_ready, NORM_JOB[4] + 1)
                link(dve.tensor_tensor(rstd[:, n, 0:NB], rstd[:, n, 0:NB], rstd[:, j, 0:NB], ALU.mult))
                split_roots(NORM_JOB[4], NB)
                dve.wait_ge(rb_ready, 5)

            def norm(v, st, layer, which, fused=False):
                base = MOD_COLS * layer + 3 * KT * which
                dve.wait_ge(mod_kept, (base + 2 * KT) // 4)
                link(dve.tensor_scalar(scale1[:, :], modc[:, base + KT:base + 2 * KT], 1.0, None, ALU.add))
                column = scale1
                if fused:
                    column = gain_scale
                    link(dve.tensor_tensor(gain_scale[:, :], scale1[:, :], cols[:, 8:8 + KT], ALU.mult))
                    spread_both()
                elif st:
                    spread_rstd(st)

                def lower(k):
                    dve.wait_ge(h_rounded, KT * v + k + 1)
                    dve.scalar_tensor_tensor(out=h_lo[:, k, :], in0=dve_tmp[:, k % 2, :],
                                             scalar=modc[:, base + k:base + k + 1],
                                             in1=h_hi[:, k, :].bitcast(F32), op0=ALU.add, op1=ALU.subtract)\
                        .then_inc(h_ready, 1)
                for k in range(KT):
                    if k >= 2:
                        dve.wait_ge(h_ready, KT * v + k - 1)
                    dve.scalar_tensor_tensor(out=dve_tmp[:, k % 2, :], in0=xT[:, k, :], scalar=column[:, k:k + 1],
                                             in1=bank[RB][:, :], op0=ALU.mult, op1=ALU.mult).then_inc(normed, 1)
                    if k:
                        lower(k - 1)
                lower(KT - 1)

            def make_gate(layer, which):
                base = MOD_COLS * layer + 3 * KT * which + 2 * KT
                dve.wait_ge(mod_kept, (base + KT) // 4)
                link(dve.tensor_scalar(gate[:, :], modc[:, base:base + KT], 0.5, None, ALU.mult))

            def add_x(s, d, i, g):
                dve.wait_ge(unit_done, s + 1 + 4 * i)
                dve.scalar_tensor_tensor(out=xT[:, bass.ds(i * 4 + d, 1), :], in0=bank[s % 4][:, :].unsqueeze(1),
                                         scalar=g[:, bass.ds(i * 4 + d, 1)], in1=xT[:, bass.ds(i * 4 + d, 1), :],
                                         op0=ALU.mult, op1=ALU.add).then_inc(evicted, 1)

            def down_stats(down, st, g):
                for d in range(KT):
                    add_x(down + d, d, 0, g)
                    add_sq(st, d - 1)
                    if st == 3 and 2 <= d:
                        dve.wait_ge(gsq_ready, d)
                        if d > 2:
                            dve.wait_ge(gsum_added, d - 2)
                        dve.tensor_tensor(gain_sum, gain_sum, gain_sq[:, (d - 1) % 2, :], ALU.add)\
                            .then_inc(gsum_added, 1)
                    if d:
                        lo(down + d + 3)

            def ffn(f, st):
                plan = mod_plan(f)
                for t, (f0, k) in enumerate(THIRDS):
                    up, down = third_units(f, t)
                    tile0 = HID_BASE[("ffn", f)] + f0
                    pair0 = PAIR_BASE[f] + f0
                    mod_up, mod_down = plan.get(("up", t)), plan.get(("down", t))

                    def up_body(i):
                        for q in range(2):
                            s = up + 2 * q
                            if mod_up is not None:
                                mod_ops(mod_up, i, 4 * q, 4 * q + 4)
                            dve.wait_ge(act_out, pair0 + q + 1 + 2 * i)
                            dve.tensor_tensor(dve_tmp[:, q, :], act_tmp[:, q, :], bank[(s + 1) % 4][:, :], ALU.mult)\
                                .then_inc(evicted, 2)
                            lo(s + 4, i)
                            dve.wait_ge(hid_rounded, tile0 + q + 1 + 2 * i)
                            dve.tensor_tensor(hid_lo[:, bass.ds(i * 2 + q, 1), :], dve_tmp[:, q:q + 1, :],
                                              hid_hi[:, bass.ds(i * 2 + q, 1), :].bitcast(F32), ALU.subtract)\
                                .then_inc(hid_ready, 1)
                            lo(s + 5, i)
                        if mod_up is not None:
                            mod_keep(mod_up, i)
                    with dve.Fori(0, k // 2) as i:
                        up_body(i)
                    if t == 0:
                        make_gate(f // 2, 2 * (f % 2))
                    if t < 2:
                        with dve.Fori(0, 2) as i:
                            for q in range(4):
                                if mod_down is not None:
                                    mod_ops(mod_down, i, 2 * q, 2 * q + 2)
                                add_x(down + q, q, i, gate)
                                lo(down + q + 4, i)
                            if mod_down is not None:
                                mod_keep(mod_down, i)
                    else:
                        down_stats(down, st, gate)

            def post(st, layer):
                spread_rstd(st)
                for d in range(KT):
                    at = 8 + KT * layer + d
                    dve.scalar_tensor_tensor(out=xT[:, d, :], in0=xT[:, d, :], scalar=cols[:, at:at + 1],
                                             in1=bank[RB][:, :], op0=ALU.mult, op1=ALU.mult).then_inc(posted, 1)

            def mask_rows(J, S, b, bias, scale):
                dve.wait_ge(s_done, NB * J + b + 1)
                if J >= len(S) and b == 0:
                    dve.wait_ge(p_turned, NB * (J - len(S) + 1))
                w, slot = (b + 1) * P, J % len(S)
                dve.tensor_tensor_reduce(out=S[slot][:, BOFF[b]:BOFF[b] + w], in0=bank[S_BANK[b % 2]][:, 0:w],
                                         in1=bias, scale=scale, scalar=-3e38, op0=ALU.add, op1=ALU.max,
                                         accum_out=rowmax[:, slot, b:b + 1]).then_inc(masked, 1)

            def negate_max(J, S):
                slot = J % len(S)
                dve.wait_ge(masked, NB * (J + 1))
                dve.tensor_scalar(negmax[:, slot, :], rowmax[:, slot, :], -1.0, None, ALU.mult)\
                    .then_inc(negmax_ready, 1)

            def invert_sums(J, S):
                slot = J % len(S)
                dve.wait_ge(exp_done, NB * (J + 1))
                link(dve.reciprocal(rowinv[:, slot, :], rowsum[:, slot, :]))

            def normalise(J, S, b):
                slot = J % len(S)
                sb_ = S[slot][:, BOFF[b]:BOFF[b] + (b + 1) * P]
                dve.tensor_scalar(sb_, sb_, rowinv[:, slot, b:b + 1], None, ALU.mult).then_inc(p_ready, 1)

            def split_pt(J, t):
                dve.wait_ge(pt_rounded, NB * J + t + 1)
                at, w = TOFF[t], (NB - t) * P
                dve.tensor_tensor(pt_lo[:, at:at + w], bank[T_BANK[t % 2]][:, 0:w], pt_hi[:, at:at + w].bitcast(F32),
                                  ALU.subtract).then_inc(pt_ready, 1)

            def split_v(slot, src, n):
                dve.wait_ge(v_rounded, n)
                dve.tensor_tensor(v_lo[:, slot, :, :], src[:, :].rearrange("p (b n) -> p b n", b=NB),
                                  v_hi[:, slot, :, :].bitcast(F32), ALU.subtract).then_inc(v_ready, 1)

            dve.wait_ge(const_ready, 6)
            dve.tensor_copy(ident_r[:, :], ident[:, :])
            dve.tensor_copy(ident_b[:, :], ident[:, :]).then_inc(bf_ready, 1)
            dve.wait_ge(cond_ready, 1)
            first_ops(0)
            for d in range(KT):
                add_sq(0, d)
            first_ops(1)
            spread_rstd(0)
            dve.wait_ge(rows_turned, 1)
            dve.tensor_copy(modb[:, :], bank[4][:, 32:32 + 2 * MOD_COLS])
            dve.tensor_copy(cols[:, :], bank[4][:, 0:28]).then_inc(cols_ready, 1)
            dve.wait_ge(cols_ready, 1)
            dve.tensor_scalar(kgain[:, 0:1], cols[:, 25:26], float(HD) ** 0.5, None, ALU.mult)
            link(dve.tensor_scalar(kgain[:, 1:2], cols[:, 27:28], float(HD) ** 0.5, None, ALU.mult))
            for k in range(PE_TILES, KT):
                if k % 2 == 0:
                    dve.wait_ge(mod_first[12 + k // 2], 16)
                src = mod_slots[12 + k // 2][:, k % 2, :]
                if k == PE_TILES:
                    dve.wait_ge(mod_summed, 1)
                    ins = dve.tensor_scalar(mod_acc[:, :], src, cond[:, k:k + 1], None, ALU.mult)
                else:
                    dve.wait_ge(mod_rest, k - PE_TILES)
                    ins = dve.scalar_tensor_tensor(out=mod_acc[:, :], in0=src, scalar=cond[:, k:k + 1],
                                                   in1=mod_acc[:, :], op0=ALU.mult, op1=ALU.add)
                ins.then_inc(mod_rest, 1)
            lo(0)
            lo(1)
            dve.wait_ge(mod_summed, 4)
            dve.tensor_tensor(modc[:, 0:16], bank[MODB][:, 0:16], modb[:, 0:16], ALU.add).then_inc(mod_kept, 4)
            norm(0, 0, 0, 0)
            lo(2)
            lo(3)
            ffn(0, 1)
            norm(1, 1, 0, 1)

            U = DSA_BASE
            for n in range(4):
                dve.wait_ge(iq_rounded, n + 1)
                dve.tensor_tensor(hid_lo[:, n, :], bank[(U + n) % 2][:, :], hid_hi[:, n, :].bitcast(F32), ALU.subtract)\
                    .then_inc(evicted, 1)
                lo(U + 4 + n)
            dve.wait_ge(unit_done, U + 5)
            dve.tensor_copy(ikx[0:72, :], bank[(U + 4) % 2][0:72, :]).then_inc(evicted, 1)
            for g in range(KV_HEADS):
                dve.wait_ge(qk_sq, g + 1)
                dve.tensor_scalar(dsa_k[:, g, :], bank[(U + 5 + g) % 2][:, :], kgain[:, 0:1], None, ALU.mult)\
                    .then_inc(evicted, 1)
                lo(U + 8 + g)
            dve.wait_ge(iw_turned, 1)
            link(dve.tensor_scalar(iw[:, :], bank[T_BANK[0]][:, 0:NB * 8], float(IDX_HEADS * IDX_DIM) ** -0.5, None,
                                   ALU.mult))
            for n, (r, src) in enumerate(((0, ikx), (64, ikd))):
                dve.wait_ge(ik_rounded, n + 1)
                dve.tensor_tensor(ik_lo[r:r + 64, :], src[r:r + 64, :], ik_hi[r:r + 64, :].bitcast(F32), ALU.subtract)\
                    .then_inc(ik_split, 1)
            for m in range(3 * IDX_HEADS):
                b, head = m // IDX_HEADS + 1, m % IDX_HEADS
                dve.wait_ge(relu_ready, m + 1)
                w, at = (b + 1) * P, 8 * b + head
                sc = mask[:, BOFF[b]:BOFF[b] + w]
                if head == 0:
                    ins = dve.tensor_scalar(sc, relu[:, m % 2, 0:w], iw[:, at:at + 1], None, ALU.mult)
                else:
                    dve.wait_ge(relu_used, m)
                    ins = dve.scalar_tensor_tensor(out=sc, in0=relu[:, m % 2, 0:w], scalar=iw[:, at:at + 1], in1=sc,
                                                   op0=ALU.mult, op1=ALU.add)
                ins.then_inc(relu_used, 1)
            lo(U + 10)
            lo(U + 11)
            link(dve.memset(mask[:, 0:P], 0.0))
            link(dve.memset(mask[0:CHUNK, P - CHUNK:P], MASKED))
            dve.wait_ge(qk_stat, 1)
            dve.tensor_scalar(var[:, 0, 0:8], bank[STAT][:, 0:8], 1.0, HD * EPS, ALU.mult, ALU.add)\
                .then_inc(var_ready, 1)

            def top_k(b, r0, r1):
                w = (b + 1) * P
                sc = mask[:, BOFF[b]:BOFF[b] + w]
                if r0 == 0:
                    link(dve.memset(mask[0:CHUNK, BOFF[b] + w - CHUNK:BOFF[b] + w], OUTSIDE))
                for r in range(r0, r1):
                    link(dve.max(top8[:, :], sc))
                    link(dve.match_replace(out=sc, in_to_replace=top8[:, :], in_values=sc, imm_value=TAKEN))
                if r1 == TOPK // 8:
                    link(dve.tensor_scalar(sc, sc, (TAKEN + OUTSIDE) / 2, MASKED, ALU.is_gt, ALU.mult))

            top_k(1, 0, 3)
            split_roots(2, 2 * NB)
            top_k(1, 3, 16)
            for g in range(KV_HEADS):
                dve.wait_ge(k_rb, g + 1)
                dve.tensor_tensor(dsa_k[:, g, :], dsa_k[:, g, :], bank[K_BANK[g]][:, :], ALU.mult)\
                    .then_inc(qk_normed, 1)
            for g in range(KV_HEADS):
                dve.wait_ge(qk_rounded, g + 1)
                dve.tensor_tensor(qk[:, 2 + g, :], dsa_k[:, g, :], qk[:, g, :].bitcast(F32), ALU.subtract)\
                    .then_inc(k_ready, 1)
            top_k(2, 0, 16)
            top_k(3, 0, 10)
            dve.wait_ge(qk_stat, 1 + EARLY)
            dve.tensor_scalar(var[:, 1, 0:NB * EARLY], bank[STAT][:, 0:NB * EARLY], 1.0, HD * EPS, ALU.mult,
                              ALU.add).then_inc(var_ready, 1)
            top_k(3, 10, 16)
            dve.wait_ge(qk_stat, 1 + HEADS)
            dve.tensor_scalar(var[:, 0, NB * EARLY:], bank[STAT][:, NB * EARLY:NB * HEADS], 1.0, HD * EPS, ALU.mult,
                              ALU.add).then_inc(var_ready, 1)
            dve.wait_ge(rstd_ready, 4)
            for j in range(HEADS + 3):
                if j == EARLY:
                    dve.wait_ge(rstd_ready, 5)
                if 2 <= j <= HEADS + 1:
                    invert_sums(j - 2, dsa_S)
                if j >= 3:
                    split_pt(j - 3, 0)
                for b in range(NB):
                    if j >= 3 and b < NB - 1:
                        split_pt(j - 3, b + 1)
                    if j < HEADS:
                        at = NB * j + b
                        mask_rows(j, dsa_S, b, mask[:, BOFF[b]:BOFF[b] + (b + 1) * P],
                                  rstd[:, int(j < EARLY), at:at + 1])
                    if 2 <= j <= HEADS + 1:
                        normalise(j - 2, dsa_S, b)
                if j < HEADS:
                    negate_max(j, dsa_S)
                if j == 1:
                    for g in range(KV_HEADS):
                        split_v(g, bank[T_BANK[g]], g + 1)
                if j == HEADS:
                    dve.wait_ge(lo_ready, U + 20)
                    lo(U + 20)
                if j >= 3:
                    dve.wait_ge(hid_rounded, HID_BASE["dsa"] + j - 2)
                    dve.tensor_tensor(hid_lo[:, j - 3, :], bank[OB][:, :], hid_hi[:, j - 3, :].bitcast(F32),
                                      ALU.subtract).then_inc(hid_ready, 1)
            down_stats(U + 17, 2, modc[:, 5 * KT:6 * KT])
            norm(2, 2, 0, 2)
            ffn(1, 3)
            norm(3, 3, 1, 0, fused=True)
            for d in range(KT):
                dve.scalar_tensor_tensor(out=xT[:, d, :], in0=xT[:, d, :], scalar=cols[:, 8 + d:9 + d],
                                         in1=bank[POST_RB][:, :], op0=ALU.mult, op1=ALU.mult).then_inc(posted, 1)
            dve.wait_ge(posted, KT)
            ffn(2, 5)
            norm(4, 5, 1, 1)

            U = FOX_BASE
            z, z_small = dve_tmp[0:HEADS, 0, :], dve_tmp[0:HEADS, 1, :]
            dve.wait_ge(unit_done, U + 1)
            dve.memset(sq[0:HEADS, 0, :], 1.0)
            dve.tensor_scalar(z, bank[U % 2][0:HEADS, :], f_bias[:, 0:1], None, ALU.add).then_inc(evicted, 1)
            dve.wait_ge(evicted, U + 1)
            dve.scalar_tensor_tensor(out=z_small, in0=z, scalar=-1.0, in1=z, op0=ALU.mult, op1=ALU.min)\
                .then_inc(fz_ready, 1)
            lo(U + 4)
            dve.wait_ge(ls_ready, 2)
            link(dve.scalar_tensor_tensor(out=z, in0=z, scalar=0.0, in1=z_small, op0=ALU.min, op1=ALU.subtract))
            link(dve.tensor_tensor_scan(cum[0:HEADS, :], sq[0:HEADS, 0, :], z, 0.0, ALU.mult, ALU.subtract))
            link(dve.tensor_copy(cum_hi, cum[0:HEADS, :]))
            dve.tensor_tensor(cum_lo, cum[0:HEADS, :], cum_hi.bitcast(F32), ALU.subtract).then_inc(cum_ready, 1)

            def fox_units(j):
                n = U + 1 + 4 * j
                for q, g in enumerate((cols[:, 26:27], kgain[:, 1:2])):
                    dve.wait_ge(qk_sq, 11 + 2 * j + q)
                    if j:
                        dve.wait_ge(k_ready, 2 + 2 * j)
                    dve.tensor_scalar(fox_qk[:, q, :], bank[(n + q) % 2][:, :], g, None, ALU.mult).then_inc(evicted, 1)
                    lo(n + q + 4)
                dve.wait_ge(qk_stat, 10 + j)
                dve.tensor_scalar(var[:, (9 + j) % 2, 0:8], bank[STAT][:, 0:8], 1.0, HD * EPS, ALU.mult, ALU.add)\
                    .then_inc(var_ready, 1)
                split_roots(9 + j, 2 * NB)
                for q in range(2):
                    dve.wait_ge(k_rb, 3 + 2 * j + q)
                    dve.tensor_tensor(fox_qk[:, q, :], fox_qk[:, q, :], bank[KV_BANK[q]][:, :], ALU.mult)\
                        .then_inc(qk_normed, 1)
                for q in range(2):
                    dve.wait_ge(qk_rounded, 3 + 2 * j + q)
                    dve.tensor_tensor(qk[:, 2 + q, :], fox_qk[:, q, :], qk[:, q, :].bitcast(F32), ALU.subtract)\
                        .then_inc(k_ready, 1)
                split_v(j % 2, bank[VB], 3 + j)
                lo(n + 6)
                if j == 0:
                    lo(n + 7)

            fox_units(0)
            for j in range(HEADS + 1):
                J = HEADS + j
                if j:
                    split_pt(J - 1, 0)
                for b in range(NB):
                    if j and b < NB - 1:
                        split_pt(J - 1, b + 1)
                    if j < HEADS:
                        if b == 0:
                            dve.wait_ge(nb_ready, j + 1)
                        mask_rows(J, fox_S, b, fox_nb[:, j % 2, 0:(b + 1) * P], 1.0)
                if j < HEADS:
                    negate_max(J, fox_S)
                if j:
                    dve.wait_ge(pv_done, J)
                    dve.wait_ge(hid_ready, HID_BASE["fox"] + j - 1)
                    dve.tensor_tensor(dve_tmp[:, 1, :], bank[OB][:, :], fox_sig[:, (j - 1) % 2, :], ALU.mult)\
                        .then_inc(gated, 1)
                    dve.wait_ge(hid_rounded, HID_BASE["fox"] + j)
                    dve.tensor_tensor(hid_lo[:, j - 1, :], dve_tmp[:, 1, :], hid_hi[:, j - 1, :].bitcast(F32),
                                      ALU.subtract).then_inc(hid_ready, 1)
                if 1 <= j < HEADS:
                    lo(U + 1 + 4 * j + 7)
                if j < HEADS:
                    invert_sums(J, fox_S)
                    for b in range(NB):
                        normalise(J, fox_S, b)
                if j + 1 < HEADS:
                    fox_units(j + 1)
            down_stats(U + 33, 6, modc[:, MOD_COLS + 5 * KT:MOD_COLS + 6 * KT])
            norm(5, 6, 1, 2)
            ffn(3, 7)
            post(7, 1)
            for d in range(1, KT, 2):
                dve.wait_ge(y_turned, d + 1)
                dve.tensor_copy(y_out[:, :, d * P:(d + 1) * P],
                                bank[d % 4][:, :].rearrange("p (b n) -> p b n", b=NB)).then_inc(y_copied_d, 1)

        @block.tensor
        def _(pe):
            def with_hi(dst, s, k, hi_, first):
                w = s % RING
                pe.matmul(dst, whi[:, w, k, :], hi_, start=first, stop=False)
                pe.matmul(dst, wlo[:, w, k, :], hi_, start=False, stop=False)

            def with_lo(dst, s, k, lo_, last):
                return pe.matmul(dst, whi[:, s % RING, k, :], lo_, start=False, stop=last)

            def keep_warm(n, st=1):
                for _ in range(n if st else 0):
                    pe.matmul(bank[MODB][:, :], ident_r[:, :], hid_hi[:, 0, :], start=True, stop=True)

            def unit(s, i, dst, K, A_hi, A_lo, free, ready=None):
                pe.wait_ge(lo_ready, s + 1 + RING * i)
                if free > 0 or not isinstance(i, int):
                    pe.wait_ge(evicted, free + RING * i)
                for k in range(K):
                    if ready is not None:
                        pe.wait_ge(hid_rounded, ready + k + 1)
                    with_hi(dst, s, k, A_hi[:, k, :], k == 0)
                    if ready is not None:
                        pe.wait_ge(hid_ready, ready + k + 1)
                    ins = with_lo(dst, s, k, A_lo[:, k, :], k == K - 1)
                ins.then_inc(unit_done, 1)

            def pair(s, i, banks, free, v=None):
                pe.wait_ge(lo_ready, s + 2 + RING * i)
                if s > 2 or not isinstance(i, int):
                    pe.wait_ge(evicted, free + RING * i)
                for k in range(KT):
                    if v is not None:
                        pe.wait_ge(h_rounded, KT * v + k + 1)
                    for q in range(2):
                        with_hi(bank[banks[q]][:, :], s + q, k, h_hi[:, k, :], k == 0)
                    if v is not None:
                        pe.wait_ge(h_ready, KT * v + k + 1)
                    for q in range(2):
                        ins = with_lo(bank[banks[q]][:, :], s + q, k, h_lo[:, k, :], k == KT - 1)
                ins.then_inc(unit_done, 2)

            def mod_sum(c0, i):
                pe.wait_ge(mod_step, 8 * (c0 - PE_CHUNKS + 1) + 8 * i)
                pe.wait_ge(mod_kept, c0 + i)
                for q in range(4):
                    ins = pe.matmul(bank[MODB][:, q:q + 1], mod_acc[:, q * P:(q + 1) * P], ones[:, 0:1], start=True,
                                    stop=True)
                ins.then_inc(mod_summed, 1)

            def first_sum(ch):
                pe.wait_ge(mod_step, 8 * (ch + 1))
                for q in range(4):
                    ins = pe.matmul(bank[MODB][:, 4 * ch + q:4 * ch + q + 1], first_acc[ch][:, q * P:(q + 1) * P],
                                    ones[:, 0:1], start=True, stop=True)
                ins.then_inc(mod_summed, 1)

            def first_direct(ch, tiles):
                for k in range(tiles):
                    f = 4 * FIRST_CHUNKS.index(ch) + k // 2
                    if k % 2 == 0:
                        pe.wait_ge(mod_first[f], 16)
                    ins = pe.matmul(bank[ch - 2][0:1, :], cond[:, k:k + 1], mod_slots[f][:, k % 2, :], start=(k == 0),
                                    stop=(k == tiles - 1))
                ins.then_inc(mod_direct, 1)

            def row_to_columns(ch):
                pe.wait_ge(row_ready, ch - 1)
                if ch == 3:
                    pe.wait_ge(mod_rest, KT - PE_TILES)
                for q in range(4):
                    dst = bank[MODB][:, 4 * ch + q:4 * ch + q + 1]
                    ins = pe.matmul(dst, mod_row[ch - 2][:, q * P:(q + 1) * P], ones[0:1, 0:1], start=True,
                                    stop=(ch == 2))
                    if ch == 3:
                        ins = pe.matmul(dst, mod_acc[:, q * P:(q + 1) * P], ones[:, 0:1], start=False, stop=True)
                ins.then_inc(mod_summed, 1)

            def spread(dst, j, at):
                for b in range(NB):
                    for part in range(2):
                        column = root[:, j % 2, part, at + b:at + b + 1].broadcast_to([P, P])
                        ins = pe.matmul(dst[:, b * P:(b + 1) * P], column, ident_r[:, :], start=(part == 0),
                                        stop=(part == 1))
                return ins

            def stat(st):
                keep_warm(3, st)
                pe.wait_ge(ssum_added, 6 * (SUMS_BEFORE[st] + 1))
                for b in range(NB):
                    pe.matmul(bank[OB][:, b:b + 1], ssum[:, b * P:(b + 1) * P], ones[:, 0:1], start=(b == 0),
                              stop=False, skip_group_check=True)
                if st == 3:
                    pe.wait_ge(gsum_added, 6)
                    for b in range(NB):
                        pe.matmul(bank[OB][:, NB + b:NB + b + 1], gain_sum[:, b * P:(b + 1) * P], ones[:, 0:1],
                                  start=False, stop=False, skip_group_check=True)
                    pe.wait_ge(gsq_ready, KT)
                    for b in range(NB):
                        pe.matmul(bank[OB][:, NB + b:NB + b + 1], gain_sq[:, 1, b * P:(b + 1) * P], ones[:, 0:1],
                                  start=False, stop=True, skip_group_check=True)
                keep_warm(2, st)
                pe.wait_ge(sq_ready, KT * (SUMS_BEFORE[st] + 1))
                for b in range(NB):
                    ins = pe.matmul(bank[OB][:, b:b + 1], sq[:, 1, b * P:(b + 1) * P], ones[:, 0:1], start=False,
                                    stop=True, skip_group_check=True)
                ins.then_inc(stat_done, 1)
                keep_warm(8, st)
                pe.wait_ge(root_ready, ROOTS_BEFORE[st] + 1)
                spread(bank[POST_RB if st == 3 else RB], NORM_JOB[st], 0).then_inc(rb_ready, 1)
                if st == 3:
                    keep_warm(8)
                    pe.wait_ge(root_ready, ROOTS_BEFORE[4] + 1)
                    spread(bank[RB], NORM_JOB[4], 0).then_inc(rb_ready, 1)
                keep_warm(6, st)

            def ffn(f, v):
                plan = mod_plan(f)
                for t, (f0, k) in enumerate(THIRDS):
                    up, down = third_units(f, t)
                    mod_up, mod_down = plan.get(("up", t)), plan.get(("down", t))

                    def up_body(i, first):
                        for q in range(2):
                            s = up + 2 * q
                            pair(s, i, (s % 4, (s + 1) % 4), s - 2, v if first and q == 0 else None)
                        if mod_up is not None:
                            mod_sum(mod_up, i)
                    if t == 0:
                        up_body(0, True)
                        up += 4
                        if mod_up is not None:
                            mod_up += 1
                        with pe.Fori(0, k // 2 - 1) as i:
                            up_body(i, False)
                    else:
                        with pe.Fori(0, k // 2) as i:
                            up_body(i, False)
                    tile0 = HID_BASE[("ffn", f)] + f0

                    def down_body(i, q0, n):
                        for q in range(q0, n):
                            s = down + q
                            unit(s, i, bank[s % 4][:, :], k, hid_hi, hid_lo, s - 3, tile0 if q == 0 else None)
                    if t < 2:
                        with pe.Fori(0, 2) as i:
                            down_body(i, 0, 4)
                            if mod_down is not None:
                                mod_sum(mod_down, i)
                    else:
                        down_body(0, 0, KT)

            def turn_p(J, S, t):
                if t == 0:
                    pe.wait_ge(p_ready, NB * (J + 1))
                if J or t >= 2:
                    pe.wait_ge(pt_ready, NB * J + t - 1)
                for b in range(t, NB):
                    ins = pe.transpose(bank[T_BANK[t % 2]][:, (b - t) * P:(b - t + 1) * P],
                                       S[J % len(S)][:, BOFF[b] + t * P:BOFF[b] + (t + 1) * P], ident[:, :])
                ins.then_inc(p_turned, 1)

            def pv(J, v):
                pe.wait_ge(pt_ready, NB * (J + 1))
                for t in range(NB):
                    cols_ = slice(TOFF[t], TOFF[t] + (NB - t) * P)
                    for n, (V, PT) in enumerate(((v_hi, pt_hi), (v_hi, pt_lo), (v_lo, pt_hi))):
                        ins = pe.matmul(bank[OB][:, t * P:SEQ], V[:, v, t, :], PT[:, cols_], start=(t == n == 0),
                                        stop=(t == NB - 1 and n == 2))
                ins.then_inc(pv_done, 1)

            def score(dst, q_hi, q_lo, k_hi, k_lo, last):
                pe.matmul(dst, q_hi, k_hi, start=True, stop=False)
                pe.matmul(dst, q_hi, k_lo, start=False, stop=False)
                return pe.matmul(dst, q_lo, k_hi, start=False, stop=last)

            pe.wait_ge(const_ready, 6)
            pe.wait_ge(c_load, 16)
            pe.transpose(bank[RB][:, 0:KT], rows[0:KT, :], ident[0:KT, 0:KT]).then_inc(c_turned, 1)
            pe.wait_ge(x_load, 16 * NB)
            for k in range(KT):
                if k >= 4:
                    pe.wait_ge(xt_copied, k - 3)
                for b in range(NB):
                    ins = pe.transpose(bank[k % 4][:, b * P:(b + 1) * P], x_in[:, b, k * P:(k + 1) * P], ident[:, :])
                ins.then_inc(xt_done, 1)
            pe.wait_ge(xt_copied, KT)
            pe.wait_ge(cond_ready, 1)
            first_sum(0)
            first_direct(2, KT)
            stat(0)
            pe.wait_ge(small_load, 16 * 8)
            pe.transpose(bank[4][:, 0:28], rows[0:28, :], ident[0:28, 0:28])
            for l in range(2):
                ins = pe.transpose(bank[4][:, 32 + MOD_COLS * l:32 + MOD_COLS * (l + 1)], modb_rows[0:MOD_COLS, l, :],
                                   ident[0:MOD_COLS, 0:MOD_COLS])
            ins.then_inc(rows_turned, 1)
            row_to_columns(2)
            first_sum(1)
            first_direct(3, PE_TILES)
            row_to_columns(3)
            ffn(0, 0)
            stat(1)

            U = DSA_BASE
            pair(U, 0, (U % 2, (U + 1) % 2), U, 1)
            for n in range(2, 7):
                unit(U + n, 0, bank[(U + n) % 2][:, :], KT, h_hi, h_lo, U + n - 1)
            pe.wait_ge(ik_spread, 32)
            for b in range(NB):
                ins = pe.transpose(bank[T_BANK[0]][:, 8 * b:8 * b + 8], act_tmp[0:8, 0, b * P:(b + 1) * P],
                                   ident[0:8, 0:8])
            ins.then_inc(iw_turned, 1)
            unit(U + 7, 0, bank[(U + 7) % 2][:, :], KT, h_hi, h_lo, U + 6)
            pe.wait_ge(ik_split, 2)
            for m in range(3 * IDX_HEADS):
                b, head = m // IDX_HEADS + 1, m % IDX_HEADS
                if m >= 2:
                    pe.wait_ge(relu_ready, m - 1)
                r = 64 * (head % 2)
                w = (b + 1) * P
                score(bank[S_BANK[m % 2]][:, 0:w], hid_hi[r:r + 64, head // 2, b * P:w],
                      hid_lo[r:r + 64, head // 2, b * P:w], ik_hi[r:r + 64, 0:w], ik_lo[r:r + 64, 0:w], True)\
                    .then_inc(dots_done, 1)
            pe.wait_ge(qk_sq, 2)
            for g in range(KV_HEADS):
                for b in range(NB):
                    ins = pe.matmul(bank[STAT][:, NB * g + b:NB * g + b + 1], sq[:, g, b * P:(b + 1) * P],
                                    ones[:, 0:1], start=True, stop=True)
            ins.then_inc(qk_stat, 1)

            def dsa_q_stat(j):
                pe.wait_ge(qk_sq, 3 + j)
                if j == 0:
                    pe.wait_ge(var_ready, 3)
                if j == EARLY:
                    pe.wait_ge(var_ready, 4)
                for b in range(NB):
                    ins = pe.matmul(bank[STAT][:, NB * j + b:NB * j + b + 1], sq[:, j % 2, b * P:(b + 1) * P],
                                    ones[:, 0:1], start=True, stop=True)
                ins.then_inc(qk_stat, 1)

            for j in range(HEADS):
                n = U + 8 + j
                unit(n, 0, bank[n % 2][:, :], KT, h_hi, h_lo, n - 1)
                if j:
                    dsa_q_stat(j - 1)
                if j == 0:
                    pe.wait_ge(root_ready, 3)
                    for g in range(KV_HEADS):
                        spread(bank[K_BANK[g]], 2, NB * g).then_inc(k_rb, 1)
            unit(U + 16, 0, bank[(U + 16) % 2][:, :], KT, h_hi, h_lo, U + 15)
            dsa_q_stat(HEADS - 1)
            pe.wait_ge(evicted, U + 17)
            for g in range(KV_HEADS):
                for b in range(NB):
                    ins = pe.transpose(bank[T_BANK[g]][:, b * P:(b + 1) * P], dsa_vT[:, g, b * P:(b + 1) * P],
                                       ident[:, :])
                ins.then_inc(v_turned, 1)

            def dsa_score(j, b):
                if j or b >= 2:
                    pe.wait_ge(masked, NB * j + b - 1)
                if b == 0 and j < HEADS:
                    pe.wait_ge(q_split, j + 1)
                w, g = (b + 1) * P, j // GROUP
                score(bank[S_BANK[b % 2]][:, 0:w], hid_hi[:, j, b * P:w], hid_lo[:, j, b * P:w], qk[:, g, 0:w],
                      qk[:, 2 + g, 0:w], True).then_inc(s_done, 1)

            def heads(j, lag, score_of, turn_of, pv_of):
                order = [(0, 0), (0, 1), (1, 0), (0, 2), (1, 1), (0, 3), (1, 2), (1, 3), (2, 0)]
                for kind, b in order:
                    if kind == 0 and j >= lag:
                        turn_of(b)
                    if kind == 1 and j < HEADS:
                        score_of(b)
                    if kind == 2 and j >= lag:
                        pv_of()

            for j in range(HEADS + 3):
                def pv_of():
                    if j >= 4:
                        pe.wait_ge(hid_ready, HID_BASE["dsa"] + j - 3)
                    pv(j - 3, (j - 3) // GROUP)
                if j == 3:
                    pe.wait_ge(v_ready, 2)
                heads(j, 3, lambda b: dsa_score(j, b), lambda t: turn_p(j - 3, dsa_S, t), pv_of)
            for d in range(KT):
                s = U + 17 + d
                unit(s, 0, bank[s % 4][:, :], KT, hid_hi, hid_lo, s - 1, HID_BASE["dsa"] if d == 0 else None)
            stat(2)
            ffn(1, 2)
            stat(3)
            ffn(2, 3)
            stat(5)

            U = FOX_BASE
            pair(U, 0, (U % 2, (U + 1) % 2), U, 4)

            def fox_units(j):
                n = U + 1 + 4 * j
                if j:
                    unit(n, 0, bank[n % 2][:, :], KT, h_hi, h_lo, n - 1)
                unit(n + 1, 0, bank[(n + 1) % 2][:, :], KT, h_hi, h_lo, n)
                if j == 0:
                    pe.wait_ge(cum_ready, 1)
                if j > 1:
                    pe.wait_ge(gated, j - 1)
                head = ident_r[0:HEADS, j:j + 1].broadcast_to([HEADS, P])
                pe.matmul(bank[OB][:, :], head, cum_hi, start=True, stop=False)
                pe.matmul(bank[OB][:, :], head, cum_lo, start=False, stop=True).then_inc(nb_done, 1)
                pe.wait_ge(qk_sq, 12 + 2 * j)
                for q in range(2):
                    for b in range(NB):
                        ins = pe.matmul(bank[STAT][:, NB * q + b:NB * q + b + 1], act_tmp[:, q, b * P:(b + 1) * P],
                                        ones[:, 0:1], start=True, stop=True)
                ins.then_inc(qk_stat, 1)
                unit(n + 2, 0, bank[n % 2][:, :], KT, h_hi, h_lo, n + 1)
                pe.wait_ge(root_ready, 8 + j)
                for q in range(2):
                    spread(bank[KV_BANK[q]], 9 + j, NB * q).then_inc(k_rb, 1)
                pe.wait_ge(evicted, n + 3)
                if j:
                    pe.wait_ge(masked, NB * (HEADS + j))
                for b in range(NB):
                    ins = pe.transpose(bank[VB][:, b * P:(b + 1) * P], fox_vT[:, b * P:(b + 1) * P], ident[:, :])
                ins.then_inc(v_turned, 1)
                unit(n + 3, 0, bank[(n + 1) % 2][:, :], KT, h_hi, h_lo, n + 2)

            def fox_score(j, b):
                if b == 0:
                    pe.wait_ge(k_ready, 4 + 2 * j)
                    pe.wait_ge(v_ready, 3 + j)
                pe.wait_ge(masked, NB * (HEADS + j) + b - 1)
                w = (b + 1) * P
                dst = bank[S_BANK[b % 2]]
                score(dst[:, 0:w], qk[:, 0, b * P:w], qk[:, 2, b * P:w], qk[:, 1, 0:w], qk[:, 3, 0:w], False)
                pe.matmul(dst[:, b * P:w], ident_b[:, :], causal[:, :], start=False, stop=True).then_inc(s_done, 1)

            pe.wait_ge(bf_ready, 1)
            fox_units(0)
            for j in range(HEADS + 1):
                J = HEADS + j

                def pv_of():
                    pe.wait_ge(nb_ready, min(j + 1, HEADS))
                    if j >= 2:
                        pe.wait_ge(gated, j - 1)
                    pv(J - 1, (j - 1) % 2)

                def turn_of(t):
                    if t == 1:
                        pe.wait_ge(qk_normed, 3 + 2 * min(j, HEADS - 1))
                    turn_p(J - 1, fox_S, t)
                heads(j, 1, lambda b: fox_score(j, b), turn_of, pv_of)
                if j + 1 < HEADS:
                    fox_units(j + 1)
            for d in range(KT):
                s = U + 33 + d
                unit(s, 0, bank[s % 4][:, :], KT, hid_hi, hid_lo, s - 1, HID_BASE["fox"] if d == 0 else None)
            stat(6)
            ffn(3, 5)
            stat(7)
            for d in range(KT):
                pe.wait_ge(posted, KT + d + 1)
                if d >= 4:
                    pe.wait_ge((y_copied_a, y_copied_d)[d % 2], d // 2 - 1)
                for b in range(NB):
                    ins = pe.transpose(bank[d % 4][:, b * P:(b + 1) * P], xT[:, d, b * P:(b + 1) * P], ident[:, :])
                ins.then_inc(y_turned, 1)


HID_BASE = {("ffn", 0): 0, "dsa": 22, ("ffn", 1): 30, ("ffn", 2): 52, "fox": 74, ("ffn", 3): 82}
PAIR_BASE = [0, 22, 44, 66]

_INS = ['x', 'c', 'mod_w', 'mod_b', 'ffn1_w_gu', 'ffn1_w_down', 'ffn2_w_gu', 'ffn2_w_down', 'post_gain',
        'dsa_w_in', 'dsa_q_gain', 'dsa_k_gain', 'dsa_w_out',
        'fox_w_in', 'fox_f_bias', 'fox_q_gain', 'fox_k_gain', 'fox_w_out']


def kernel(**inputs):
    import numpy as _np
    import concourse.bacc as _bacc
    from concourse import mybir as _mybir
    from concourse.bass_utils import run_bass_kernel_spmd as _run

    nc = _bacc.Bacc("TRN2", target_bir_lowering=False, num_devices=1)
    arrays, args = {}, []
    for name in _INS:
        a = _np.ascontiguousarray(inputs[name])
        arrays[f"in_{name}_dram"] = a
        args.append(nc.dram_tensor(f"in_{name}_dram", a.shape, _mybir.dt.from_np(a.dtype), kind="ExternalInput").ap())
    args.append(nc.dram_tensor("out_0_dram", (1, SEQ, D), _mybir.dt.float32, kind="ExternalOutput").ap())
    build(nc, *args)
    r = _run(nc, [arrays], core_ids=[0])
    return r.results[0]["out_0_dram"]
```
